# Optimizing a Trainium2 kernel written in Bass

```python
import math
import jax
import jax.numpy as jnp
from jax import lax
import numpy as np

D_MODEL = 1024
BATCH = 1
SEQ = 1024
DEPTH = 2
DEC_BATCH = 8
DEC_SEQ = 8
PAST_LEN = 2048
PAGE_SIZE = 128

HEAD_DIM = 64
N_MIXERS = 4
GROUP_WIDTH = D_MODEL // N_MIXERS
N_HEADS_A = GROUP_WIDTH // HEAD_DIM
C_CONV = GROUP_WIDTH
CONV_WIDTH = 31
N_HEADS_C = GROUP_WIDTH // HEAD_DIM
N_BRANCH = 3
CMP_BLOCK = 32
SEL_BLOCK = 64
N_SELECT = 16
WINDOW = 512
N_GROUPS_D = GROUP_WIDTH // HEAD_DIM
CHUNK = 128
D_FF = 4 * D_MODEL
Q_BLOCK = 128
ROPE_THETA = 10000.0
EPS = 1e-6
FORCED_SCORE = 1e4
FORGET_BIAS = 4.0

SPLIT_SIZES = (GROUP_WIDTH, GROUP_WIDTH, GROUP_WIDTH, N_HEADS_A,
               2 * C_CONV,
               GROUP_WIDTH, 2 * N_BRANCH * HEAD_DIM, N_BRANCH * N_HEADS_C,
               GROUP_WIDTH, GROUP_WIDTH)
IN_WIDTH = sum(SPLIT_SIZES)
SPLIT_IDX = tuple(int(i) for i in np.cumsum(SPLIT_SIZES)[:-1])

kernel_name = 'hybrid_fox_conformer_nsa_gmlp_step'

def rmsnorm(x, g):
    xf = x.astype(jnp.float32)
    xf = xf * lax.rsqrt(jnp.mean(xf * xf, axis=-1, keepdims=True) + EPS)
    return xf.astype(x.dtype) * g

def layernorm(x, g, b):
    xf = x.astype(jnp.float32)
    mu = jnp.mean(xf, axis=-1, keepdims=True)
    var = jnp.mean(jnp.square(xf - mu), axis=-1, keepdims=True)
    return ((xf - mu) * lax.rsqrt(var + EPS)).astype(x.dtype) * g + b

def rope(x, pos):
    half = HEAD_DIM // 2
    inv = ROPE_THETA ** (-jnp.arange(half, dtype=jnp.float32) / half)
    ang = pos.astype(jnp.float32)[:, None] * inv
    ang = ang.reshape(ang.shape[:1] + (1,) * (x.ndim - 3) + ang.shape[1:])
    cos = jnp.cos(ang).astype(x.dtype)
    sin = jnp.sin(ang).astype(x.dtype)
    x1, x2 = x[..., :half], x[..., half:]
    return jnp.concatenate([x1 * cos - x2 * sin, x2 * cos + x1 * sin], axis=-1)

def masked_softmax(s, mask):
    s = jnp.where(mask, s.astype(jnp.float32), -jnp.inf)
    m = jnp.max(s, axis=-1, keepdims=True)
    m = jnp.where(jnp.isfinite(m), m, 0.0)
    e = jnp.where(mask, jnp.exp(s - m), 0.0)
    return e / jnp.maximum(jnp.sum(e, axis=-1, keepdims=True), 1e-30)

def project(xn, pos, p):
    B, T = xn.shape[:2]
    z = xn @ p['w_in']
    qa, ka, va, fa, glu_in, qc, kvc, gc, ud, vd = jnp.split(z, SPLIT_IDX, axis=-1)
    hs = (B, T, N_HEADS_A, HEAD_DIM)
    qa = rmsnorm(qa.reshape(hs), p['fox_qn_g'])
    ka = rmsnorm(ka.reshape(hs), p['fox_kn_g'])
    va = va.reshape(hs)
    logf = jax.nn.log_sigmoid(fa.astype(jnp.float32) + p['fox_bf'].astype(jnp.float32))
    ga, gb = jnp.split(glu_in, 2, axis=-1)
    glu = ga * jax.nn.sigmoid(gb)
    qc = rope(rmsnorm(qc.reshape(B, T, N_HEADS_C, HEAD_DIM), p['nsa_qn_g']), pos)
    kvc = kvc.reshape(B, T, 2 * N_BRANCH, HEAD_DIM)
    keys = rope(rmsnorm(kvc[:, :, 0::2], p['nsa_kn_g']), pos)
    kvc = jnp.stack([keys, kvc[:, :, 1::2]], axis=3).reshape(B, T, 2 * N_BRANCH, HEAD_DIM)
    gc = jax.nn.sigmoid(gc).reshape(B, T, N_HEADS_C, N_BRANCH)
    return qa, ka, va, logf, glu, qc, kvc, gc, ud, vd

def fox_attend(q, fq, qpos, k, v, fk, kpos):
    s = jnp.einsum('bqhd,bkhd->bhqk', q, k).astype(jnp.float32) * (HEAD_DIM ** -0.5)
    s = s + jnp.transpose(fq, (0, 2, 1))[..., :, None] - jnp.transpose(fk, (0, 2, 1))[..., None, :]
    mask = (kpos[None, :] <= qpos[:, None])[None, None]
    pr = masked_softmax(s, mask)
    return jnp.einsum('bhqk,bkhd->bqhd', pr.astype(v.dtype), v)

def fox_prompt(q, k, v, logf):
    B, S = q.shape[:2]
    F = jnp.cumsum(logf, axis=1)
    kpos = jnp.arange(S)

    def blk(i):
        st = i * Q_BLOCK
        qb = lax.dynamic_slice_in_dim(q, st, Q_BLOCK, axis=1)
        fb = lax.dynamic_slice_in_dim(F, st, Q_BLOCK, axis=1)
        return fox_attend(qb, fb, st + jnp.arange(Q_BLOCK), k, v, F, kpos)

    o = lax.map(blk, jnp.arange(S // Q_BLOCK))
    return jnp.moveaxis(o, 0, 1).reshape(B, S, N_HEADS_A, HEAD_DIM)

def fox_sample(q, k, v, logf, past_k, past_v, past_logf):
    P, T = past_k.shape[1], q.shape[1]
    suf = jnp.cumsum(past_logf[:, ::-1], axis=1)[:, ::-1] - past_logf
    lnew = jnp.cumsum(logf, axis=1)
    fk = jnp.concatenate([-suf, lnew], axis=1)
    keys = jnp.concatenate([past_k, k], axis=1)
    vals = jnp.concatenate([past_v, v], axis=1)
    return fox_attend(q, lnew, P + jnp.arange(T), keys, vals, fk, jnp.arange(P + T))

def conformer_conv(glu, buf, p):
    xin = jnp.concatenate([buf, glu], axis=1)
    y = lax.conv_general_dilated(xin, p['conv_w'][:, None, :], window_strides=(1,), padding='VALID',
                                 dimension_numbers=('NWC', 'WIO', 'NWC'), feature_group_count=C_CONV)
    y = layernorm(y + p['conv_b'], p['conv_ln_g'], p['conv_ln_b'])
    return jax.nn.silu(y), xin[:, -(CONV_WIDTH - 1):]

def nsa_compress(rows, p):
    B, L = rows.shape[:2]
    n = L // CMP_BLOCK
    blocks = rows[:, :n * CMP_BLOCK, :2].reshape(B, n, CMP_BLOCK, 2, HEAD_DIM)
    kb = (blocks[:, :, :, 0] + p['nsa_pe'][0]).reshape(B, n, CMP_BLOCK * HEAD_DIM)
    vb = (blocks[:, :, :, 1] + p['nsa_pe'][1]).reshape(B, n, CMP_BLOCK * HEAD_DIM)
    return kb @ p['nsa_phi_k'], vb @ p['nsa_phi_v']

def nsa_attend(q, qpos, g, kc, vc, ksel, vsel, kw, vw, kwpos):
    scale = HEAD_DIM ** -0.5
    B, Tq = q.shape[:2]
    L, nc = ksel.shape[1], kc.shape[1]
    s = jnp.einsum('bqhd,bnd->bhqn', q, kc) * scale
    cmask = (((jnp.arange(nc) + 1) * CMP_BLOCK - 1)[None, :] <= qpos[:, None])[None, None]
    p_cmp = masked_softmax(s, cmask)
    o_cmp = jnp.einsum('bhqn,bnd->bqhd', p_cmp.astype(vc.dtype), vc)
    ns = -(-L // SEL_BLOCK)
    per = SEL_BLOCK // CMP_BLOCK
    imp = jnp.sum(p_cmp, axis=1)
    imp = jnp.pad(imp, ((0, 0), (0, 0), (0, ns * per - nc))).reshape(B, Tq, ns, per).sum(-1)
    j = jnp.arange(ns)[None, :]
    cur = (qpos // SEL_BLOCK)[:, None]
    forced = (j == 0) | (j == cur) | (j == cur - 1)
    imp = jnp.where(forced, FORCED_SCORE, imp)
    imp = jnp.where(j <= cur, imp, -1.0)
    n_sel = min(N_SELECT, ns)
    top, idx = lax.top_k(imp, n_sel)
    kpos = (idx[..., None] * SEL_BLOCK + jnp.arange(SEL_BLOCK)).reshape(B, Tq, n_sel * SEL_BLOCK)
    blk_ok = jnp.broadcast_to((top >= 0)[..., None], top.shape + (SEL_BLOCK,)).reshape(B, Tq, n_sel * SEL_BLOCK)
    smask = blk_ok & (kpos <= qpos[None, :, None])
    kpos = jnp.minimum(kpos, L - 1)
    bidx = jnp.arange(B)[:, None, None]
    kg, vg = ksel[bidx, kpos], vsel[bidx, kpos]
    s = jnp.einsum('bqhd,bqkd->bhqk', q, kg) * scale
    p_sel = masked_softmax(s, smask[:, None])
    o_sel = jnp.einsum('bhqk,bqkd->bqhd', p_sel.astype(vg.dtype), vg)
    s = jnp.einsum('bqhd,bkd->bhqk', q, kw) * scale
    wmask = ((kwpos[None, :] <= qpos[:, None]) & (qpos[:, None] - kwpos[None, :] < WINDOW)
             & (kwpos[None, :] >= 0))[None, None]
    p_win = masked_softmax(s, wmask)
    o_win = jnp.einsum('bhqk,bkd->bqhd', p_win.astype(vw.dtype), vw)
    return g[..., 0:1] * o_cmp + g[..., 1:2] * o_sel + g[..., 2:3] * o_win

def nsa_prompt(q, g, kvc, p):
    B, S = q.shape[:2]
    kc, vc = nsa_compress(kvc, p)
    ksel, vsel = kvc[:, :, 2], kvc[:, :, 3]
    kwp = jnp.pad(kvc[:, :, 4], ((0, 0), (WINDOW, 0), (0, 0)))
    vwp = jnp.pad(kvc[:, :, 5], ((0, 0), (WINDOW, 0), (0, 0)))

    def blk(i):
        st = i * Q_BLOCK
        qb = lax.dynamic_slice_in_dim(q, st, Q_BLOCK, axis=1)
        gb = lax.dynamic_slice_in_dim(g, st, Q_BLOCK, axis=1)
        kwb = lax.dynamic_slice_in_dim(kwp, st, WINDOW + Q_BLOCK, axis=1)
        vwb = lax.dynamic_slice_in_dim(vwp, st, WINDOW + Q_BLOCK, axis=1)
        kwpos = st - WINDOW + jnp.arange(WINDOW + Q_BLOCK)
        return nsa_attend(qb, st + jnp.arange(Q_BLOCK), gb, kc, vc, ksel, vsel, kwb, vwb, kwpos)

    o = lax.map(blk, jnp.arange(S // Q_BLOCK))
    return jnp.moveaxis(o, 0, 1).reshape(B, S, N_HEADS_C, HEAD_DIM)

def gmlp_gate(u, v, p):
    B, T = u.shape[:2]
    vn = layernorm(v, p['gmlp_ln_g'], p['gmlp_ln_b'])
    nch = -(-T // CHUNK)
    vp = jnp.pad(vn, ((0, 0), (0, nch * CHUNK - T), (0, 0))).reshape(B, nch, CHUNK, N_GROUPS_D, HEAD_DIM)
    wm = p['gmlp_ws'] * jnp.tril(jnp.ones((CHUNK, CHUNK), p['gmlp_ws'].dtype))
    mixed = jnp.einsum('gts,bcsgd->bctgd', wm, vp) + jnp.transpose(p['gmlp_bs'])[:, :, None]
    mixed = mixed.reshape(B, nch * CHUNK, GROUP_WIDTH)[:, :T]
    return u * mixed, vn

def merge_and_ffn(x, outs, p):
    B, T = x.shape[:2]
    o = jnp.concatenate([rmsnorm(o_i.reshape(B, T, GROUP_WIDTH), p['gnorm_g'][i])
                         for i, o_i in enumerate(outs)], axis=-1)
    h = x + o @ p['w_out']
    u = jax.nn.relu(rmsnorm(h, p['norm2_g']) @ p['w_ff1'])
    return h + jnp.square(u) @ p['w_ff2']

def layer_prompt(x, p):
    B, S = x.shape[:2]
    pos = jnp.arange(S)
    xn = rmsnorm(x, p['norm1_g'])
    qa, ka, va, logf, glu, qc, kvc, gc, ud, vd = project(xn, pos, p)
    o_a = fox_prompt(qa, ka, va, logf)
    o_b, conv_new = conformer_conv(glu, jnp.zeros((B, CONV_WIDTH - 1, C_CONV), glu.dtype), p)
    o_c = nsa_prompt(qc, gc, kvc, p)
    o_d, _ = gmlp_gate(ud, vd, p)
    y = merge_and_ffn(x, (o_a, o_b, o_c, o_d), p)
    wp = min(WINDOW, S)
    return y, (jnp.stack([ka, va], axis=2), logf, kvc[:, :, :4], kvc[:, -wp:, 4:], conv_new)

def layer_sample(x, p, past_k, past_v, past_logf, past_nsa, win_buf, conv_buf):
    B, T = x.shape[:2]
    P = past_k.shape[1]
    pos = P + jnp.arange(T)
    xn = rmsnorm(x, p['norm1_g'])
    qa, ka, va, logf, glu, qc, kvc, gc, ud, vd = project(xn, pos, p)
    o_a = fox_sample(qa, ka, va, logf, past_k.astype(ka.dtype), past_v.astype(va.dtype),
                     past_logf.astype(jnp.float32))
    o_b, conv_new = conformer_conv(glu, conv_buf.astype(glu.dtype), p)
    full = jnp.concatenate([past_nsa.astype(kvc.dtype), kvc[:, :, :4]], axis=1)
    win = jnp.concatenate([win_buf.astype(kvc.dtype), kvc[:, :, 4:]], axis=1)
    wb = win_buf.shape[1]
    kc, vc = nsa_compress(full, p)
    o_c = nsa_attend(qc, pos, gc, kc, vc, full[:, :, 2], full[:, :, 3], win[:, :, 0], win[:, :, 1],
                     P - wb + jnp.arange(wb + T))
    o_d, vn = gmlp_gate(ud, vd, p)
    y = merge_and_ffn(x, (o_a, o_b, o_c, o_d), p)
    new_win = win[:, -min(WINDOW, wb + T):]
    return y, (jnp.stack([ka, va], axis=2), logf, kvc[:, :, :4], new_win, conv_new, vn)

def setup_inputs(seed: int = 0) -> dict:
    key = jax.random.key(seed)
    ks = jax.random.split(key, 32)
    n_pages = PAST_LEN // PAGE_SIZE
    n_used = DEC_BATCH * n_pages
    n_pool = n_used + n_used // 4
    win_buf = min(WINDOW, PAST_LEN)
    nrm = jax.random.normal

    def gain(k, shape):
        return 1.0 + 0.02 * nrm(k, shape)

    page_table = jax.random.permutation(ks[7], n_pool)[:n_used].reshape(DEC_BATCH, n_pages).astype(jnp.int32)
    return {
        'x_prompt': nrm(ks[0], (BATCH, SEQ, D_MODEL)),
        'x_sample': nrm(ks[1], (DEC_BATCH, DEC_SEQ, D_MODEL)),
        'cache_fox_kv': nrm(ks[2], (DEPTH, n_pool, PAGE_SIZE, 2, N_HEADS_A, HEAD_DIM)),
        'cache_fox_logf': jax.nn.log_sigmoid(FORGET_BIAS + nrm(ks[3], (DEPTH, n_pool, PAGE_SIZE, N_HEADS_A))),
        'cache_nsa_kv': nrm(ks[4], (DEPTH, n_pool, PAGE_SIZE, 4, HEAD_DIM)),
        'state_nsa_win': nrm(ks[5], (DEPTH, DEC_BATCH, win_buf, 2, HEAD_DIM)),
        'state_conv': 0.5 * nrm(ks[6], (DEPTH, DEC_BATCH, CONV_WIDTH - 1, C_CONV)),
        'page_table': page_table,
        'norm1_g': gain(ks[8], (DEPTH, D_MODEL)),
        'w_in': nrm(ks[9], (DEPTH, D_MODEL, IN_WIDTH)) * D_MODEL ** -0.5,
        'fox_bf': 2.0 + 4.0 * jax.random.uniform(ks[10], (DEPTH, N_HEADS_A)),
        'fox_qn_g': gain(ks[11], (DEPTH, HEAD_DIM)),
        'fox_kn_g': gain(ks[12], (DEPTH, HEAD_DIM)),
        'conv_w': nrm(ks[13], (DEPTH, CONV_WIDTH, C_CONV)) * CONV_WIDTH ** -0.5,
        'conv_b': 0.02 * nrm(ks[14], (DEPTH, C_CONV)),
        'conv_ln_g': gain(ks[15], (DEPTH, C_CONV)),
        'conv_ln_b': 0.02 * nrm(ks[16], (DEPTH, C_CONV)),
        'nsa_qn_g': gain(ks[17], (DEPTH, HEAD_DIM)),
        'nsa_kn_g': gain(ks[18], (DEPTH, N_BRANCH, HEAD_DIM)),
        'nsa_pe': 0.1 * nrm(ks[19], (DEPTH, 2, CMP_BLOCK, HEAD_DIM)),
        'nsa_phi_k': nrm(ks[20], (DEPTH, CMP_BLOCK * HEAD_DIM, HEAD_DIM)) * (CMP_BLOCK * HEAD_DIM) ** -0.5,
        'nsa_phi_v': nrm(ks[21], (DEPTH, CMP_BLOCK * HEAD_DIM, HEAD_DIM)) * (CMP_BLOCK * HEAD_DIM) ** -0.5,
        'gmlp_ln_g': gain(ks[22], (DEPTH, GROUP_WIDTH)),
        'gmlp_ln_b': 0.02 * nrm(ks[23], (DEPTH, GROUP_WIDTH)),
        'gmlp_ws': nrm(ks[24], (DEPTH, N_GROUPS_D, CHUNK, CHUNK)) * CHUNK ** -0.5,
        'gmlp_bs': 1.0 + 0.1 * nrm(ks[25], (DEPTH, N_GROUPS_D, CHUNK)),
        'gnorm_g': gain(ks[26], (DEPTH, N_MIXERS, GROUP_WIDTH)),
        'w_out': nrm(ks[27], (DEPTH, D_MODEL, D_MODEL)) * D_MODEL ** -0.5,
        'norm2_g': gain(ks[28], (DEPTH, D_MODEL)),
        'w_ff1': nrm(ks[29], (DEPTH, D_MODEL, D_FF)) * D_MODEL ** -0.5,
        'w_ff2': nrm(ks[30], (DEPTH, D_FF, D_MODEL)) * D_FF ** -0.5,
    }

def reference(x_prompt, x_sample, cache_fox_kv, cache_fox_logf, cache_nsa_kv, state_nsa_win, state_conv,
              page_table, norm1_g, w_in, fox_bf, fox_qn_g, fox_kn_g, conv_w, conv_b, conv_ln_g, conv_ln_b,
              nsa_qn_g, nsa_kn_g, nsa_pe, nsa_phi_k, nsa_phi_v, gmlp_ln_g, gmlp_ln_b, gmlp_ws, gmlp_bs,
              gnorm_g, w_out, norm2_g, w_ff1, w_ff2):
    DB = x_sample.shape[0]
    P = page_table.shape[1] * cache_fox_kv.shape[2]
    xp, xs = x_prompt, x_sample
    states_p, states_s = [], []
    for l in range(DEPTH):
        p = dict(norm1_g=norm1_g[l], w_in=w_in[l], fox_bf=fox_bf[l], fox_qn_g=fox_qn_g[l],
                 fox_kn_g=fox_kn_g[l], conv_w=conv_w[l], conv_b=conv_b[l], conv_ln_g=conv_ln_g[l],
                 conv_ln_b=conv_ln_b[l], nsa_qn_g=nsa_qn_g[l], nsa_kn_g=nsa_kn_g[l], nsa_pe=nsa_pe[l],
                 nsa_phi_k=nsa_phi_k[l], nsa_phi_v=nsa_phi_v[l], gmlp_ln_g=gmlp_ln_g[l],
                 gmlp_ln_b=gmlp_ln_b[l], gmlp_ws=gmlp_ws[l], gmlp_bs=gmlp_bs[l], gnorm_g=gnorm_g[l],
                 w_out=w_out[l], norm2_g=norm2_g[l], w_ff1=w_ff1[l], w_ff2=w_ff2[l])
        xp, st_p = layer_prompt(xp, p)
        states_p.append(st_p)
        past_k = cache_fox_kv[l, page_table, :, 0].reshape(DB, P, N_HEADS_A, HEAD_DIM)
        past_v = cache_fox_kv[l, page_table, :, 1].reshape(DB, P, N_HEADS_A, HEAD_DIM)
        past_logf = cache_fox_logf[l, page_table].reshape(DB, P, N_HEADS_A)
        past_nsa = cache_nsa_kv[l, page_table].reshape(DB, P, 4, HEAD_DIM)
        xs, st_s = layer_sample(xs, p, past_k, past_v, past_logf, past_nsa, state_nsa_win[l], state_conv[l])
        states_s.append(st_s)
    fox_kv_p, fox_logf_p, nsa_kv_p, nsa_win_p, conv_p = [jnp.stack(a) for a in zip(*states_p)]
    fox_kv_s, fox_logf_s, nsa_kv_s, nsa_win_s, conv_s, gmlp_v_s = [jnp.stack(a) for a in zip(*states_s)]
    return (xp, xs, fox_kv_p, fox_kv_s, fox_logf_p, fox_logf_s, nsa_kv_p, nsa_kv_s,
            nsa_win_p, nsa_win_s, conv_p, conv_s, gmlp_v_s)


_drawn_inputs = setup_inputs


def setup_inputs(seed=0):
    import zlib

    import numpy as np

    out = dict(_drawn_inputs(seed))
    spreads = {}
    factors = {'fox_qn_g': 6.168,
     'fox_kn_g': 4.159,
     'conv_b': 2.979,
     'conv_ln_g': 41.922,
     'conv_ln_b': 45.727,
     'nsa_qn_g': 3.916,
     'nsa_kn_g': 3.623,
     'gmlp_ln_g': 21.299,
     'gmlp_ln_b': 21.541,
     'gnorm_g': 3.041,
     'norm2_g': 2.705}
    for name, (base, spread) in spreads.items():
        noise = np.random.default_rng([zlib.crc32(name.encode()), seed]).standard_normal(out[name].shape)
        drawn = base * np.exp(spread * noise) if base else spread * noise
        out[name] = jnp.asarray(drawn.astype(out[name].dtype))
    for name, factor in factors.items():
        out[name] = (out[name] * factor).astype(out[name].dtype)
    return out
```

```python
import math
from contextlib import ExitStack

import numpy as np

import concourse.bass as bass
from concourse import mybir

F32 = mybir.dt.float32
BF16 = mybir.dt.bfloat16
I32 = mybir.dt.int32
ALU = mybir.AluOpType
ACT = mybir.ActivationFunctionType
AX = mybir.AxisListType.X

DM = 1024
SEQ = 1024
NB = 8
NT = 8
DEPTH = 2
PAST = 2048
PAGE = 128
HD = 64
NH = 4
GW = NH * HD
CW = 31
BLK = 32
SEL = 64
NSEL = 16
WIN = 512
DFF = 4 * DM
EPS = 1e-6
NEG = -1e30

P = 128
NS = NB * NT
ROWS = SEQ + NS
QT = SEQ // P
KD = DM // P
NPG = PAST // PAGE
POOL = NB * NPG * 5 // 4
NCB = PAST // BLK
NSB = PAST // SEL + 1
NPB = SEQ // BLK
LK = PAST + NT
AUG = HD + 2
IN_W = 2448
C_QK, C_V, C_GLU, C_NSA, C_UV = 0, 512, 772, 1284, 1936
TOKW = IN_W - 2 * GW
CHUNKS = ((0, 512), (512, 772), (772, 1156), (1156, 1424), (1424, 1936))
WIDTHS = (512, 512, NS)
STARTS = (0, 512, SEQ)


def shape_constants():
    r = np.arange(P)
    q, k = r[:, None], r[None, :]
    parts = {}
    parts["ident"] = (q == k)
    parts["mhalf"] = np.full((P, 1), -0.5)
    parts["ones"] = np.ones((P, P))
    parts["triu"] = (q <= k)
    same = (q // NT == k // NT)
    parts["btriu"] = (same & (q <= k))[:, :NS]
    parts["cneg"] = np.where(k > q, NEG, 0.0)
    parts["wneg"] = np.where(k <= q, NEG, 0.0)
    end = (np.arange(NPB) + 1) * BLK - 1
    pos = np.arange(QT)[None, :, None] * P + r[:, None, None]
    ok = end[None, None, :] <= pos
    parts["cmpneg"] = np.where(ok, 0.0, NEG).reshape(P, -1)
    parts["cmp01"] = ok.reshape(P, -1)
    half = HD // 2
    inv = (10000.0 ** (-np.arange(half, dtype=np.float64) / half)).astype(np.float32)
    rows = np.concatenate([np.arange(QT)[None, :] * P + r[:, None], (PAST + r % NT)[:, None]], axis=1)
    ang = rows.astype(np.float32)[:, :, None] * inv
    parts["cos"] = np.cos(ang).astype(np.float32).reshape(P, -1)
    parts["sin"] = np.sin(ang).astype(np.float32).reshape(P, -1)
    parts["tril"] = (k <= q)
    parts["btril"] = (same & (k <= q))[:, :NS]
    parts["later"] = ((q // NPG == k // NPG) & (q > k))
    m = np.arange(NS // 2)[None, :]
    parts["hsum"] = ((q // (NH * NT) == m // NT) & (q % NT == m % NT))
    parts["hmask"] = ((r[:, None] % (NH * NT)) // NT == np.arange(NH)[None, :])
    parts["newneg"] = np.where(np.arange(NT)[None, :] > r[:, None] % NT, NEG, 0.0)
    parts["winneg"] = np.where(np.arange(NT)[None, :] <= r[:, None] % NT, NEG, 0.0)
    j = np.arange(NSB)
    parts["before"] = np.broadcast_to((j[None, :] < j[:, None]).reshape(1, -1), (P, NSB * NSB))
    at, cols, off = {}, [], 0
    for name, a in parts.items():
        a = np.ascontiguousarray(a, dtype=np.float32)
        at[name] = (off, a.shape[1])
        cols.append(a)
        off += a.shape[1]
    return at, np.concatenate(cols, axis=1)


CONST_AT, _ = shape_constants()
CONST_W = sum(w for _, w in CONST_AT.values())
ARENA_W = 53100


class Layout:

    def __init__(self, arena, start, end):
        self.arena, self.at, self.end = arena, start, end

    def take(self, cols, dtype=F32, **shape):
        words = cols if dtype == F32 else (cols + 1) // 2
        a = self.arena[:, self.at:self.at + words]
        self.at += words
        assert self.at <= self.end, (self.at, self.end)
        if dtype != F32:
            a = a.bitcast(dtype)
        if shape:
            names = list(shape)
            a = a.rearrange(f"p ({' '.join(names)}) -> p {' '.join(names)}", **shape)
        return a


class Chain:

    def __init__(self, eng, sem):
        self.eng, self.sem, self.n = eng, sem, 0

    def next(self):
        self.n += 1
        return self.n

    def restart(self):
        self.eng.sem_clear(self.sem)
        self.n = 0


def build_step(nc, A, O, layers=DEPTH, stop=99):
    ctx = ExitStack()
    with ctx, nc.allow_non_contiguous_dma(reason="columns of a few elements in small tables"):
        arena = ctx.enter_context(nc.sbuf_tensor("arena", [P, ARENA_W], F32))
        PS = ctx.enter_context(nc.psum_tensor("PS", [P, 4096], F32))

        def bank(n, cols=512, dtype=F32):
            return PS[:, n * 512:n * 512 + cols]

        def scratch(name, shape):
            return nc.dram_tensor(name, shape, F32).ap()

        qa_s = scratch("qa_s", (ROWS, NH, AUG))
        ka_s = scratch("ka_s", (ROWS, NH, AUG))
        va_s = scratch("va_s", (ROWS, NH, HD))
        qc_s = scratch("qc_s", (ROWS, NH, HD))
        kvc_s = scratch("kvc_s", (ROWS, 6, HD))
        g_s = scratch("g_s", (ROWS, 12))
        o_s = scratch("o_s", (ROWS, 4, NH, HD))
        y_s = scratch("y_s", (P, 2 * ROWS))
        suf_s = scratch("suf_s", (NB, NH, LK))
        sel_s = scratch("sel_s", (NS, NSB))
        oc_s = scratch("oc_s", (NB, NH * NT, HD))
        of_s = scratch("of_s", (NB, 2, NH * NT, HD))

        fixed = Layout(arena, 0, ARENA_W)
        const = fixed.take(CONST_W)

        def C(name, rows=P):
            off, w = CONST_AT[name]
            return const[0:rows, off:off + w]

        ident, ones, triu = C("ident"), C("ones"), C("triu")
        identb = fixed.take(P, BF16)
        cnegb = fixed.take(P, BF16)
        wnegb = fixed.take(P, BF16)
        pages = fixed.take(NB * NPG)[0:1, :].bitcast(I32)
        page_rows = fixed.take(1).bitcast(I32)
        XT = fixed.take(KD * ROWS, k=KD, n=ROWS)
        base = fixed.at

        lo = Layout(arena, base, ARENA_W)
        XNT = lo.take(KD * ROWS, k=KD, n=ROWS)
        after_xnt = lo.at
        Wt = lo.take(KD * TOKW, k=KD, n=TOKW)
        glu_at = lo.at
        Wg = lo.take(KD * 512, k=KD, n=512)
        SG = lo.take(ROWS)
        t1 = Layout(arena, glu_at, ARENA_W)
        Z = t1.take(1164)
        SQ = t1.take(1152)
        T10 = t1.take(640)
        SN = t1.take(640)
        XTT = [t1.take(KD * P, k=KD, n=P) for _ in range(2)]
        lo.at = max(lo.at, t1.at)
        Yc = arena[:, glu_at:glu_at + 2 * ROWS].rearrange("p (c n) -> p c n", c=2)
        tile_at = lo.at
        ZA = [lo.take(8 * AUG, g=8, d=AUG) for _ in range(2)]
        RN = [lo.take(640, g=10, d=HD) for _ in range(2)]
        VB = [lo.take(260) for _ in range(2)]
        UV = [lo.take(512) for _ in range(2)]
        VN = [lo.take(GW) for _ in range(2)]
        OD = [lo.take(GW) for _ in range(2)]
        G12 = [lo.take(12) for _ in range(2)]
        LF = [lo.take(4) for _ in range(2)]
        n1 = Layout(arena, tile_at, lo.at)
        SQ2 = n1.take(2 * ROWS, k=2, n=ROWS)
        RST = n1.take(ROWS)
        n1 = Layout(arena, tile_at, lo.at)
        WMr = n1.take(4 * P, g=4, n=P)
        WM8r = n1.take(4 * NS, g=4, n=NS)
        GL = lo.take(2 * (CW - 1 + SEQ), c=2, n=CW - 1 + SEQ)
        GLS = lo.take(2 * NB * (CW - 1 + NT), c=2, b=NB, n=CW - 1 + NT)
        SGL = lo.take(2 * NS, c=2, n=NS)
        CS = lo.take(2 * GW, c=2, n=GW)
        CPO = CS.rearrange("p c n -> p (c n)")
        GQK = lo.take(2 * HD, a=2, d=HD)
        GN10 = lo.take(640, g=10, d=HD)
        LNG = lo.take(2 * GW, a=2, n=GW)
        BS = lo.take(4)
        BS8 = lo.take(4)
        BFB = lo.take(4)
        G1 = lo.take(KD)
        CWT = lo.take(2 * CW, c=2, j=CW)
        CB = lo.take(2)
        WMT = lo.take(4 * P, g=4, n=P)
        WM8T = lo.take(4 * NS, g=4, n=NS)
        SS18 = lo.take(19)
        EX = lo.take(64)
        CARRY = lo.take(4)
        BN6 = lo.take(6)
        BN2 = lo.take(2)

        lo = Layout(arena, base, ARENA_W)
        NTOK = NB * PAST + SEQ
        CT = lo.take(NTOK + BLK)
        PHI = lo.take(BLK * P, c=BLK, n=P)
        PG = [lo.take(4 * P, j=4, n=P) for _ in range(4)]
        CP8 = lo.take(QT * P, t=QT, n=P)
        PE2 = lo.take(P)
        LFP = lo.take(PAGE * NH, t=PAGE, h=NH)
        PFX = lo.take(NH * PAGE, h=NH, t=PAGE)
        TOT = lo.take(4)
        LAT = lo.take(4)
        assert lo.at <= ARENA_W - 700
        KVC = arena[:, ARENA_W - 545:ARENA_W]

        lo = Layout(arena, base, ARENA_W - 545)
        QF = lo.take(QT * AUG, t=QT, d=AUG)
        KF = lo.take(QT * AUG, t=QT, d=AUG)
        VF = lo.take(QT * HD, t=QT, d=HD)
        QN = lo.take(QT * HD, t=QT, d=HD)
        GH = lo.take(QT * 3, t=QT, c=3)
        KV4 = lo.take(QT * 4 * HD, t=QT, g=4, d=HD)
        QFT = lo.take(SEQ)
        KFT = lo.take(SEQ)
        QNT = lo.take(SEQ)
        KST = lo.take(SEQ)
        KWT = lo.take(SEQ)
        VREP = lo.take(P, i=4, n=NPB)
        VBD = lo.take(4 * HD, i=4, d=HD)
        PR = [lo.take(SEQ) for _ in range(2)]
        PTR = [lo.take(SEQ) for _ in range(2)]
        NMX = lo.take(24)
        RS = lo.take(24)
        RI = lo.take(24)
        SC = lo.take(QT * NPB, t=QT, n=NPB)
        SC8 = lo.take(QT)
        PTC = lo.take(2 * P, g=2, n=P)
        OF = lo.take(QT * HD, t=QT, d=HD)
        ON = lo.take(QT * HD, t=QT, d=HD)

        lo = Layout(arena, base, ARENA_W - 545)
        KVP = [lo.take(NPG * 512, j=NPG, n=512) for _ in range(2)]
        SLP = [lo.take(NPG * P, j=NPG, n=P) for _ in range(2)]
        WNP = [lo.take(4 * P, j=4, n=P) for _ in range(2)]
        KNEW = [lo.take(GW) for _ in range(2)]
        VNEW = [lo.take(GW) for _ in range(2)]
        KV4N = [lo.take(GW, g=4, d=HD) for _ in range(2)]
        KT2 = lo.take(2 * LK, a=2, n=LK)
        KSTs = lo.take(LK)
        KWTs = lo.take(WIN + NT)
        BIAS = lo.take(LK)
        SF = lo.take(LK)
        SSL = lo.take(LK)
        SW = lo.take(WIN + NT)
        WMASK = lo.take(WIN + NT)
        PTF = lo.take(17 * 32, j=17, n=32)
        OO = lo.take(GW)
        OH = [lo.take(HD) for _ in range(2)]
        OCM = [lo.take(HD) for _ in range(2)]
        QALL = lo.take(2 * NB * 32, a=2, b=NB, n=32)
        QNALL = lo.take(NB * 32, b=NB, n=32)
        QB = lo.take(2 * 32, a=2, n=32)
        QNB = lo.take(32)
        FQ = lo.take(NB)
        GB = lo.take(NB * 3, b=NB, c=3)
        SNB = lo.take(NB * NSB, b=NB, j=NSB)
        SNB1 = [lo.take(NSB) for _ in range(2)]
        OCB = lo.take(NB * HD, b=NB, d=HD)
        MX8 = lo.take(8)
        ST = lo.take(8)
        l2 = Layout(arena, base + 8192, base + 16384)
        QS = l2.take(NH * HD, h=NH, d=HD)
        QCS = l2.take(NH * HD, h=NH, d=HD)
        PC = l2.take(2 * NCB, g=2, n=NCB)
        PC4 = l2.take(4)
        PTCs = l2.take(2 * P, g=2, n=P)
        VCT = l2.take(NB * P, b=NB, n=P)
        IMP = l2.take(NSB)
        GT = l2.take(NSB * NSB, j=NSB, i=NSB)
        EQ = l2.take(NSB * NSB, j=NSB, i=NSB)
        RK = l2.take(NSB)
        OCS = l2.take(2 * HD, g=2, d=HD)

        lo = Layout(arena, base, ARENA_W)
        OTH = lo.take(KD * ROWS, BF16, k=KD, n=ROWS)
        OTL = lo.take(KD * ROWS, BF16, k=KD, n=ROWS)
        gemm_at = lo.at
        WF = [lo.take(16 * P, k=16, n=P) for _ in range(2)]
        WH = [lo.take(16 * P, BF16, k=16, n=P) for _ in range(2)]
        WL = [lo.take(16 * P, BF16, k=16, n=P) for _ in range(2)]
        RL = [lo.take(ROWS) for _ in range(2)]
        merge_at = lo.at
        OA = [lo.take(3 * GW, g=3, n=GW) for _ in range(2)]
        OAQ = lo.take(GW)
        GNB = lo.take(3 * GW, g=3, n=GW)
        S3 = [lo.take(3) for _ in range(2)]
        GCB = lo.take(2)
        CB2 = lo.take(2)
        CLG = lo.take(2)
        CLB = lo.take(2)
        YB = lo.take(2 * ROWS, c=2, n=ROWS)
        YQ = lo.take(2 * ROWS, c=2, n=ROWS)
        YM = lo.take(ROWS)
        XNH, XNL = OTH, OTL
        lo = Layout(arena, merge_at, ARENA_W)
        UH = lo.take(16 * ROWS, BF16, k=16, n=ROWS)
        UL = lo.take(16 * ROWS, BF16, k=16, n=ROWS)
        XR = arena[:, merge_at:merge_at + KD * ROWS].rearrange("p (k n) -> p k n", k=KD)
        SQN = Layout(arena, merge_at + KD * ROWS, ARENA_W)
        SQN2 = SQN.take(2 * ROWS, k=2, n=ROWS)
        RST2 = SQN.take(ROWS)
        G2 = lo.take(KD)

        lo = Layout(arena, base, ARENA_W)
        XS = [lo.take(DM) for _ in range(2)]
        XO = [lo.take(KD * P, k=KD, n=P) for _ in range(2)]

        def sem(name):
            return ctx.enter_context(nc.semaphore(name))

        phase_names = []
        S = {}

        def names(text):
            for n in text.split():
                S[n] = sem(n)
                phase_names.append(n)

        all_in = sem("all_in")
        all_in2 = sem("all_in2")
        go2 = {n: sem(f"go2_{n}") for n in ("pe", "act", "dve")}
        go = {n: sem(f"go_{n}") for n in ("pe", "act", "dve", "sp")}
        lfp_in = sem("lfp_in")
        loaded_once = sem("loaded_once")
        names("act_done dve_done")
        names("col_inv col_mean col_rstd row_mean row_rstd row_in0 row_in1 row_T row_ev row_out0 row_out1 row_cp")
        names("sq_ready sq_summed xn_ready w_glu w_tok gains glu_mm glu_sig glu_done")
        names("ct_in ct_T ct_ev wm_in wm_raw wm_T wm_ev")
        names("xt_ready z_mm z_ev z_free na_ready ex_ready lf_ready small_mm fin st0 st1 tail_T tail_ev tail_out y_out old_out")
        names("phi_in pe_in pg0 pg1 pg2 pg3 pg_T pg_evA pg_evD cp_in lfp_ready page_next tot_ready lat_mm suf_ready suf_out kvc_mm kvc_ready zero_ready")
        names("head_in kv4_in tr_T tr_ev vb_ready s_mm nm_ready p_ready pt_T pt_ev pv_mm o_done cs_mm cs_ready ce_ready cp_ready cpt_T cpt_ev cpv_mm on_ready o_ready o_out")
        names("q_in q_T q_ev vct_ev sm_ready imp_mm rank_ready rank_out aux_in kv_in0 kv_in1 kv_free0 kv_free1 bias_in bias_free os_out")
        names("oa_hi u_hi oa_in0 oa_in1 ss_ready oa_ready oa_T oa_ev y_in y_sq y_mm y_c y_done")
        names("xh_ready w_in0 w_in1 w_hi w_lo g_mm g_ev u_ready")
        batch_at = len(phase_names)
        names("pool_done2 new_T new_ev bias_ready os_stored")
        names("kt_T kt_evA kt_evD qb_ready sc_mm sc_ev mx_ready e_ready ptn_T ptn_ev ov_mm ov_done os_ready")
        first_sem, last_sem = S[phase_names[0]].num, S[phase_names[-1]].num
        assert last_sem - first_sem == len(phase_names) - 1, (first_sem, last_sem)

        batch_sem = S[phase_names[batch_at]].num

        block = ctx.enter_context(nc.Block())

        def arrive(e, who):
            e.drain().then_inc(all_in, 1)
            e.wait_ge(go[who], 1)
            e.sem_clear(go[who])

        def arrive2(e, who):
            e.drain().then_inc(all_in2, 1)
            e.wait_ge(go2[who], 1)
            e.sem_clear(go2[who])

        def over_tiles(e, step, chain=None):
            step(0, 0, 0)
            step(1, 1, 0)
            with e.Fori(0, 2) as i:
                if chain:
                    chain.restart()
                step(2 * i + 2, 0, i + 1)
                step(2 * i + 3, 1, i + 1)
            if chain:
                chain.restart()
            step(6, 0, 3)
            step(7, 1, 3)
            step(8, 0, 4)

        @block.sync
        def _(sp):
            sp.dma_start(const, A["consts"]).then_inc(loaded_once, 16)
            sp.dma_start(pages, A["page_table"].rearrange("b j -> (b j)").unsqueeze(0)).then_inc(loaded_once, 16)

            sp.dma_start(page_rows, A["page_table"].rearrange("b j -> (b j)").unsqueeze(1)).then_inc(loaded_once, 16)

            def row_in(t, k, m):
                if isinstance(t, int):
                    src = A["x_prompt"][0, t * P:(t + 1) * P, :] if t < QT else A["x_sample"].rearrange("b t d -> (b t) d")
                    rows = P if t < QT else NS
                else:
                    src, rows = A["x_prompt"][0, bass.ds(t * P, P), :], P
                if not (isinstance(t, int) and t < 2):
                    sp.wait_ge(S["row_T"], t - 1)
                sp.dma_start(XS[k][0:rows, :], src).then_inc(S[f"row_in{k}"], 16)

            over_tiles(sp, row_in)
            arrive(sp, "sp")

            with sp.Fori(0, layers) as l:
                def w(name):
                    return A[name][bass.ds(l, 1)]

                sp.dma_start(Wg, w("w_in")[:, :, C_GLU:C_NSA].rearrange("o (k p) n -> p (o k) n", p=P)).then_inc(S["w_glu"], 16)
                sp.dma_start(G1, w("norm1_g").rearrange("o (k p) -> p (o k)", p=P)).then_inc(S["gains"], 16)
                sp.dma_start(CS[0:4 * (CW - 1), :, :],
                    w("state_conv").rearrange("o (g b) r n -> (o b r) g n", g=2)).then_inc(S["ct_in"], 16)
                for c, (a, b) in enumerate(CHUNKS):
                    src = a if a < C_GLU else a - C_GLU + C_NSA
                    sp.dma_start(Wt[:, :, a:b], w("w_in")[:, :, src:src + b - a].rearrange("o (k p) n -> p (o k) n", p=P)).then_inc(S["w_tok"], 16)

                def spread(dst, src, name="gains"):
                    sp.dma_start(dst, src.to_broadcast([dst.shape[0], src.shape[-1]])).then_inc(S[name], 16)

                spread(GQK[:, 0, :], w("fox_qn_g"))
                spread(GQK[:, 1, :], w("fox_kn_g"))
                for h in range(NH):
                    spread(GN10[:, h, :], w("nsa_qn_g"))
                for b in range(3):
                    spread(GN10[:, NH + 2 * b, :], w("nsa_kn_g")[:, b, :])
                spread(LNG[:, 0, :], w("gmlp_ln_g"))
                spread(LNG[:, 1, :], w("gmlp_ln_b"))
                spread(BFB, w("fox_bf"))
                sp.dma_start(BS, w("gmlp_bs").rearrange("o g t -> t (o g)")).then_inc(S["gains"], 16)
                for b in range(NB):
                    sp.dma_start(BS8[b * NT:(b + 1) * NT, :], w("gmlp_bs")[:, :, 0:NT].rearrange("o g t -> t (o g)")).then_inc(S["gains"], 16)
                for c in range(2):
                    sp.dma_start(CWT[:, c, :], w("conv_w")[:, :, c * P:(c + 1) * P].rearrange("o j p -> p (o j)")).then_inc(S["gains"], 16)
                sp.dma_start(CB, w("conv_b").rearrange("o (c p) -> p (o c)", p=P)).then_inc(S["gains"], 16)
                sp.wait_ge(S["sq_summed"], KD)
                sp.wait_ge(S["xn_ready"], KD)
                sp.dma_start(WMr, w("gmlp_ws").rearrange("o g t s -> t (o g) s")).then_inc(S["wm_in"], 16)
                for b in range(NB):
                    for c in range(NB):
                        sp.dma_start(WM8r[b * NT:(b + 1) * NT, :, c * NT:(c + 1) * NT],
                            w("gmlp_ws")[:, :, 0:NT, 0:NT].rearrange("o g t s -> t (o g) s")).then_inc(S["wm_in"], 16)
                sp.dma_start(O["nsa_win_s"][bass.ds(l, 1), :, 0:WIN - NT], w("state_nsa_win")[:, :, NT:WIN]).then_inc(S["old_out"], 16)
                sp.dma_start(O["conv_s"][bass.ds(l, 1), :, 0:CW - 1 - NT], w("state_conv")[:, :, NT:CW - 1]).then_inc(S["old_out"], 16)

                def store_tile(t, k):
                    s = f"st{k}"
                    sp.wait_ge(S["fin"], t + 1)
                    if isinstance(t, int) and t == QT:
                        rows = NS
                        r = slice(SEQ, ROWS)
                        fox = O["fox_kv_s"][bass.ds(l, 1)].rearrange("o b t c h d -> (o b t) c h d")
                        nsa = O["nsa_kv_s"][bass.ds(l, 1)].rearrange("o b t c d -> (o b t) c d")
                        logf = O["fox_logf_s"][bass.ds(l, 1)].rearrange("o b t h -> (o b t) h")
                    else:
                        rows = P
                        r = bass.ds(t * P, P)
                        fox = O["fox_kv_p"][bass.ds(l, 1), 0, r].rearrange("o r c h d -> (o r) c h d")
                        nsa = O["nsa_kv_p"][bass.ds(l, 1), 0, r].rearrange("o r c d -> (o r) c d")
                        logf = O["fox_logf_p"][bass.ds(l, 1), 0, r].rearrange("o r h -> (o r) h")
                    v3 = VB[k][0:rows, 0:GW].rearrange("p (h d) -> p h d", h=NH)
                    sp.dma_start(qa_s[r], ZA[k][0:rows, 0:NH, :]).then_inc(S[s], 16)
                    sp.dma_start(ka_s[r], ZA[k][0:rows, NH:2 * NH, :]).then_inc(S[s], 16)
                    sp.dma_start(va_s[r], v3).then_inc(S[s], 16)
                    sp.dma_start(fox[:, 0], ZA[k][0:rows, NH:2 * NH, 0:HD]).then_inc(S[s], 16)
                    sp.dma_start(fox[:, 1], v3).then_inc(S[s], 16)
                    sp.dma_start(qc_s[r], RN[k][0:rows, 0:NH, :]).then_inc(S[s], 16)
                    sp.dma_start(kvc_s[r], RN[k][0:rows, NH:, :]).then_inc(S[s], 16)
                    sp.dma_start(nsa, RN[k][0:rows, NH:NH + 4, :]).then_inc(S[s], 16)
                    sp.dma_start(g_s[r], G12[k][0:rows, :]).then_inc(S[s], 16)
                    sp.dma_start(o_s[r, 3].rearrange("r h d -> r (h d)"), OD[k][0:rows, :]).then_inc(S[s], 16)
                    sp.dma_start(logf, LF[k][0:rows, :]).then_inc(S[s], 16)
                    if isinstance(t, int) and t == QT:
                        sp.dma_start(O["gmlp_v_s"][bass.ds(l, 1)].rearrange("o b t n -> (o b t) n"), VN[k][0:NS, :]).then_inc(S[s], 16)

                def store_step(t, k, m):
                    if not (isinstance(t, int) and t == 0):
                        store_tile(t - 1, 1 - k)

                over_tiles(sp, store_step)
                store_tile(8, 0)
                sp.wait_ge(S["tail_ev"], 1)
                sp.dma_start(O["conv_p"][bass.ds(l, 1)].rearrange("o b r n -> (o b r) n"), CPO[0:CW - 1, 0:GW]).then_inc(S["tail_out"], 16)
                sp.dma_start(O["conv_s"][bass.ds(l, 1), :, CW - 1 - NT:].rearrange("o b t n -> (o b) t n"),
                    CPO[0:NS, GW:2 * GW]).then_inc(S["tail_out"], 16)
                sp.wait_ge(S["y_done"], 1)
                sp.dma_start(y_s, Yc.rearrange("p c n -> p (c n)")).then_inc(S["y_out"], 16)
                sp.wait_ge(S["st0"], 16 * (11 * 5 + 1))
                sp.wait_ge(S["st1"], 16 * 11 * 4)
                sp.wait_ge(S["w_tok"], 80)
                sp.dma_start(O["nsa_win_p"][bass.ds(l, 1), 0].rearrange("o r c d -> (o r) c d"), kvc_s[SEQ - WIN:SEQ, 4:6, :]).then_inc(S["old_out"], 16)
                sp.dma_start(O["nsa_win_s"][bass.ds(l, 1), :, WIN - NT:].rearrange("o b t c d -> (o b) t c d"),
                    kvc_s[SEQ:ROWS, 4:6, :].rearrange("(b t) c d -> b t c d", b=NB)).then_inc(S["old_out"], 16)
                for h in range(NH):
                    sp.dma_start(suf_s[:, h, PAST:LK], ka_s[SEQ:ROWS, h, HD + 1].rearrange("(b t) -> b t", b=NB)).then_inc(S["old_out"], 16)
                sp.wait_ge(S["tail_out"], 32)
                sp.wait_ge(S["y_out"], 16)
                sp.wait_ge(S["old_out"], 128)
                arrive(sp, "sp")
                if stop <= 2:
                    return

                sp.wait_ge(S["zero_ready"], 1)
                sp.dma_start(PHI[0:HD, :, 0:HD], w("nsa_phi_k").rearrange("o (c d) e -> d (o c) e", d=HD)).then_inc(S["phi_in"], 16)
                sp.dma_start(PHI[HD:P, :, HD:P], w("nsa_phi_v").rearrange("o (c d) e -> d (o c) e", d=HD)).then_inc(S["phi_in"], 16)
                sp.dma_start(PE2[0:BLK, :].rearrange("p (s d) -> p s d", s=2), w("nsa_pe").rearrange("o s c d -> c (o s) d")).then_inc(S["pe_in"], 16)
                sp.dma_start(CP8.rearrange("p t (s d) -> p t s d", s=2), kvc_s[0:SEQ, 0:2, :].rearrange("(t p) s d -> p t s d", p=P)).then_inc(S["cp_in"], 16)

                with sp.Fori(0, NB) as i:
                    for k in range(4):
                        for j in range(4):
                            page = sp.value_load(pages[:, bass.ds(i * NPG + (4 * k + j), 1)], min_val=0, max_val=POOL - 1)
                            if j == 0:
                                sp.wait_ge(S["pg_T"], 4 * i + k + 1)
                            sp.dma_start(PG[k][:, j, :].rearrange("p (s d) -> p s d", s=2),
                                         A["cache_nsa_kv"][bass.ds(l, 1), bass.ds(page, 1), :, 0:2, :]
                                         .rearrange("o a p s d -> (o a p) s d")).then_inc(S[f"pg{k}"], 16)
                sp.wait_ge(S["suf_ready"], 1)
                for b in range(NB):
                    sp.dma_start(suf_s[b, :, 0:PAST].rearrange("h (j t) -> j h t", j=NPG),
                        PFX[b * NPG:(b + 1) * NPG, :, :]).then_inc(S["suf_out"], 16)
                sp.wait_ge(S["suf_out"], 16 * NB)
                sp.wait_ge(S["kvc_ready"], 1)
                arrive(sp, "sp")
                if stop <= 3:
                    return

                sp.dma_start(KV4, kvc_s[0:SEQ, 2:6, :].rearrange("(t p) g d -> p t g d", p=P)).then_inc(S["kv4_in"], 16)
                sp.wait_ge(S["kv4_in"], 16)
                arrive(sp, "sp")
                with sp.Fori(0, NH) as h:
                    one = bass.ds(h, 1)

                    def rows_of(x, width):
                        return x[0:SEQ, one, 0:width].rearrange("(t p) o d -> p t (o d)", p=P)

                    sp.dma_start(QF, rows_of(qa_s, AUG)).then_inc(S["head_in"], 16)
                    sp.dma_start(KF, rows_of(ka_s, AUG)).then_inc(S["head_in"], 16)
                    sp.dma_start(VF, rows_of(va_s, HD)).then_inc(S["head_in"], 16)
                    sp.dma_start(QN, rows_of(qc_s, HD)).then_inc(S["head_in"], 16)
                    sp.dma_start(GH, g_s[0:SEQ, bass.ds(h * 3, 3)].rearrange("(t p) c -> p t c", p=P)).then_inc(S["head_in"], 16)
                    sp.wait_ge(S["o_ready"], 1)
                    sp.dma_start(o_s[0:SEQ, 0, one, :].rearrange("(t p) o d -> p t (o d)", p=P), OF).then_inc(S["o_out"], 16)
                    sp.dma_start(o_s[0:SEQ, 2, one, :].rearrange("(t p) o d -> p t (o d)", p=P), ON).then_inc(S["o_out"], 16)
                    sp.wait_ge(S["o_out"], 32)
                    arrive(sp, "sp")
                if stop <= 4:
                    return

                sp.dma_start(QS[0:NS], qa_s[SEQ:ROWS, :, 0:HD]).then_inc(S["q_in"], 16)
                sp.dma_start(QCS[0:NS], qc_s[SEQ:ROWS]).then_inc(S["q_in"], 16)
                for h in range(NH):
                    r = slice(h * NT, (h + 1) * NT)
                    sp.dma_start(FQ[r, :], qa_s[SEQ:ROWS, h, HD].rearrange("(b t) -> t b", t=NT)).then_inc(S["aux_in"], 16)
                    sp.dma_start(GB[r], g_s[SEQ:ROWS, 3 * h:3 * h + 3].rearrange("(b t) c -> t b c", t=NT)).then_inc(S["aux_in"], 16)
                sp.wait_ge(S["rank_ready"], 1)
                sp.dma_start(sel_s, RK[0:NS, :]).then_inc(S["rank_out"], 16)
                sp.wait_ge(S["os_ready"], 1)
                for g in range(2):
                    sp.dma_start(oc_s[4 * g:4 * g + 4].rearrange("b r d -> (b r) d"), OCS[:, g, :]).then_inc(S["rank_out"], 16)
                sp.wait_ge(S["rank_out"], 48)
                sp.dma_start(OCB[0:32], oc_s.rearrange("b r d -> r b d")).then_inc(S["aux_in"], 16)
                for h in range(NH):
                    r = slice(h * NT, (h + 1) * NT)
                    sp.dma_start(SNB[r], sel_s.rearrange("(b t) j -> t b j", t=NT)).then_inc(S["aux_in"], 16)
                sp.wait_ge(S["aux_in"], 16 * 13)
                arrive(sp, "sp")
                if stop <= 5:
                    return

                with sp.Fori(0, NB // 2) as i:
                    for k in range(2):
                        b = 2 * i + k
                        row = bass.ds(SEQ + b * NT, NT)
                        bb = bass.ds(b, 1)
                        sp.wait_ge(S[f"kv_free{k}"], i + 1)
                        for j in range(NPG):
                            page = sp.value_load(pages[:, bass.ds(b * NPG + j, 1)], min_val=0, max_val=POOL - 1)
                            at = A["cache_fox_kv"][bass.ds(l, 1), bass.ds(page, 1)]
                            sp.dma_start(KVP[k][:, j, :], at.rearrange("o a p c h d -> (o a p) (c h d)")).then_inc(S[f"kv_in{k}"], 16)
                            at = A["cache_nsa_kv"][bass.ds(l, 1), bass.ds(page, 1), :, 2:4, :]
                            sp.dma_start(SLP[k][:, j, :].rearrange("p (s d) -> p s d", s=2),
                                at.rearrange("o a p s d -> (o a p) s d")).then_inc(S[f"kv_in{k}"], 16)
                        sp.dma_start(WNP[k], A["state_nsa_win"][bass.ds(l, 1), bb].rearrange("o b (j p) s d -> p (o b j) (s d)", p=P)).then_inc(S[f"kv_in{k}"], 16)
                        sp.dma_start(KNEW[k][0:NT, :].rearrange("p (h d) -> p h d", h=NH), ka_s[row, :, 0:HD]).then_inc(S[f"kv_in{k}"], 16)
                        sp.dma_start(VNEW[k][0:NT, :].rearrange("p (h d) -> p h d", h=NH), va_s[row]).then_inc(S[f"kv_in{k}"], 16)
                        sp.dma_start(KV4N[k][0:NT], kvc_s[row, 2:6, :]).then_inc(S[f"kv_in{k}"], 16)
                        sp.wait_ge(S["bias_free"], b + 1)
                        for h in range(NH):
                            sp.dma_start(BIAS[h * NT:(h + 1) * NT, :],
                                suf_s[bb, h, :].to_broadcast([NT, LK])).then_inc(S["bias_in"], 16)
                sp.wait_ge(S["os_out"], 16 * 2 * NB)
                arrive(sp, "sp")
                if stop <= 6:
                    return

                sp.dma_start(YB, y_s.rearrange("p (c n) -> p c n", c=2)).then_inc(S["y_in"], 16)
                sp.dma_start(GCB, w("gnorm_g")[:, 1, :].rearrange("o (c p) -> p (o c)", p=P)).then_inc(S["y_in"], 16)
                sp.dma_start(CLG, w("conv_ln_g").rearrange("o (c p) -> p (o c)", p=P)).then_inc(S["y_in"], 16)
                sp.dma_start(CLB, w("conv_ln_b").rearrange("o (c p) -> p (o c)", p=P)).then_inc(S["y_in"], 16)
                for n, g in enumerate((0, 2, 3)):
                    spread(GNB[:, n, :], w("gnorm_g")[:, g, :], "y_in")

                def oa_in(t, k, m):
                    rows = NS if isinstance(t, int) and t == QT else P
                    r = slice(SEQ, ROWS) if rows == NS else bass.ds(t * P, P)
                    if not (isinstance(t, int) and t < 2):
                        sp.wait_ge(S["oa_T"], t - 1)
                    if rows == NS:
                        for b in range(NB):
                            for g in range(2):
                                sp.dma_start(OA[k][b * NT:(b + 1) * NT, g, :].rearrange("p (h d) -> p h d", h=NH),
                                    of_s[b, g].rearrange("(h t) d -> t h d", h=NH)).then_inc(S[f"oa_in{k}"], 16)
                    else:
                        sp.dma_start(OA[k][0:rows, 0, :], o_s[r, 0].rearrange("r h d -> r (h d)")).then_inc(S[f"oa_in{k}"], 16)
                        sp.dma_start(OA[k][0:rows, 1, :], o_s[r, 2].rearrange("r h d -> r (h d)")).then_inc(S[f"oa_in{k}"], 16)
                    sp.dma_start(OA[k][0:rows, 2, :], o_s[r, 3].rearrange("r h d -> r (h d)")).then_inc(S[f"oa_in{k}"], 16)

                over_tiles(sp, oa_in)
                with sp.Fori(0, KD // 2) as i:
                    for k in range(2):
                        n = 2 * i + k
                        sp.wait_ge(S["w_lo"], n + 1)
                        sp.dma_start(WF[k][:, 0:KD, :], w("w_out")[:, :, bass.ds(n * P, P)].rearrange("o (k p) n -> p (o k) n", p=P)).then_inc(S[f"w_in{k}"], 16)
                arrive(sp, "sp")
                if stop <= 7:
                    return

                sp.dma_start(G2, w("norm2_g").rearrange("o (k p) -> p (o k)", p=P)).then_inc(S["gains"], 16)
                sp.wait_ge(S["gains"], 16)
                arrive(sp, "sp")
                with sp.Fori(0, 2) as half:
                    with sp.Fori(0, 8) as i:
                        for k in range(2):
                            n = 2 * i + k
                            sp.wait_ge(S["w_lo"], n + 1)
                            sp.dma_start(WF[k][:, 0:KD, :], w("w_ff1")[:, :, bass.ds(half * (DFF // 2) + n * P, P)]
                                .rearrange("o (k p) n -> p (o k) n", p=P)).then_inc(S[f"w_in{k}"], 16)
                    with sp.Fori(0, KD // 2) as i:
                        for k in range(2):
                            n = 2 * i + k
                            sp.wait_ge(S["w_lo"], 16 + n + 1)
                            sp.dma_start(WF[k], w("w_ff2")[:, bass.ds(half * (DFF // 2), DFF // 2), bass.ds(n * P, P)]
                                .rearrange("o (k p) n -> p (o k) n", p=P)).then_inc(S[f"w_in{k}"], 16)
                    arrive(sp, "sp")

            def row_out(t, k, m):
                sp.wait_ge(S["row_ev"], t + 1)
                if isinstance(t, int):
                    dst = O["y_prompt"][0, t * P:(t + 1) * P, :] if t < QT else O["y_sample"].rearrange("b t d -> (b t) d")
                    rows = P if t < QT else NS
                else:
                    dst, rows = O["y_prompt"][0, bass.ds(t * P, P), :], P
                sp.dma_start(dst, XS[k][0:rows, :]).then_inc(S[f"row_out{k}"], 16)

            over_tiles(sp, row_out)
            sp.wait_ge(S["row_out0"], 16 * 5)
            sp.wait_ge(S["row_out1"], 16 * 4)

        @block.tensor
        def _(pe):
            mm, tr = nc.tensor.matmul, nc.tensor.transpose

            def rows_of(t):
                return NS if isinstance(t, int) and t == QT else P

            pe.wait_ge(loaded_once, 48)

            def row_T(t, k, m):
                r = rows_of(t)
                pe.wait_ge(S[f"row_in{k}"], 16 * (m + 1))
                if not (isinstance(t, int) and t < 2):
                    pe.wait_ge(S["row_ev"], t - 1)
                for j in range(KD):
                    at = (2 * k + j // 4) * 512 + (j % 4) * P
                    last = tr(PS[:, at:at + r], XS[k][0:r, j * P:(j + 1) * P], ident[0:r, 0:r])
                last.then_inc(S["row_T"], 1)

            over_tiles(pe, row_T)
            arrive(pe, "pe")

            def sum_squares(src, ready, summed):
                for k in range(KD):
                    pe.wait_ge(S[ready], k + 1)
                    for a, n in zip(STARTS, WIDTHS):
                        last = mm(PS[:, a:a + n], ones, src[:, k % 2, a:a + n], start=k == 0, stop=k == KD - 1)
                    last.then_inc(S[summed], 1)

            def gemm(k, blocks, xh, xl, wh, wl):
                base_col = 1536 * k
                for c in range(blocks):
                    for n, (ww, xx) in enumerate(((wh, xh), (wh, xl), (wl, xh))):
                        for a, wd in zip(STARTS, WIDTHS):
                            last = mm(PS[:, base_col + a:base_col + a + wd], ww[:, c, :], xx[:, c, a:a + wd],
                                      start=c == 0 and n == 0, stop=c == blocks - 1 and n == 2)
                return last

            with pe.Fori(0, layers) as l:
                sum_squares(SQ2, "sq_ready", "sq_summed")
                pe.wait_ge(S["w_glu"], 16)
                pe.wait_ge(S["xn_ready"], KD)
                for f in range(2):
                    if f:
                        pe.wait_ge(S["glu_done"], 1)
                    for s in range(2):
                        for k in range(KD):
                            for a, n in zip(STARTS, WIDTHS):
                                last = mm(PS[:, 1536 * s + a:1536 * s + a + n],
                                          Wg[:, k, (2 * s + f) * P:(2 * s + f + 1) * P],
                                          XNT[:, k, a:a + n], start=k == 0, stop=k == KD - 1)
                    last.then_inc(S["glu_mm"], 1)
                pe.wait_ge(S["ct_in"], 16)
                n = NB // 2 * (CW - 1)
                for g in range(2):
                    for c in range(2):
                        at = 3072 + (2 * g + c) * n
                        last = tr(PS[:, at:at + n], CS[0:n, g, c * P:(c + 1) * P], ident[0:n, 0:n])
                last.then_inc(S["ct_T"], 1)
                pe.wait_ge(S["wm_raw"], 2)
                for g in range(4):
                    last = tr(PS[:, 3584 + g * P:3584 + (g + 1) * P], WMr[:, g, :], ident)
                last.then_inc(S["wm_T"], 1)
                pe.wait_ge(S["glu_done"], 2)
                for g in range(4):
                    last = tr(PS[0:NS, g * NS:(g + 1) * NS], WM8r[0:NS, g, :], ident[0:NS, 0:NS])
                last.then_inc(S["wm_T"], 1)
                pe.wait_ge(S["wm_ev"], 2)
                pe.wait_ge(S["w_tok"], 80)

                def small(t, k):
                    r = rows_of(t)
                    pe.wait_ge(S["lf_ready"], t + 1)
                    if not (isinstance(t, int) and t == 0):
                        pe.wait_ge(S["fin"], t)
                    tri, wm = (triu, WMT) if r == P else (C("btriu"), WM8T)
                    mm(PS[0:r, 2560:2564], tri[0:r, 0:r], LF[k][0:r, :], start=True, stop=True)
                    mm(PS[0:r, 2564:2568], ones[0:r, 0:r], LF[k][0:r, :], start=True, stop=True)
                    for g in range(4):
                        last = mm(PS[0:r, 3072 + g * HD:3072 + (g + 1) * HD], wm[0:r, g, :],
                                  VN[k][0:r, g * HD:(g + 1) * HD], start=True, stop=True)
                    last.then_inc(S["small_mm"], 1)

                def z_step(t, k, m):
                    r = rows_of(t)
                    pe.wait_ge(S["xt_ready"], t + 1)
                    for c, (a, b) in enumerate(CHUNKS):
                        if not (isinstance(t, int) and t == 0):
                            pe.wait_ge(S["z_ev"], 8 * (t - 1) + (2, 3, 5, 7, 8)[c])
                        for j in range(KD):
                            last = mm(PS[0:r, c * 512:c * 512 + b - a], XTT[k][:, j, 0:r], Wt[:, j, a:b],
                                      start=j == 0, stop=j == KD - 1)
                        last.then_inc(S["z_mm"], 1)
                    if not (isinstance(t, int) and t == 0):
                        small(t - 1, 1 - k)

                over_tiles(pe, z_step)
                small(8, 0)
                for c in range(2):
                    tr(PS[0:CW - 1, 3584 + c * P:3584 + (c + 1) * P], GL[:, c, SEQ:SEQ + CW - 1], ident)
                    last = tr(PS[0:NS, 3840 + c * P:3840 + (c + 1) * P], SGL[:, c, :], ident)
                last.then_inc(S["tail_T"], 1)
                arrive(pe, "pe")
                if stop <= 2:
                    return

                pe.sem_inc(S["pg_T"], 4)
                pe.wait_ge(S["pe_in"], 16)
                tr(bank(6, BLK), PE2[0:BLK, :], ident[0:BLK, 0:BLK]).then_inc(S["kvc_mm"], 1)
                pe.wait_ge(S["cp_in"], 16)
                for g in range(2):
                    for j in range(4):
                        last = tr(bank(4 + g)[:, j * P:(j + 1) * P], CP8[:, 4 * g + j, :], ident)
                last.then_inc(S["kvc_mm"], 1)
                with pe.Fori(0, NB) as i:
                    for k in range(4):
                        pe.wait_ge(S[f"pg{k}"], 64 * i + 64)
                        pe.wait_ge(S["pg_evA" if k % 2 == 0 else "pg_evD"], 2 * i + k // 2 + 1)
                        for j in range(4):
                            last = tr(bank(k)[:, j * P:(j + 1) * P], PG[k][:, j, :], ident)
                        last.then_inc(S["pg_T"], 1)
                pe.wait_ge(S["tot_ready"], 1)
                mm(bank(7, 4), C("later"), TOT, start=True, stop=True).then_inc(S["lat_mm"], 1)
                pe.wait_ge(S["phi_in"], 32)
                pe.wait_ge(S["pg_evA"], 2 * NB + 3)
                pe.wait_ge(S["pg_evD"], 2 * NB + 2)
                blocks = CT.rearrange("p (n c) -> p n c", c=BLK)
                for a, n in ((0, 272), (272, 273)):
                    for c in range(BLK):
                        last = mm(bank(0 if a == 0 else 1, n), PHI[:, c, :], blocks[:, a:a + n, c],
                                  start=c == 0, stop=c == BLK - 1)
                last.then_inc(S["kvc_mm"], 1)
                arrive(pe, "pe")
                if stop <= 3:
                    return

                def transposes(src, dst_rows, g, at_bank):
                    for j in range(4):
                        last = tr(bank(at_bank)[0:dst_rows, j * P:(j + 1) * P], src[:, 4 * g + j, :], ident)
                    last.then_inc(S["tr_T"], 1)

                pe.wait_ge(S["kv4_in"], 16)
                for n, (src, g) in enumerate(((0, 0), (0, 1), (2, 0), (2, 1))):
                    if n >= 2:
                        pe.wait_ge(S["tr_ev"], n - 1)
                    transposes(KV4[:, :, src, :], HD, g, 4 + n % 2)
                pe.wait_ge(S["vb_ready"], 1)
                tr(bank(7, HD), VREP[HD:P].rearrange("p i n -> p (i n)"), ident[HD:P, HD:P]).then_inc(S["vb_ready"], 1)
                arrive(pe, "pe")

                units = [(kind, i) for kind in ("sel", "fox", "win") for i in range(QT)]

                def keys_of(u):
                    kind, i = units[u]
                    return list(range(max(0, i - WIN // P) if kind == "win" else 0, i + 1))

                with pe.Fori(0, NH) as h:
                    pe.wait_ge(S["head_in"], 80)
                    for n, (src, r) in enumerate(((QN, HD), (QN, HD), (QF, AUG), (QF, AUG), (KF, AUG), (KF, AUG))):
                        if n >= 2:
                            pe.wait_ge(S["tr_ev"], n - 1)
                        transposes(src, r, n % 2, 4 + n % 2)
                    pe.wait_ge(S["tr_ev"], 6)
                    for i in range(QT):
                        last = mm(bank(7)[:, i * NPB:(i + 1) * NPB], QNT[0:HD, i * P:(i + 1) * P], KVC[0:HD, 512:544],
                                  start=True, stop=True)
                    last.then_inc(S["cs_mm"], 1)

                    def scores(u):
                        kind, i = units[u]
                        if u >= 2:
                            pe.wait_ge(S["p_ready"], u - 1)
                        q, kt, rows = {"sel": (QNT, KST, HD), "win": (QNT, KWT, HD), "fox": (QFT, KFT, AUG)}[kind]
                        js = keys_of(u)
                        for a in range(0, len(js), 4):
                            part = js[a:a + 4]
                            at = (u % 2) * 1024 + a * P
                            masks = []
                            if kind == "win" and i >= 4 and a == 0:
                                masks.append((0, wnegb))
                            if part[-1] == i:
                                masks.append((len(part) - 1, cnegb))
                            last = mm(PS[:, at:at + len(part) * P], q[0:rows, i * P:(i + 1) * P],
                                      kt[0:rows, part[0] * P:(part[-1] + 1) * P], start=True, stop=not masks)
                            for n, (c, mask) in enumerate(masks):
                                last = mm(PS[:, at + c * P:at + (c + 1) * P], identb, mask,
                                          start=False, stop=n == len(masks) - 1)
                        last.then_inc(S["s_mm"], 1)

                    groups = 0
                    scores(0)
                    scores(1)
                    pe.wait_ge(S["cp_ready"], 1)
                    for g in range(2):
                        last = tr(bank(7)[:, 256 + g * P:256 + (g + 1) * P],
                                  SC.rearrange("p t n -> p (t n)")[:, g * P:(g + 1) * P], ident)
                    last.then_inc(S["cpt_T"], 1)
                    pe.wait_ge(S["cpt_ev"], 1)
                    for g in range(2):
                        last = mm(bank(7)[:, g * GW:(g + 1) * GW], PTC[:, g, :],
                                  VBD.rearrange("p i d -> p (i d)"), start=True, stop=True)
                    last.then_inc(S["cpv_mm"], 1)
                    for u, (kind, i) in enumerate(units):
                        js = keys_of(u)
                        pe.wait_ge(S["p_ready"], u + 1)
                        for a in range(0, len(js), 4):
                            if groups >= 2:
                                pe.wait_ge(S["pt_ev"], groups - 1)
                            for j in range(a, min(a + 4, len(js))):
                                last = tr(bank(4 + groups % 2)[:, (j - a) * P:(j - a + 1) * P],
                                          PR[u % 2][:, j * P:(j + 1) * P], ident)
                            last.then_inc(S["pt_T"], 1)
                            groups += 1
                        if u + 2 < len(units):
                            scores(u + 2)
                        pe.wait_ge(S["pt_ev"], groups)
                        if u >= 2:
                            pe.wait_ge(S["o_done"], u - 1)
                        if u == 1:
                            pe.wait_ge(S["on_ready"], 1)
                        for n, j in enumerate(js):
                            v = {"fox": VF[:, j, :], "sel": KV4[:, j, 1, :], "win": KV4[:, j, 3, :]}[kind]
                            last = mm(bank(6 + u % 2, HD), PTR[u % 2][:, n * P:(n + 1) * P], v,
                                      start=n == 0, stop=n == len(js) - 1)
                        last.then_inc(S["pv_mm"], 1)
                    arrive(pe, "pe")
                if stop <= 4:
                    return

                pe.wait_ge(S["q_in"], 32)
                for a in range(2):
                    tr(bank(0)[:, a * NS:(a + 1) * NS], QS[0:NS].rearrange("p h d -> p (h d)")[:, a * P:(a + 1) * P], ident[0:NS, 0:NS])
                for h in range(NH):
                    last = tr(bank(1)[0:HD, h * NS:(h + 1) * NS], QCS[0:NS, h, :], ident[0:NS, 0:NS])
                last.then_inc(S["q_T"], 1)
                for b in range(NB):
                    last = tr(bank(2 + b // 4)[0:NCB, (b % 4) * P:(b % 4 + 1) * P], KVC[:, b * NCB:(b + 1) * NCB], ident)
                last.then_inc(S["q_T"], 1)
                pe.wait_ge(S["q_ev"], 1)
                for b in range(NB):
                    g, r = b // 4, (b % 4) * 32
                    last = mm(bank(4)[r:r + 32, g * NCB:(g + 1) * NCB], QNALL[0:HD, b, :],
                              KVC[0:HD, b * NCB:(b + 1) * NCB], start=True, stop=True)
                last.then_inc(S["sc_mm"], 1)
                pe.wait_ge(S["sm_ready"], 1)
                for g in range(2):
                    mm(bank(5)[g * 32:(g + 1) * 32, 0:NCB], C("hsum"), PC[:, g, :], start=True, stop=True)
                for g in range(2):
                    last = tr(bank(6)[0:NCB, g * P:(g + 1) * P], PC[:, g, :], ident)
                last.then_inc(S["imp_mm"], 1)
                pe.wait_ge(S["vct_ev"], 3)
                for b in range(NB):
                    g, r = b // 4, (b % 4) * 32
                    last = mm(bank(7)[r:r + 32, g * HD:(g + 1) * HD], PTCs[0:NCB, g, r:r + 32],
                              VCT[0:NCB, b, HD:P], start=True, stop=True)
                last.then_inc(S["imp_mm"], 1)
                arrive(pe, "pe")
                if stop <= 5:
                    return

                def key_groups(k, what):
                    if what == "fox":
                        return [(KVP[k][:, 4 * g:4 * g + 4, a * P:(a + 1) * P], P) for a in range(2) for g in range(4)]
                    if what == "sel":
                        return [(SLP[k][:, 4 * g:4 * g + 4, 0:HD], HD) for g in range(4)]
                    return [(WNP[k][:, :, 0:HD], HD)]

                for k in range(2):
                    pe.sem_inc(S[f"kv_free{k}"], 1)
                with pe.Fori(0, NB // 2) as i:
                    count = {"kt": 0, "s": 0, "pt": 0}

                    def key_T(k, what):
                        for src, r in key_groups(k, what):
                            g = count["kt"]
                            if g >= 2:
                                pe.wait_ge(S["kt_evA" if g % 2 == 0 else "kt_evD"], g // 2)
                            for j in range(4):
                                last = tr(bank(g % 2)[0:r, j * P:(j + 1) * P], src[:, j, :], ident)
                            last.then_inc(S["kt_T"], 1)
                            count["kt"] += 1

                    def keys_out():
                        pe.wait_ge(S["kt_evA"], (count["kt"] + 1) // 2)
                        pe.wait_ge(S["kt_evD"], count["kt"] // 2)

                    def sample_scores(parts, keys):
                        for a in range(0, keys, 512):
                            n = min(512, keys - a)
                            if count["s"] >= 2:
                                pe.wait_ge(S["sc_ev"], count["s"] - 1)
                            for m, (q, kt, r) in enumerate(parts):
                                last = mm(bank(2 + count["s"] % 2)[0:32, 0:n], q[0:r, :], kt[0:r, a:a + n],
                                          start=m == 0, stop=m == len(parts) - 1)
                            last.then_inc(S["sc_mm"], 1)
                            count["s"] += 1

                    def mix(k, probs, pages_n, value, new_value, width, col, order):
                        pe.wait_ge(S["e_ready"], order)
                        if count["pt"] >= 1:
                            pe.wait_ge(S["ptn_ev"], count["pt"])
                        for j in range(pages_n):
                            tr(bank(4)[:, j * 32:(j + 1) * 32], probs[0:32, j * P:(j + 1) * P], ident[0:32, 0:32])
                        tr(bank(6)[0:NT, 0:32], probs[0:32, pages_n * P:pages_n * P + NT],
                           ident[0:32, 0:32]).then_inc(S["ptn_T"], 1)
                        count["pt"] += 1
                        pe.wait_ge(S["ptn_ev"], count["pt"])
                        if order > 1:
                            pe.wait_ge(S["ov_done"], order - 1)
                        for j in range(pages_n):
                            mm(bank(5)[0:32, col:col + width], PTF[:, j, :], value(j), start=j == 0, stop=False)
                        mm(bank(5)[0:32, col:col + width], PTF[0:NT, 16, :], new_value, start=False,
                           stop=True).then_inc(S["ov_mm"], 1)

                    for k in range(2):
                        pe.wait_ge(S[f"kv_in{k}"], 576 * i + 576)
                        key_T(k, "fox")
                        for a in range(2):
                            tr(bank(7)[:, a * NT:(a + 1) * NT], KNEW[k][0:NT, a * P:(a + 1) * P], ident[0:NT, 0:NT])
                        tr(bank(7)[0:HD, 16:24], KV4N[k][0:NT, 0, :], ident[0:NT, 0:NT])
                        tr(bank(7)[0:HD, 24:32], KV4N[k][0:NT, 2, :], ident[0:NT, 0:NT]).then_inc(S["new_T"], 1)
                        pe.wait_ge(S["new_ev"], k + 1)
                        pe.wait_ge(S["qb_ready"], k + 1)
                        keys_out()
                        sample_scores([(QB[:, 0, :], KT2[:, 0, :], P), (QB[:, 1, :], KT2[:, 1, :], P)], LK)
                        key_T(k, "sel")
                        keys_out()
                        sample_scores([(QNB, KSTs, HD)], LK)
                        key_T(k, "win")
                        keys_out()
                        sample_scores([(QNB, KWTs, HD)], WIN + NT)
                        mix(k, SF, NPG, lambda j: KVP[k][:, j, GW:2 * GW], VNEW[k][0:NT, :], GW, 0, 3 * k + 1)
                        mix(k, SSL, NPG, lambda j: SLP[k][:, j, HD:P], KV4N[k][0:NT, 1, :], HD, GW, 3 * k + 2)
                        mix(k, SW, 4, lambda j: WNP[k][:, j, HD:P], KV4N[k][0:NT, 3, :], HD, GW + HD, 3 * k + 3)
                        pe.drain().then_inc(S[f"kv_free{k}"], 1)
                    arrive2(pe, "pe")
                arrive(pe, "pe")
                if stop <= 6:
                    return

                pe.wait_ge(S["y_in"], 112)
                for n in range(3):
                    if n:
                        pe.wait_ge(S["y_sq"], n)
                    src = (YB, YQ, YQ)[n]
                    for c in range(2):
                        for a, wd in zip(STARTS, WIDTHS):
                            last = mm(PS[:, a:a + wd], ones, src[:, c, a:a + wd], start=c == 0, stop=c == 1)
                    last.then_inc(S["y_mm"], 1)

                def oa_T(t, k, m):
                    r = rows_of(t)
                    pe.wait_ge(S["oa_ready"], t + 1)
                    if not (isinstance(t, int) and t < 2):
                        pe.wait_ge(S["oa_ev"], t - 1)
                    for j in range(6):
                        at = (4 + 2 * k) * 512 + j * P if j < 2 else (5 + 2 * k) * 512 + (j - 2) * P
                        last = tr(PS[:, at:at + r], OA[k][0:r, j // 2, (j % 2) * P:(j % 2 + 1) * P], ident[0:r, 0:r])
                    last.then_inc(S["oa_T"], 1)

                over_tiles(pe, oa_T)
                arrive2(pe, "pe")
                pe.sem_inc(S["g_mm"], 2)
                with pe.Fori(0, KD // 2) as i:
                    for k in range(2):
                        n = 2 * i + k
                        pe.wait_ge(S["w_lo"], n + 3)
                        pe.wait_ge(S["g_ev"], n + 1)
                        gemm(k, KD, OTH, OTL, WH[k], WL[k]).then_inc(S["g_mm"], 1)
                arrive(pe, "pe")
                if stop <= 7:
                    return

                arrive(pe, "pe")
                sum_squares(SQN2, "sq_ready", "sq_summed")
                pe.wait_ge(S["xn_ready"], KD)
                arrive2(pe, "pe")
                with pe.Fori(0, 2) as half:
                    pe.sem_inc(S["g_mm"], 2)
                    with pe.Fori(0, 8) as i:
                        for k in range(2):
                            n = 2 * i + k
                            pe.wait_ge(S["w_lo"], n + 3)
                            pe.wait_ge(S["g_ev"], n + 1)
                            gemm(k, KD, XNH, XNL, WH[k], WL[k]).then_inc(S["g_mm"], 1)
                    pe.wait_ge(S["u_ready"], 18)
                    with pe.Fori(0, KD // 2) as i:
                        for k in range(2):
                            n = 2 * i + k
                            pe.wait_ge(S["w_lo"], 16 + n + 3)
                            pe.wait_ge(S["g_ev"], 16 + n + 1)
                            gemm(k, 16, UH, UL, WH[k], WL[k]).then_inc(S["g_mm"], 1)
                    arrive(pe, "pe")

            def row_out(t, k, m):
                r = rows_of(t)
                pe.wait_ge(S["row_cp"], t + 1)
                if not (isinstance(t, int) and t < 2):
                    pe.wait_ge(S["row_ev"], t - 1)
                for j in range(KD):
                    at = (2 * k + j // 4) * 512 + (j % 4) * P
                    last = tr(PS[0:r, at:at + P], XO[k][:, j, 0:r], ident)
                last.then_inc(S["row_T"], 1)

            over_tiles(pe, row_out)

        @block.scalar
        def _(act):
            run = nc.scalar.activation

            def rows_of(t):
                return NS if isinstance(t, int) and t == QT else P

            def cols(t):
                return bass.ds(t * P, rows_of(t)) if not isinstance(t, int) else slice(t * P, t * P + rows_of(t))

            def row_ev(t, k, m):
                r = rows_of(t)
                act.wait_ge(S["row_T"], t + 1)
                for g in range(2):
                    last = run(XT[:, 4 * g:4 * g + 4, cols(t)],
                               PS[:, (2 * k + g) * 512:(2 * k + g + 1) * 512].rearrange("p (j n) -> p j n", j=4)[:, :, 0:r],
                               ACT.Copy)
                last.then_inc(S["row_ev"], 1)

            over_tiles(act, row_ev)
            arrive(act, "act")

            def squares(dst):
                for k in range(KD):
                    if k >= 2:
                        act.wait_ge(S["sq_summed"], k - 1)
                    run(dst[:, k % 2, :], XT[:, k, :], ACT.Square).then_inc(S["sq_ready"], 1)

            def root(x, n):
                act.wait_ge(S["col_mean"], n)
                run(x, x, ACT.Sqrt).then_inc(S["col_rstd"], 1)

            def split_weights(k, blocks, n, pair):
                act.wait_ge(S[f"w_in{k}"], 16 * (pair + 1))
                act.wait_ge(S["g_mm"], n + 1)
                run(WH[k][:, 0:blocks, :], WF[k][:, 0:blocks, :], ACT.Copy).then_inc(S["w_hi"], 1)

            with act.Fori(0, layers) as l:
                chain = Chain(act, S["act_done"])
                squares(SQ2)
                root(RST, 1)
                for f in range(2):
                    act.wait_ge(S["glu_mm"], f + 1)
                    if f:
                        act.wait_ge(S["glu_done"], 1)
                    run(SG, PS[:, 1536:1536 + ROWS], ACT.Sigmoid).then_inc(S["glu_sig"], 1)
                act.wait_ge(S["ct_T"], 1)
                n = NB // 2 * (CW - 1)
                for g in range(2):
                    for c in range(2):
                        at = 3072 + (2 * g + c) * n
                        last = run(GLS[:, c, 4 * g:4 * g + 4, 0:CW - 1],
                                   PS[:, at:at + n].rearrange("p (b r) -> p b r", r=CW - 1), ACT.Copy)
                last.then_inc(S["ct_ev"], 1)
                act.wait_ge(S["wm_T"], 1)
                run(WMT, PS[:, 3584:4096].rearrange("p (g n) -> p g n", g=4), ACT.Copy).then_inc(S["wm_ev"], 1)
                act.wait_ge(S["wm_T"], 2)
                run(WM8T[0:NS], PS[0:NS, 0:4 * NS].rearrange("p (g n) -> p g n", g=4), ACT.Copy).then_inc(S["wm_ev"], 1)
                act.wait_ge(S["glu_done"], 2)

                def xt(t, k):
                    r = rows_of(t)
                    if not (isinstance(t, int) and t < 2):
                        act.wait_ge(S["z_mm"], 5 * (t - 1))
                    run(XTT[k][:, :, 0:r], XNT[:, :, cols(t)], ACT.Copy).then_inc(S["xt_ready"], 1)

                xt(0, 0)

                def z_out(t, k, m):
                    r = rows_of(t)
                    if not (isinstance(t, int) and t == QT):
                        xt(t + 1, 1 - k)
                    if not (isinstance(t, int) and t == 0):
                        act.wait_ge(S["z_free"], t)
                    if not (isinstance(t, int) and t < 2):
                        act.wait_ge(S[f"st{k}"], 176 * m)
                        act.wait_ge(S["fin"], t - 1)

                    def out(c, dst, width, func=ACT.Copy):
                        act.wait_ge(S["z_mm"], 5 * t + c + 1)
                        run(dst, PS[0:r, c * 512:c * 512 + width], func).then_inc(S["z_ev"], 1)

                    out(0, Z[0:r, 0:512], 512)
                    out(0, SQ[0:r, 0:512], 512, ACT.Square)
                    out(1, VB[k][0:r, :], 260)
                    out(2, Z[0:r, 512:896], 384)
                    out(2, SQ[0:r, 512:896], 384, ACT.Square)
                    out(3, Z[0:r, 896:1164], 268)
                    out(3, SQ[0:r, 896:1152], 256, ACT.Square)
                    out(4, UV[k][0:r, :], 512)
                    act.wait_ge(S["z_ev"], 8 * t + 8)
                    run(EX[0:r, 0:12], Z[0:r, 1152:1164], ACT.Exp, scale=-1.0).then_inc(S["ex_ready"], 1)
                    act.wait_ge(S["na_ready"], t + 1)
                    run(EX[0:r, 16:20], EX[0:r, 32:36], ACT.Exp).then_inc(S["ex_ready"], 1)

                over_tiles(act, z_out)
                act.wait_ge(S["tail_T"], 1)
                run(CPO[0:CW - 1, 0:GW], PS[0:CW - 1, 3584:3584 + GW], ACT.Copy)
                run(CPO[0:NS, GW:2 * GW], PS[0:NS, 3840:3840 + GW], ACT.Copy).then_inc(S["tail_ev"], 1)
                arrive(act, "act")
                if stop <= 2:
                    return

                act.sem_inc(S["pg_evA"], 1)
                act.wait_ge(S["kvc_mm"], 1)
                run(CT[:, NTOK:NTOK + BLK], bank(6, BLK), ACT.Copy).then_inc(S["pg_evA"], 1)
                with act.Fori(0, NB) as i:
                    for k in (0, 2):
                        act.wait_ge(S["pg_T"], 4 * i + k + 5)
                        run(CT[:, bass.ds((4 * i + k) * 512, 512)], bank(k), ACT.Copy).then_inc(S["pg_evA"], 1)
                act.wait_ge(S["kvc_mm"], 2)
                run(CT[:, NB * PAST:NB * PAST + 512], bank(4), ACT.Copy).then_inc(S["pg_evA"], 1)
                arrive(act, "act")
                if stop <= 3:
                    return

                for n, dst in enumerate((KST, KST, KWT, KWT)):
                    act.wait_ge(S["tr_T"], n + 1)
                    run(dst[0:HD, (n % 2) * 512:(n % 2 + 1) * 512], bank(4 + n % 2)[0:HD, :], ACT.Copy).then_inc(S["tr_ev"], 1)
                arrive(act, "act")
                units = [(kind, i) for kind in ("sel", "fox", "win") for i in range(QT)]
                with act.Fori(0, NH) as h:
                    for n, (dst, r) in enumerate(((QNT, HD), (QNT, HD), (QFT, AUG), (QFT, AUG), (KFT, AUG), (KFT, AUG))):
                        act.wait_ge(S["tr_T"], n + 1)
                        run(dst[0:r, (n % 2) * 512:(n % 2 + 1) * 512], bank(4 + n % 2)[0:r, :], ACT.Copy).then_inc(S["tr_ev"], 1)
                    act.wait_ge(S["cs_ready"], 1)
                    run(SC, SC, ACT.Exp).then_inc(S["ce_ready"], 1)
                    done = []
                    for u, (kind, i) in enumerate(units):
                        width = P * (min(i, WIN // P) + 1 if kind == "win" else i + 1)
                        done.append((done[-1] if done else 0) + -(-width // 512))
                        act.wait_ge(S["nm_ready"], u + 1)
                        if u >= 2:
                            act.wait_ge(S["pt_T"], done[u - 2])
                        run(PR[u % 2][:, 0:width], PS[:, (u % 2) * 1024:(u % 2) * 1024 + width], ACT.Exp,
                            bias=NMX[:, u:u + 1], accum_out=RS[:, u:u + 1]).then_inc(S["p_ready"], 1)
                        if u == 1:
                            act.wait_ge(S["cpt_T"], 1)
                            run(PTC, bank(7)[:, 256:512].rearrange("p (g n) -> p g n", g=2), ACT.Copy).then_inc(S["cpt_ev"], 1)
                    arrive(act, "act")
                if stop <= 4:
                    return

                act.wait_ge(S["q_T"], 2)
                for g in range(2):
                    run(VCT[0:NCB, 4 * g:4 * g + 4, :], bank(2 + g)[0:NCB, :].rearrange("p (b n) -> p b n", b=4),
                        ACT.Copy).then_inc(S["vct_ev"], 1)
                act.wait_ge(S["mx_ready"], 1)
                run(PC, PC, ACT.Exp).then_inc(S["e_ready"], 1)
                act.wait_ge(S["imp_mm"], 1)
                run(PTCs[0:NCB], bank(6)[0:NCB, 0:2 * P].rearrange("p (g n) -> p g n", g=2), ACT.Copy).then_inc(S["vct_ev"], 1)
                arrive(act, "act")
                if stop <= 5:
                    return

                with act.Fori(0, NB // 2) as i:
                    for k in range(2):
                        def keys_out(what):
                            first = 13 * k + {"fox": 0, "sel": 8, "win": 12}[what]
                            n = {"fox": 8, "sel": 4, "win": 1}[what]
                            for g in range(first, first + n):
                                if g % 2:
                                    continue
                                j = g - first
                                act.wait_ge(S["kt_T"], g + 1)
                                if what == "fox":
                                    dst, r = KT2[:, j // 4, (j % 4) * 512:(j % 4 + 1) * 512], P
                                elif what == "sel":
                                    dst, r = KSTs[0:HD, j * 512:(j + 1) * 512], HD
                                else:
                                    dst, r = KWTs[0:HD, 0:512], HD
                                run(dst, bank(g % 2)[0:r, :], ACT.Copy).then_inc(S["kt_evA"], 1)

                        def probs(n, s, width):
                            act.wait_ge(S["mx_ready"], 3 * k + n + 1)
                            run(s[0:32, 0:width], s[0:32, 0:width], ACT.Exp, bias=ST[0:32, n:n + 1],
                                accum_out=ST[0:32, 3 + n:4 + n]).then_inc(S["e_ready"], 1)

                        def probs_T(n, pages_n):
                            act.wait_ge(S["ptn_T"], 3 * k + n + 1)
                            run(PTF[:, 0:pages_n, :], bank(4)[:, 0:pages_n * 32].rearrange("p (j n) -> p j n", n=32), ACT.Copy)
                            run(PTF[0:NT, 16, :], bank(6)[0:NT, 0:32], ACT.Copy).then_inc(S["ptn_ev"], 1)

                        keys_out("fox")
                        keys_out("sel")
                        if k:
                            act.wait_ge(S["ov_done"], 3)
                        probs(0, SF, LK)
                        keys_out("win")
                        probs(1, SSL, LK)
                        probs_T(0, NPG)
                        probs(2, SW, WIN + NT)
                        probs_T(1, NPG)
                        probs_T(2, 4)
                        b = 2 * i + k
                        act.wait_ge(S["os_ready"], 2 * k + 2)
                        act.dma_start(of_s[bass.ds(b, 1), 0].rearrange("b r d -> (b r) d"), OH[k][0:32, :]).then_inc(S["os_out"], 16)
                        act.dma_start(of_s[bass.ds(b, 1), 1].rearrange("b r d -> (b r) d"), OCM[k][0:32, :]).then_inc(S["os_out"], 16)
                    arrive2(act, "act")
                arrive(act, "act")
                if stop <= 6:
                    return

                root(YM, 1)
                act.wait_ge(S["y_c"], 1)
                run(YQ, YB, ACT.Sigmoid).then_inc(S["y_c"], 1)
                root(YM, 2)
                chain.restart()

                def oa_squares(t, k, m):
                    r = rows_of(t)
                    if isinstance(t, int) and t == QT:
                        act.wait_ge(S[f"oa_in{k}"], 48 * m + 17 * 16)
                    else:
                        act.wait_ge(S[f"oa_in{k}"], 48 * m + 48)
                    if not (isinstance(t, int) and t < 2):
                        act.wait_ge(S["oa_ready"], t - 1)
                    for g in range(3):
                        run(OAQ[0:r, :], OA[k][0:r, g, :], ACT.Square, accum_out=S3[k][0:r, g:g + 1]).then_inc(S["act_done"], 1)
                        act.wait_ge(S["act_done"], chain.next())
                    act.sem_inc(S["ss_ready"], 1)

                oa_squares(0, 0, 0)

                def oa(t, k, m):
                    r = rows_of(t)
                    if not (isinstance(t, int) and t == QT):
                        oa_squares(t + 1, 1 - k, m if k == 0 else m + 1)
                    act.wait_ge(S["oa_T"], t + 1)
                    run(OTH[:, 0:2, cols(t)], PS[:, (4 + 2 * k) * 512:(4 + 2 * k) * 512 + 256]
                        .rearrange("p (j n) -> p j n", j=2)[:, :, 0:r], ACT.Copy)
                    run(OTH[:, 4:8, cols(t)], PS[:, (5 + 2 * k) * 512:(6 + 2 * k) * 512]
                        .rearrange("p (j n) -> p j n", j=4)[:, :, 0:r], ACT.Copy).then_inc(S["oa_hi"], 1)

                over_tiles(act, oa, chain)
                arrive2(act, "act")
                with act.Fori(0, KD // 2) as i:
                    for k in range(2):
                        split_weights(k, KD, 2 * i + k, i)
                arrive(act, "act")
                if stop <= 7:
                    return

                arrive(act, "act")
                squares(SQN2)
                root(RST2, 1)
                for k in range(KD):
                    act.wait_ge(S["xn_ready"], k + 1)
                    run(XNH[:, k, :], XR[:, k, :], ACT.Copy).then_inc(S["xh_ready"], 1)
                arrive2(act, "act")
                with act.Fori(0, 2) as half:
                    chain.restart()

                    def up(n, k):
                        act.wait_ge(S["g_mm"], n + 3)
                        act.wait_ge(S["u_ready"], n + 1)
                        run(RL[k], PS[:, 1536 * k:1536 * k + ROWS], ACT.Relu).then_inc(S["g_ev"], 1)
                        act.wait_ge(S["g_ev"], n + 3)
                        run(RL[k], RL[k], ACT.Square).then_inc(S["act_done"], 1)
                        act.wait_ge(S["act_done"], chain.next())
                        run(UH[:, bass.ds(n, 1), :].rearrange("p o n -> p (o n)"), RL[k], ACT.Copy).then_inc(S["u_hi"], 1)

                    split_weights(0, KD, 0, 0)
                    split_weights(1, KD, 1, 0)
                    with act.Fori(0, 7) as i:
                        chain.restart()
                        for k in range(2):
                            up(2 * i + k, k)
                            split_weights(k, KD, 2 * i + k + 2, i + 1)
                    chain.restart()
                    for k in range(2):
                        up(14 + k, k)
                        split_weights(k, 16, 16 + k, 8)
                    with act.Fori(0, 3) as i:
                        for k in range(2):
                            split_weights(k, 16, 18 + 2 * i + k, i + 9)
                    arrive(act, "act")

            def row_out(t, k, m):
                r = rows_of(t)
                act.wait_ge(S["row_T"], t + 1)
                if not (isinstance(t, int) and t < 2):
                    act.wait_ge(S[f"row_out{k}"], 16 * m)
                run(XS[k][0:r, 0:512], PS[0:r, 1024 * k:1024 * k + 512], ACT.Copy)
                run(XS[k][0:r, 512:1024], PS[0:r, 1024 * k + 512:1024 * k + 1024], ACT.Copy).then_inc(S["row_ev"], 1)

            over_tiles(act, row_out)

        @block.vector
        def _(dve):
            V = nc.vector

            def rows_of(t):
                return NS if isinstance(t, int) and t == QT else P

            def cols(t):
                return bass.ds(t * P, rows_of(t)) if not isinstance(t, int) else slice(t * P, t * P + rows_of(t))

            dve.wait_ge(loaded_once, 48)
            V.tensor_copy(identb, ident)
            V.tensor_copy(cnegb, C("cneg"))
            V.tensor_copy(wnegb, C("wneg"))
            arrive(dve, "dve")

            def rstd(out, sums, count, which, n):
                V.tensor_scalar(out, sums, 1.0 / count, EPS, ALU.mult, ALU.add).then_inc(S[f"{which}_mean"], 1)
                dve.wait_ge(S[f"{which}_rstd"], n)
                if which == "col":
                    V.reciprocal(out, out).then_inc(S["col_inv"], 1)
                    dve.wait_ge(S["col_inv"], n)

            def normed(dst, gain, rst):
                dve.wait_ge(S["sq_summed"], KD)
                rstd(rst, PS[:, 0:ROWS], DM, "col", 1)
                for k in range(KD):
                    V.scalar_tensor_tensor(dst[:, k, :], XT[:, k, :], gain[:, k:k + 1], rst, ALU.mult, ALU.mult)\
                        .then_inc(S["xn_ready"], 1)

            def low_weights(k, blocks, n):
                dve.wait_ge(S["w_hi"], n + 1)
                V.tensor_tensor(WL[k][:, 0:blocks, :], WF[k][:, 0:blocks, :], WH[k][:, 0:blocks, :], ALU.subtract)\
                    .then_inc(S["w_lo"], 1)

            with dve.Fori(0, layers) as l:
                chain = Chain(dve, S["dve_done"])
                dve.wait_ge(S["gains"], 400)
                normed(XNT, G1, RST)
                V.memset(GL[:, :, 0:CW - 1], 0.0).then_inc(S["dve_done"], 1)
                dve.wait_ge(S["dve_done"], chain.next())
                for f in range(2):
                    dve.wait_ge(S["glu_sig"], f + 1)
                    V.tensor_tensor(GL[:, f, CW - 1:], PS[:, 0:SEQ], SG[:, 0:SEQ], ALU.mult)
                    V.tensor_tensor(GLS[:, f, :, CW - 1:], PS[:, SEQ:ROWS].rearrange("p (b t) -> p b t", b=NB),
                                    SG[:, SEQ:ROWS].rearrange("p (b t) -> p b t", b=NB), ALU.mult)
                    V.tensor_tensor(SGL[:, f, :], PS[:, SEQ:ROWS], SG[:, SEQ:ROWS], ALU.mult).then_inc(S["glu_done"], 1)
                dve.wait_ge(S["wm_in"], 1040)
                V.tensor_tensor(WMr, WMr, C("tril").unsqueeze(1).to_broadcast([P, 4, P]), ALU.mult).then_inc(S["wm_raw"], 1)
                V.tensor_tensor(WM8r[0:NS], WM8r[0:NS], C("btril", NS).unsqueeze(1).to_broadcast([NS, 4, NS]),
                                ALU.mult).then_inc(S["wm_raw"], 1)
                dve.wait_ge(S["glu_mm"], 2)
                dve.wait_ge(S["wm_T"], 2)
                for x in ZA:
                    V.memset(x[:, 0:NH, HD + 1:HD + 2], 1.0)
                    V.memset(x[:, NH:2 * NH, HD:HD + 1], 1.0)
                V.memset(GN10[:, 5:10:2, :], 1.0)
                V.memset(CARRY, 0.0)
                V.tensor_scalar(GQK[:, 0, :], GQK[:, 0, :], HD ** -0.5, None, ALU.mult)
                V.tensor_scalar(GN10[:, 0:NH, :], GN10[:, 0:NH, :], HD ** -0.5, None, ALU.mult).then_inc(S["dve_done"], 1)
                dve.wait_ge(S["dve_done"], chain.next())

                def norm_rows(t, k, m):
                    r = rows_of(t)
                    bf = lambda x, shape: x.to_broadcast(shape)
                    dve.wait_ge(S["z_ev"], 8 * t + 3)
                    if not (isinstance(t, int) and t < 2):
                        dve.wait_ge(S[f"st{k}"], 176 * m)
                    x, na, lf = EX[0:r, 36:40], EX[0:r, 32:36], LF[k][0:r, :]
                    V.tensor_tensor(x, VB[k][0:r, 256:260], BFB[0:r, :], ALU.add).then_inc(S["dve_done"], 1)
                    dve.wait_ge(S["dve_done"], chain.next())
                    V.tensor_scalar(na, x, -1.0, None, ALU.mult).then_inc(S["dve_done"], 1)
                    dve.wait_ge(S["dve_done"], chain.next())
                    V.tensor_tensor(na, x, na, ALU.min).then_inc(S["na_ready"], 1)
                    V.tensor_scalar(x, x, 0.0, None, ALU.min).then_inc(S["dve_done"], 1)
                    dve.wait_ge(S["dve_done"], chain.next())
                    dve.wait_ge(S["z_ev"], 8 * t + 7)
                    V.reduce_sum(SS18[0:r, 0:18], SQ[0:r, :].rearrange("p (g d) -> p g d", d=HD), AX)
                    dve.wait_ge(S["z_ev"], 8 * t + 8)
                    vd, vn = UV[k][0:r, GW:2 * GW], VN[k][0:r, :]
                    V.bn_stats(BN6[0:r, :], vd).then_inc(S["dve_done"], 1)
                    dve.wait_ge(S["dve_done"], chain.next())
                    V.bn_aggr(BN2[0:r, :], BN6[0:r, :]).then_inc(S["dve_done"], 1)
                    dve.wait_ge(S["dve_done"], chain.next())
                    V.tensor_scalar(SS18[0:r, 18:19], BN2[0:r, 1:2], float(HD), None, ALU.mult).then_inc(S["dve_done"], 1)
                    dve.wait_ge(S["dve_done"], chain.next())
                    rstd(SS18[0:r, :], SS18[0:r, :], HD, "row", t + 1)
                    za = ZA[k][0:r, :, 0:HD]
                    V.tensor_tensor(za, Z[0:r, 0:512].rearrange("p (g d) -> p g d", d=HD),
                                    bf(SS18[0:r, 0:8].unsqueeze(2), [r, 8, HD]), ALU.mult).then_inc(S["dve_done"], 1)
                    dve.wait_ge(S["dve_done"], chain.next())
                    t10 = T10[0:r, :].rearrange("p (g d) -> p g d", d=HD)
                    z10 = Z[0:r, 512:1152].rearrange("p (g d) -> p g d", d=HD)
                    for s in range(2):
                        zs = ZA[k][0:r, 4 * s:4 * s + 4, 0:HD]
                        V.tensor_tensor(zs, zs, bf(GQK[0:r, s, :].unsqueeze(1), [r, NH, HD]), ALU.mult)
                    V.tensor_tensor(t10, z10, bf(SS18[0:r, 8:18].unsqueeze(2), [r, 10, HD]), ALU.mult).then_inc(S["dve_done"], 1)
                    dve.wait_ge(S["dve_done"], chain.next())
                    V.tensor_tensor(t10, t10, GN10[0:r], ALU.mult).then_inc(S["dve_done"], 1)
                    dve.wait_ge(S["dve_done"], chain.next())
                    tab = lambda name: C(name, r)[:, (t if isinstance(t, int) else t) * 32:((t if isinstance(t, int) else t) + 1) * 32] \
                        if isinstance(t, int) else C(name, r)[:, bass.ds(t * 32, 32)]
                    v4 = T10[0:r, :].rearrange("p (g s d) -> p g s d", s=2, d=32)
                    sn4 = SN[0:r, :].rearrange("p (g s d) -> p g s d", s=2, d=32)
                    ca4 = SQ[0:r, 0:640].rearrange("p (g s d) -> p g s d", s=2, d=32)
                    rn4 = RN[k][0:r].rearrange("p g (s d) -> p g s d", s=2)
                    cos, sin = (bf(tab(n).unsqueeze(1), [r, 10, 32]) for n in ("cos", "sin"))
                    for s in range(2):
                        V.tensor_tensor(ca4[:, :, s, :], v4[:, :, s, :], cos, ALU.mult)
                        V.tensor_tensor(sn4[:, :, s, :], v4[:, :, 1 - s, :], sin, ALU.mult).then_inc(S["dve_done"], 1)
                        dve.wait_ge(S["dve_done"], chain.next())
                    V.tensor_tensor(rn4[:, :, 0, :], ca4[:, :, 0, :], sn4[:, :, 0, :], ALU.subtract)
                    V.tensor_tensor(rn4[:, :, 1, :], ca4[:, :, 1, :], sn4[:, :, 1, :], ALU.add).then_inc(S["dve_done"], 1)
                    dve.wait_ge(S["dve_done"], chain.next())
                    V.tensor_copy(RN[k][0:r, 5:10:2, :], z10[:, 5:10:2, :]).then_inc(S["dve_done"], 1)
                    dve.wait_ge(S["dve_done"], chain.next())
                    dve.wait_ge(S["ex_ready"], 2 * t + 1)
                    V.tensor_scalar(EX[0:r, 0:12], EX[0:r, 0:12], 1.0, None, ALU.add).then_inc(S["dve_done"], 1)
                    dve.wait_ge(S["dve_done"], chain.next())
                    V.reciprocal(G12[k][0:r, :], EX[0:r, 0:12]).then_inc(S["dve_done"], 1)
                    dve.wait_ge(S["dve_done"], chain.next())
                    dve.wait_ge(S["ex_ready"], 2 * t + 2)
                    e, s1, s2, q = EX[0:r, 16:20], EX[0:r, 40:44], EX[0:r, 44:48], EX[0:r, 48:52]
                    V.tensor_scalar(s1, e, 2.0, None, ALU.add).then_inc(S["dve_done"], 1)
                    dve.wait_ge(S["dve_done"], chain.next())
                    V.reciprocal(s1, s1).then_inc(S["dve_done"], 1)
                    dve.wait_ge(S["dve_done"], chain.next())
                    V.tensor_tensor(s1, s1, e, ALU.mult).then_inc(S["dve_done"], 1)
                    dve.wait_ge(S["dve_done"], chain.next())
                    V.tensor_tensor(s2, s1, s1, ALU.mult).then_inc(S["dve_done"], 1)
                    dve.wait_ge(S["dve_done"], chain.next())
                    V.tensor_scalar(q, s2, 1.0 / 15, None, ALU.mult).then_inc(S["dve_done"], 1)
                    dve.wait_ge(S["dve_done"], chain.next())
                    for n in (13, 11, 9, 7, 5, 3):
                        V.scalar_tensor_tensor(q, q, 1.0 / n, s2, ALU.add, ALU.mult).then_inc(S["dve_done"], 1)
                        dve.wait_ge(S["dve_done"], chain.next())
                    V.scalar_tensor_tensor(q, q, 1.0, s1, ALU.add, ALU.mult).then_inc(S["dve_done"], 1)
                    dve.wait_ge(S["dve_done"], chain.next())
                    V.scalar_tensor_tensor(lf, q, -2.0, x, ALU.mult, ALU.add).then_inc(S["dve_done"], 1)
                    dve.wait_ge(S["dve_done"], chain.next())
                    dve.sem_inc(S["z_free"], 1)
                    V.tensor_scalar(vn, vd, BN2[0:r, 0:1], SS18[0:r, 18:19], ALU.subtract, ALU.mult).then_inc(S["dve_done"], 1)
                    dve.wait_ge(S["dve_done"], chain.next())
                    V.tensor_tensor(vn, vn, LNG[0:r, 0, :], ALU.mult).then_inc(S["dve_done"], 1)
                    dve.wait_ge(S["dve_done"], chain.next())
                    V.tensor_tensor(vn, vn, LNG[0:r, 1, :], ALU.add).then_inc(S["lf_ready"], 1)

                def finish(t, k):
                    r = rows_of(t)
                    dve.wait_ge(S["small_mm"], t + 1)
                    fq, fk = ZA[k][0:r, 0:NH, HD], ZA[k][0:r, NH:2 * NH, HD + 1]
                    sums = PS[0:r, 2560:2564]
                    if r == P:
                        V.tensor_tensor(fq, sums, CARRY, ALU.add).then_inc(S["dve_done"], 1)
                        dve.wait_ge(S["dve_done"], chain.next())
                        V.tensor_tensor(CARRY, PS[0:r, 2564:2568], CARRY, ALU.add)
                    else:
                        V.tensor_copy(fq, sums).then_inc(S["dve_done"], 1)
                        dve.wait_ge(S["dve_done"], chain.next())
                    V.tensor_scalar(fk, fq, -1.0, None, ALU.mult)
                    od = OD[k][0:r, :]
                    bs = BS if r == P else BS8
                    V.tensor_tensor(od.rearrange("p (g d) -> p g d", d=HD),
                                    PS[0:r, 3072:3072 + GW].rearrange("p (g d) -> p g d", d=HD),
                                    bs[0:r, :].unsqueeze(2).to_broadcast([r, 4, HD]), ALU.add).then_inc(S["dve_done"], 1)
                    dve.wait_ge(S["dve_done"], chain.next())
                    V.tensor_tensor(od, od, UV[k][0:r, 0:GW], ALU.mult).then_inc(S["fin"], 1)

                def z_step(t, k, m):
                    norm_rows(t, k, m)
                    if not (isinstance(t, int) and t == 0):
                        finish(t - 1, 1 - k)

                over_tiles(dve, z_step, chain)
                finish(8, 0)
                chain.restart()
                dve.wait_ge(S["ct_ev"], 1)
                dve.wait_ge(S["z_mm"], 45)
                for c in range(2):
                    V.memset(Yc[:, c, :], 0.0)
                dve.wait_ge(S["fin"], 9)
                dve.drain()
                for c in range(2):
                    last = V.tensor_scalar(Yc[:, c, :], Yc[:, c, :], CB[:, c:c + 1], None, ALU.add)
                last.then_inc(S["dve_done"], 1)
                dve.wait_ge(S["dve_done"], chain.next())
                with dve.Fori(0, CW) as j:
                    chain.restart()
                    tap = bass.ds(j, 1)
                    for c in range(2):
                        for y, x in ((Yc[:, c, 0:SEQ], GL[:, c, bass.ds(j, SEQ)]),
                                     (Yc[:, c, SEQ:].rearrange("p (b t) -> p b t", b=NB), GLS[:, c, :, bass.ds(j, NT)])):
                            last = V.scalar_tensor_tensor(y, x, CWT[:, c, tap], y, ALU.mult, ALU.add)
                    last.then_inc(S["dve_done"], 1)
                    dve.wait_ge(S["dve_done"], chain.next())
                dve.sem_inc(S["y_done"], 1)
                arrive(dve, "dve")
                if stop <= 2:
                    return

                chain.restart()
                V.memset(PHI, 0.0).then_inc(S["zero_ready"], 1)
                dve.sem_inc(S["pg_evD"], 1)
                dve.wait_ge(S["kvc_mm"], 2)
                V.tensor_copy(CT[:, NB * PAST + 512:NB * PAST + 1024], bank(5)).then_inc(S["pg_evD"], 1)
                with dve.Fori(0, NB) as i:
                    for k in (1, 3):
                        dve.wait_ge(S["pg_T"], 4 * i + k + 5)
                        V.tensor_copy(CT[:, bass.ds((4 * i + k) * 512, 512)], bank(k)).then_inc(S["pg_evD"], 1)
                dve.wait_ge(S["lfp_ready"], 1)
                for h in range(NH):
                    last = V.tensor_tensor_scan(PFX[:, h, :], ones, LFP[:, :, h], 0.0, ALU.mult, ALU.add)
                last.then_inc(S["dve_done"], 1)
                dve.wait_ge(S["dve_done"], chain.next())
                V.tensor_copy(TOT, PFX[:, :, PAGE - 1]).then_inc(S["tot_ready"], 1)
                dve.wait_ge(S["lat_mm"], 1)
                V.tensor_tensor(LAT, bank(7, 4), TOT, ALU.add).then_inc(S["dve_done"], 1)
                dve.wait_ge(S["dve_done"], chain.next())
                for h in range(NH):
                    last = V.tensor_scalar(PFX[:, h, :], PFX[:, h, :], -1.0, LAT[:, h:h + 1], ALU.mult, ALU.add)
                last.then_inc(S["suf_ready"], 1)
                dve.wait_ge(S["kvc_mm"], 3)
                V.tensor_copy(TOT[:, 0:1], bank(1)[:, 272:273]).then_inc(S["dve_done"], 1)
                dve.wait_ge(S["dve_done"], chain.next())
                V.tensor_scalar(KVC[:, 0:272], bank(0, 272), TOT[:, 0:1], None, ALU.add)
                V.tensor_scalar(KVC[:, 272:544], bank(1, 272), TOT[:, 0:1], None, ALU.add).then_inc(S["kvc_ready"], 1)
                arrive(dve, "dve")
                if stop <= 3:
                    return

                chain.restart()
                V.tensor_copy(VREP[HD:P],
                              KVC[HD:P, 512:544].unsqueeze(1).to_broadcast([HD, 4, NPB])).then_inc(S["vb_ready"], 1)
                V.memset(VBD, 0.0).then_inc(S["dve_done"], 1)
                dve.wait_ge(S["dve_done"], chain.next())
                dve.wait_ge(S["vb_ready"], 2)
                for i in range(4):
                    V.tensor_copy(VBD[i * NPB:(i + 1) * NPB, i, :], bank(7)[i * NPB:(i + 1) * NPB, 0:HD])
                arrive(dve, "dve")

                units = [(kind, i) for kind in ("sel", "fox", "win") for i in range(QT)]

                def blocks_of(u):
                    kind, i = units[u]
                    return min(i, WIN // P) + 1 if kind == "win" else i + 1

                with dve.Fori(0, NH) as h:
                    chain.restart()
                    dve.wait_ge(S["cs_mm"], 1)
                    scf = SC.rearrange("p t n -> p (t n)")
                    V.tensor_tensor(scf, bank(7, 256), C("cmpneg"), ALU.add).then_inc(S["dve_done"], 1)
                    dve.wait_ge(S["dve_done"], chain.next())
                    V.reduce_max(SC8, SC, AX).then_inc(S["dve_done"], 1)
                    dve.wait_ge(S["dve_done"], chain.next())
                    V.tensor_tensor(SC, SC, SC8.unsqueeze(2).to_broadcast([P, QT, NPB]), ALU.subtract).then_inc(S["cs_ready"], 1)

                    def row_max(u):
                        dve.wait_ge(S["s_mm"], u + 1)
                        V.reduce_max(NMX[:, u:u + 1], PS[:, (u % 2) * 1024:(u % 2) * 1024 + blocks_of(u) * P], AX,
                                     negate=True).then_inc(S["nm_ready"], 1)

                    row_max(0)
                    row_max(1)
                    dve.wait_ge(S["ce_ready"], 1)
                    V.tensor_tensor(scf, scf, C("cmp01"), ALU.mult).then_inc(S["dve_done"], 1)
                    dve.wait_ge(S["dve_done"], chain.next())
                    V.reduce_sum(SC8, SC, AX).then_inc(S["dve_done"], 1)
                    dve.wait_ge(S["dve_done"], chain.next())
                    V.tensor_scalar(SC8, SC8, 1e-30, None, ALU.max).then_inc(S["dve_done"], 1)
                    dve.wait_ge(S["dve_done"], chain.next())
                    V.reciprocal(SC8, SC8).then_inc(S["dve_done"], 1)
                    dve.wait_ge(S["dve_done"], chain.next())
                    V.tensor_tensor(SC, SC, SC8.unsqueeze(2).to_broadcast([P, QT, NPB]), ALU.mult).then_inc(S["cp_ready"], 1)

                    dve.wait_ge(S["cpv_mm"], 1)
                    V.tensor_tensor(ON, bank(7).rearrange("p (t d) -> p t d", d=HD),
                                    GH[:, :, 0].unsqueeze(2).to_broadcast([P, QT, HD]), ALU.mult).then_inc(S["on_ready"], 1)
                    dve.wait_ge(S["on_ready"], 1)

                    def output(u):
                        kind, i = units[u]
                        dve.wait_ge(S["pv_mm"], u + 1)
                        ri = RI[:, u:u + 1]
                        V.tensor_scalar(ri, RS[:, u:u + 1], 1e-30, None, ALU.max).then_inc(S["dve_done"], 1)
                        dve.wait_ge(S["dve_done"], chain.next())
                        V.reciprocal(ri, ri).then_inc(S["dve_done"], 1)
                        dve.wait_ge(S["dve_done"], chain.next())
                        o = bank(6 + u % 2, HD)
                        if kind == "fox":
                            V.tensor_scalar(OF[:, i, :], o, ri, None, ALU.mult).then_inc(S["o_done"], 1)
                        else:
                            V.tensor_tensor(ri, ri, GH[:, i, 1 if kind == "sel" else 2].unsqueeze(1), ALU.mult).then_inc(S["dve_done"], 1)
                            dve.wait_ge(S["dve_done"], chain.next())
                            V.scalar_tensor_tensor(ON[:, i, :], o, ri, ON[:, i, :], ALU.mult, ALU.add).then_inc(S["o_done"], 1)

                    groups = 0
                    for u in range(len(units)):
                        n = blocks_of(u)
                        if u >= 2:
                            dve.wait_ge(S["pv_mm"], u - 1)
                        for a in range(0, n, 4):
                            w4 = min(4, n - a) * P
                            dve.wait_ge(S["pt_T"], groups + 1)
                            V.tensor_copy(PTR[u % 2][:, a * P:a * P + w4], bank(4 + groups % 2, w4)).then_inc(S["pt_ev"], 1)
                            groups += 1
                        if u + 2 < len(units):
                            row_max(u + 2)
                        if u >= 1:
                            output(u - 1)
                    output(len(units) - 1)
                    dve.wait_ge(S["o_done"], len(units))
                    dve.sem_inc(S["o_ready"], 1)
                    arrive(dve, "dve")
                if stop <= 4:
                    return

                chain.restart()
                V.memset(QALL, 0.0)
                V.memset(WMASK[0:32, :], 0.0).then_inc(S["dve_done"], 1)
                dve.wait_ge(S["dve_done"], chain.next())
                V.tensor_copy(WMASK[0:32, 0:NT], C("winneg", 32))
                V.tensor_copy(WMASK[0:32, WIN:], C("newneg", 32))
                dve.wait_ge(S["q_T"], 1)
                for h in range(NH):
                    r = slice((h % 2) * HD, (h % 2 + 1) * HD)
                    V.tensor_copy(QALL[r, h // 2, :, h * NT:(h + 1) * NT],
                                  bank(0)[r, (h // 2) * NS:(h // 2 + 1) * NS].rearrange("p (b t) -> p b t", b=NB))
                    last = V.tensor_copy(QNALL[0:HD, :, h * NT:(h + 1) * NT],
                                         bank(1)[0:HD, h * NS:(h + 1) * NS].rearrange("p (b t) -> p b t", b=NB))
                last.then_inc(S["q_ev"], 1)
                dve.wait_ge(S["sc_mm"], 1)
                s4 = bank(4, 2 * NCB).rearrange("p (g n) -> p g n", g=2)
                V.reduce_max(PC4[:, 0:2], s4, AX).then_inc(S["dve_done"], 1)
                dve.wait_ge(S["dve_done"], chain.next())
                V.tensor_tensor(PC, s4, PC4[:, 0:2].unsqueeze(2).to_broadcast([P, 2, NCB]), ALU.subtract).then_inc(S["mx_ready"], 1)
                dve.wait_ge(S["e_ready"], 1)
                V.reduce_sum(PC4[:, 2:4], PC, AX).then_inc(S["dve_done"], 1)
                dve.wait_ge(S["dve_done"], chain.next())
                V.tensor_scalar(PC4[:, 2:4], PC4[:, 2:4], 1e-30, None, ALU.max).then_inc(S["dve_done"], 1)
                dve.wait_ge(S["dve_done"], chain.next())
                V.reciprocal(PC4[:, 2:4], PC4[:, 2:4]).then_inc(S["dve_done"], 1)
                dve.wait_ge(S["dve_done"], chain.next())
                V.tensor_tensor(PC, PC, PC4[:, 2:4].unsqueeze(2).to_broadcast([P, 2, NCB]), ALU.mult).then_inc(S["sm_ready"], 1)
                dve.wait_ge(S["imp_mm"], 1)
                imp = IMP[0:NS, :]
                V.reduce_sum(imp[:, 0:NSB - 1], bank(5)[0:NS, 0:NCB].rearrange("p (j s) -> p j s", s=2), AX).then_inc(S["dve_done"], 1)
                dve.wait_ge(S["dve_done"], chain.next())
                V.memset(imp[:, 0:1], 1e4)
                V.memset(imp[:, NSB - 2:NSB], 1e4).then_inc(S["dve_done"], 1)
                dve.wait_ge(S["dve_done"], chain.next())
                full = [NS, NSB, NSB]
                V.tensor_tensor(GT[0:NS], imp.unsqueeze(1).to_broadcast(full), imp.unsqueeze(2).to_broadcast(full), ALU.is_gt)
                V.tensor_tensor(EQ[0:NS], imp.unsqueeze(1).to_broadcast(full), imp.unsqueeze(2).to_broadcast(full),
                                ALU.is_equal).then_inc(S["dve_done"], 1)
                dve.wait_ge(S["dve_done"], chain.next())
                V.tensor_tensor(EQ[0:NS], EQ[0:NS], C("before", NS).rearrange("p (j i) -> p j i", j=NSB), ALU.mult).then_inc(S["dve_done"], 1)
                dve.wait_ge(S["dve_done"], chain.next())
                V.tensor_tensor(GT[0:NS], GT[0:NS], EQ[0:NS], ALU.add).then_inc(S["dve_done"], 1)
                dve.wait_ge(S["dve_done"], chain.next())
                V.reduce_sum(RK[0:NS, :], GT[0:NS], AX).then_inc(S["dve_done"], 1)
                dve.wait_ge(S["dve_done"], chain.next())
                V.tensor_scalar(RK[0:NS, :], RK[0:NS, :], NSEL - 0.5, NEG, ALU.is_gt, ALU.mult).then_inc(S["rank_ready"], 1)
                dve.wait_ge(S["imp_mm"], 2)
                V.tensor_copy(OCS, bank(7, 2 * HD).rearrange("p (g d) -> p g d", g=2)).then_inc(S["os_ready"], 1)
                arrive(dve, "dve")
                if stop <= 5:
                    return

                dve.sem_inc(S["bias_free"], 1)
                with dve.Fori(0, NB // 2) as i:
                    chain.restart()
                    for k in range(2):
                        b = 2 * i + k
                        bb = bass.ds(b, 1)
                        def keys_out(what):
                            first = 13 * k + {"fox": 0, "sel": 8, "win": 12}[what]
                            n = {"fox": 8, "sel": 4, "win": 1}[what]
                            for g in range(first, first + n):
                                if g % 2 == 0:
                                    continue
                                j = g - first
                                dve.wait_ge(S["kt_T"], g + 1)
                                if what == "fox":
                                    dst, r = KT2[:, j // 4, (j % 4) * 512:(j % 4 + 1) * 512], P
                                elif what == "sel":
                                    dst, r = KSTs[0:HD, j * 512:(j + 1) * 512], HD
                                else:
                                    dst, r = KWTs[0:HD, 0:512], HD
                                V.tensor_copy(dst, bank(g % 2)[0:r, :]).then_inc(S["kt_evD"], 1)

                        def scores_out(n, dst, keys, mask):
                            c0 = chunk_of[n]
                            parts = list(range(0, keys, 512))
                            if k:
                                dve.wait_ge(S["ptn_T"], n + 1)
                            for m, a in enumerate(parts):
                                wd = min(512, keys - a)
                                dve.wait_ge(S["sc_mm"], c0 + m + 1)
                                out, src = dst[0:32, a:a + wd], bank(2 + (c0 + m) % 2)[0:32, 0:wd]
                                in1 = mask(a, wd)
                                if len(in1.shape) == 3:
                                    out = out.rearrange("p (j n) -> p j n", n=SEL)
                                    src = src.rearrange("p (j n) -> p j n", n=SEL)
                                V.tensor_tensor_reduce(out=out, in0=src, in1=in1, scale=1.0, scalar=-3e38, op0=ALU.add,
                                                       op1=ALU.max, accum_out=MX8[0:32, m:m + 1]).then_inc(S["sc_ev"], 1)
                            dve.wait_ge(S["sc_ev"], c0 + len(parts))
                            if k:
                                dve.wait_ge(S["e_ready"], n + 1)
                            V.reduce_max(ST[0:32, n:n + 1], MX8[0:32, 0:len(parts)], AX, negate=True).then_inc(S["mx_ready"], 1)
                            dve.wait_ge(S["mx_ready"], 3 * k + n + 1)

                        chunk_of = [12 * k, 12 * k + 5, 12 * k + 10]

                        def block_mask(a, wd):
                            if a == PAST:
                                return C("newneg", 32)
                            return SNB1[k][0:32, a // SEL:a // SEL + 8].unsqueeze(2)\
                                .to_broadcast([32, 8, SEL])

                        keys_out("fox")
                        dve.wait_ge(S["new_T"], k + 1)
                        V.tensor_copy(KT2[:, :, PAST:LK], bank(7, 2 * NT).rearrange("p (a n) -> p a n", a=2))
                        V.tensor_copy(KSTs[0:HD, PAST:LK], bank(7)[0:HD, 16:24])
                        V.tensor_copy(KWTs[0:HD, WIN:], bank(7)[0:HD, 24:32]).then_inc(S["new_ev"], 1)
                        dve.wait_ge(S["bias_ready"], k + 1)
                        scores_out(0, SF, LK, lambda a, wd: BIAS[0:32, a:a + wd])
                        dve.sem_inc(S["bias_free"], 1)
                        keys_out("sel")
                        scores_out(1, SSL, LK, block_mask)
                        keys_out("win")
                        scores_out(2, SW, WIN + NT, lambda a, wd: WMASK[0:32, a:a + wd])
                        ri = ST[0:32, 6:7]

                        def inverse_sum(n):
                            V.tensor_scalar(ri, ST[0:32, 3 + n:4 + n], 1e-30, None, ALU.max).then_inc(S["dve_done"], 1)
                            dve.wait_ge(S["dve_done"], chain.next())
                            V.reciprocal(ri, ri).then_inc(S["dve_done"], 1)
                            dve.wait_ge(S["dve_done"], chain.next())

                        dve.wait_ge(S["ov_mm"], 3 * k + 1)
                        inverse_sum(0)
                        oo = OO[0:32, :].rearrange("p (h d) -> p h d", h=NH)
                        V.tensor_tensor(oo, bank(5)[0:32, 0:GW].rearrange("p (h d) -> p h d", h=NH),
                                        C("hmask", 32).unsqueeze(2).to_broadcast([32, NH, HD]), ALU.mult).then_inc(S["ov_done"], 1)
                        dve.wait_ge(S["ov_done"], 3 * k + 1)
                        V.reduce_sum(OH[k][0:32, :], oo.rearrange("p h d -> p d h"), AX).then_inc(S["dve_done"], 1)
                        dve.wait_ge(S["dve_done"], chain.next())
                        V.tensor_scalar(OH[k][0:32, :], OH[k][0:32, :], ri, None, ALU.mult).then_inc(S["os_ready"], 1)
                        dve.wait_ge(S["os_ready"], 2 * k + 1)
                        oc = OCM[k][0:32, :]
                        gate = lambda c: GB[0:32, bb, c:c + 1].rearrange("p o c -> p (o c)")
                        V.tensor_scalar(oc, OCB[0:32, bb, :].rearrange("p o d -> p (o d)"), gate(0), None, ALU.mult).then_inc(S["dve_done"], 1)
                        dve.wait_ge(S["dve_done"], chain.next())
                        for n in (1, 2):
                            dve.wait_ge(S["ov_mm"], 3 * k + n + 1)
                            inverse_sum(n)
                            V.tensor_tensor(ri, ri, gate(n), ALU.mult).then_inc(S["dve_done"], 1)
                            dve.wait_ge(S["dve_done"], chain.next())
                            o = bank(5)[0:32, GW + (n - 1) * HD:GW + n * HD]
                            V.scalar_tensor_tensor(oc, o, ri, oc, ALU.mult, ALU.add).then_inc(S["ov_done"], 1)
                            dve.wait_ge(S["ov_done"], 3 * k + n + 1)
                        dve.sem_inc(S["os_ready"], 1)
                    arrive2(dve, "dve")
                arrive(dve, "dve")
                if stop <= 6:
                    return

                chain.restart()
                both = [P, 2, ROWS]
                dve.wait_ge(S["y_in"], 112)
                dve.wait_ge(S["y_mm"], 1)
                V.tensor_scalar(YM, PS[:, 0:ROWS], 1.0 / GW, None, ALU.mult).then_inc(S["dve_done"], 1)
                dve.wait_ge(S["dve_done"], chain.next())
                V.tensor_tensor(YB, YB, YM.unsqueeze(1).to_broadcast(both), ALU.subtract).then_inc(S["dve_done"], 1)
                dve.wait_ge(S["dve_done"], chain.next())
                V.tensor_tensor(YQ, YB, YB, ALU.mult).then_inc(S["y_sq"], 1)
                dve.wait_ge(S["y_mm"], 2)
                rstd(YM, PS[:, 0:ROWS], GW, "col", 1)
                V.tensor_tensor(YB, YB, YM.unsqueeze(1).to_broadcast(both), ALU.mult).then_inc(S["dve_done"], 1)
                dve.wait_ge(S["dve_done"], chain.next())
                for c in range(2):
                    last = V.tensor_scalar(YB[:, c, :], YB[:, c, :], CLG[:, c:c + 1], CLB[:, c:c + 1], ALU.mult, ALU.add)
                last.then_inc(S["y_c"], 1)
                dve.wait_ge(S["y_c"], 2)
                V.tensor_tensor(YB, YB, YQ, ALU.mult).then_inc(S["dve_done"], 1)
                dve.wait_ge(S["dve_done"], chain.next())
                V.tensor_tensor(YQ, YB, YB, ALU.mult).then_inc(S["y_sq"], 1)
                dve.wait_ge(S["y_mm"], 3)
                rstd(YM, PS[:, 0:ROWS], GW, "col", 2)
                for c in range(2):
                    last = V.scalar_tensor_tensor(YQ[:, c, :], YB[:, c, :], GCB[:, c:c + 1], YM, ALU.mult, ALU.mult)
                last.then_inc(S["dve_done"], 1)
                dve.wait_ge(S["dve_done"], chain.next())
                V.tensor_copy(OTH[:, 2:4, :], YQ).then_inc(S["dve_done"], 1)
                dve.wait_ge(S["dve_done"], chain.next())
                V.tensor_tensor(OTL[:, 2:4, :], YQ, OTH[:, 2:4, :], ALU.subtract).then_inc(S["dve_done"], 1)
                dve.wait_ge(S["dve_done"], chain.next())

                def group_norm(t, k):
                    r = rows_of(t)
                    dve.wait_ge(S["ss_ready"], t + 1)
                    rstd(S3[k][0:r, :], S3[k][0:r, :], GW, "row", t + 1)
                    V.tensor_tensor(OA[k][0:r], OA[k][0:r], S3[k][0:r, :].unsqueeze(2).to_broadcast([r, 3, GW]), ALU.mult).then_inc(S["dve_done"], 1)
                    dve.wait_ge(S["dve_done"], chain.next())
                    V.tensor_tensor(OA[k][0:r], OA[k][0:r], GNB[0:r], ALU.mult).then_inc(S["oa_ready"], 1)

                group_norm(0, 0)

                def oa(t, k, m):
                    r = rows_of(t)
                    if not (isinstance(t, int) and t == QT):
                        group_norm(t + 1, 1 - k)
                    dve.wait_ge(S["oa_hi"], t + 1)
                    V.tensor_tensor(OTL[:, 0:2, cols(t)], PS[:, (4 + 2 * k) * 512:(4 + 2 * k) * 512 + 256]
                                    .rearrange("p (j n) -> p j n", j=2)[:, :, 0:r], OTH[:, 0:2, cols(t)], ALU.subtract)
                    V.tensor_tensor(OTL[:, 4:8, cols(t)], PS[:, (5 + 2 * k) * 512:(6 + 2 * k) * 512]
                                    .rearrange("p (j n) -> p j n", j=4)[:, :, 0:r], OTH[:, 4:8, cols(t)],
                                    ALU.subtract).then_inc(S["oa_ev"], 1)

                over_tiles(dve, oa, chain)
                arrive2(dve, "dve")

                def residual(n, k, before):
                    dve.wait_ge(S["g_mm"], before + n + 3)
                    x = XT[:, bass.ds(n, 1), :].rearrange("p o n -> p (o n)")
                    V.tensor_tensor(x, PS[:, 1536 * k:1536 * k + ROWS], x, ALU.add).then_inc(S["g_ev"], 1)

                def residuals(blocks, before):
                    with dve.Fori(0, KD // 2 - 1) as i:
                        for k in range(2):
                            residual(2 * i + k, k, before)
                            low_weights(k, blocks, before + 2 * i + k + 2)
                    for k in range(2):
                        residual(KD - 2 + k, k, before)

                dve.sem_inc(S["w_lo"], 2)
                dve.sem_inc(S["g_ev"], 2)
                for k in range(2):
                    low_weights(k, KD, k)
                residuals(KD, 0)
                arrive(dve, "dve")
                if stop <= 7:
                    return

                arrive(dve, "dve")
                chain.restart()
                normed(XR, G2, RST2)
                for k in range(KD):
                    dve.wait_ge(S["xh_ready"], k + 1)
                    last = V.tensor_tensor(XNL[:, k, :], XR[:, k, :], XNH[:, k, :], ALU.subtract)
                arrive2(dve, "dve")
                with dve.Fori(0, 2) as half:
                    dve.sem_inc(S["w_lo"], 2)
                    dve.sem_inc(S["g_ev"], 2)
                    dve.sem_inc(S["u_ready"], 2)

                    def low_up(n, k):
                        dve.wait_ge(S["u_hi"], n + 1)
                        V.tensor_tensor(UL[:, bass.ds(n, 1), :].rearrange("p o n -> p (o n)"), RL[k],
                                        UH[:, bass.ds(n, 1), :].rearrange("p o n -> p (o n)"),
                                        ALU.subtract).then_inc(S["u_ready"], 1)

                    for k in range(2):
                        low_weights(k, KD, k)
                    with dve.Fori(0, 7) as i:
                        for k in range(2):
                            low_up(2 * i + k, k)
                            low_weights(k, KD, 2 * i + k + 2)
                    for k in range(2):
                        low_up(14 + k, k)
                        low_weights(k, 16, 16 + k)
                    residuals(16, 16)
                    arrive(dve, "dve")

            def row_cp(t, k, m):
                r = rows_of(t)
                if not (isinstance(t, int) and t < 2):
                    dve.wait_ge(S["row_T"], t - 1)
                V.tensor_copy(XO[k][:, :, 0:r], XT[:, :, cols(t)]).then_inc(S["row_cp"], 1)

            over_tiles(dve, row_cp)

        @block.gpsimd
        def _(pool):
            G = nc.gpsimd

            def release(first, last, entry, ways, stored=None):
                pool.drain()
                if stored is not None:
                    pool.wait_ge(S["os_out"], stored)
                    pool.sem_inc(S["os_stored"], 1)
                pool.wait_ge(entry, len(ways))
                pool.sem_clear(range(first, last + 1))
                pool.sem_clear(entry)
                for s in ways.values():
                    pool.sem_inc(s, 1)

            def everyone():
                release(first_sem, last_sem, all_in, go)

            def computers(stored=None):
                release(batch_sem, last_sem, all_in2, go2, stored)

            def power(x, which, n):
                pool.wait_ge(S[f"{which}_mean"], n)
                G.tensor_tensor(x, x, C("mhalf", x.shape[0]).to_broadcast(list(x.shape)), ALU.pow).then_inc(S[f"{which}_rstd"], 1)

            def row_powers(of):
                def step(t, k, m):
                    r = NS if isinstance(t, int) and t == QT else P
                    power(of(k)[0:r, :], "row", t + 1)
                over_tiles(pool, step)

            pool.wait_ge(loaded_once, 48)
            everyone()
            with pool.Fori(0, layers) as l:
                row_powers(lambda k: SS18)
                everyone()
                if stop <= 2:
                    return
                G.indirect_dma_start(LFP.rearrange("p t h -> p (t h)"), None,
                                     A["cache_fox_logf"].rearrange("l n t h -> (l n) (t h)"),
                                     bass.IndirectOffsetOnAxis(page_rows, 0)).then_inc(lfp_in, 16)
                pool.wait_ge(lfp_in, 16 * l + 16)
                pool.sem_inc(S["lfp_ready"], 1)
                G.tensor_scalar(page_rows, page_rows, POOL, None, ALU.add).then_inc(S["page_next"], 1)
                pool.wait_ge(S["page_next"], 1)
                everyone()
                if stop <= 3:
                    return
                everyone()
                with pool.Fori(0, NH) as h:
                    everyone()
                if stop <= 4:
                    return
                everyone()
                if stop <= 5:
                    return
                with pool.Fori(0, NB // 2) as i:
                    for k in range(2):
                        b = 2 * i + k
                        bb = bass.ds(b, 1)
                        if k:
                            pool.wait_ge(S["sc_mm"], 12)
                        G.tensor_copy(QB, QALL[:, :, bb, :].rearrange("p a o n -> p a (o n)"))
                        G.tensor_copy(SNB1[k][0:32, :], SNB[0:32, bb, :].rearrange("p o j -> p (o j)"))
                        G.tensor_copy(QNB[0:HD, :], QNALL[0:HD, bb, :].rearrange("p o n -> p (o n)")).then_inc(S["qb_ready"], 1)
                        pool.wait_ge(S["bias_in"], 64 * b + 64)
                        G.tensor_tensor(BIAS[0:32, :], BIAS[0:32, :], FQ[0:32, bb].to_broadcast([32, LK]), ALU.add)\
                            .then_inc(S["pool_done2"], 1)
                        pool.wait_ge(S["pool_done2"], k + 1)
                        G.tensor_tensor(BIAS[0:32, PAST:], BIAS[0:32, PAST:], C("newneg", 32), ALU.add)\
                            .then_inc(S["bias_ready"], 1)
                    computers(64 * i + 64)
                everyone()
                if stop <= 6:
                    return
                row_powers(lambda k: S3[k])
                computers()
                everyone()
                if stop <= 7:
                    return
                everyone()
                computers()
                with pool.Fori(0, 2) as half:
                    everyone()


_OUTS = [
    ("y_prompt", (1, SEQ, DM)), ("y_sample", (NB, NT, DM)),
    ("fox_kv_p", (DEPTH, 1, SEQ, 2, NH, HD)), ("fox_kv_s", (DEPTH, NB, NT, 2, NH, HD)),
    ("fox_logf_p", (DEPTH, 1, SEQ, NH)), ("fox_logf_s", (DEPTH, NB, NT, NH)),
    ("nsa_kv_p", (DEPTH, 1, SEQ, 4, HD)), ("nsa_kv_s", (DEPTH, NB, NT, 4, HD)),
    ("nsa_win_p", (DEPTH, 1, WIN, 2, HD)), ("nsa_win_s", (DEPTH, NB, WIN, 2, HD)),
    ("conv_p", (DEPTH, 1, CW - 1, GW)), ("conv_s", (DEPTH, NB, CW - 1, GW)),
    ("gmlp_v_s", (DEPTH, NB, NT, GW)),
]


def program(nc, arrays, layers=DEPTH, stop=99):
    ins = {n: nc.dram_tensor(f"in_{n}", a.shape, mybir.dt.from_np(a.dtype), kind="ExternalInput").ap()
           for n, a in arrays.items()}
    outs = {n: nc.dram_tensor(f"out_{n}", shape, F32, kind="ExternalOutput").ap() for n, shape in _OUTS}
    build_step(nc, ins, outs, layers, stop)


def kernel(**inputs):
    import concourse.bacc as _bacc
    from concourse.bass_utils import run_bass_kernel_spmd as _run

    nc = _bacc.Bacc("TRN2", target_bir_lowering=False, num_devices=1)
    arrays = {n: np.ascontiguousarray(a) for n, a in inputs.items()}
    arrays["consts"] = shape_constants()[1]
    program(nc, arrays)
    r = _run(nc, [{f"in_{n}": a for n, a in arrays.items()}], core_ids=[0])
    return tuple(r.results[0][f"out_{n}"] for n, _ in _OUTS)
```

```python
from contextlib import ExitStack

import numpy as np

import concourse.bass as bass
from concourse import mybir

F32 = mybir.dt.float32
BF16 = mybir.dt.bfloat16
I32 = mybir.dt.int32
ALU = mybir.AluOpType
ACT = mybir.ActivationFunctionType
AX = mybir.AxisListType.X

DM = 1024
SEQ = 1024
NB = 8
NT = 8
DEPTH = 2
PAST = 2048
PAGE = 128
HD = 64
NH = 4
GW = NH * HD
CW = 31
BLK = 32
SEL = 64
NSEL = 16
WIN = 512
DFF = 4 * DM
EPS = 1e-6
NEG = -1e30

P = 128
NS = NB * NT
ROWS = SEQ + NS
QT = SEQ // P
KD = DM // P
NPG = PAST // PAGE
POOL = NB * NPG * 5 // 4
NCB = PAST // BLK
NSB = PAST // SEL + 1
NPB = SEQ // BLK
LK = PAST + NT
AUG = HD + 2
IN_W = 2448
C_QK, C_V, C_GLU, C_NSA, C_UV = 0, 512, 772, 1284, 1936
TOKW = IN_W - 2 * GW
CHUNKS = ((0, 512), (512, 772), (772, 1156), (1156, 1424), (1424, 1936))
WIDTHS = (512, 512, NS)
STARTS = (0, 512, SEQ)
SUMS_AT = (6 * 512, 7 * 512, 5 * 512 + NS)


def shape_constants():
    r = np.arange(P)
    q, k = r[:, None], r[None, :]
    parts = {}
    parts["ident"] = (q == k)
    parts["mhalf"] = np.full((P, 1), -0.5)
    parts["ones"] = np.ones((P, P))
    parts["triu"] = (q <= k)
    same = (q // NT == k // NT)
    parts["btriu"] = (same & (q <= k))[:, :NS]
    parts["cneg"] = np.where(k > q, NEG, 0.0)
    parts["wneg"] = np.where(k <= q, NEG, 0.0)
    end = (np.arange(NPB) + 1) * BLK - 1
    pos = np.arange(QT)[None, :, None] * P + r[:, None, None]
    ok = end[None, None, :] <= pos
    parts["cmpneg"] = np.where(ok, 0.0, NEG).reshape(P, -1)
    parts["cmp01"] = ok.reshape(P, -1)
    half = HD // 2
    inv = (10000.0 ** (-np.arange(half, dtype=np.float64) / half)).astype(np.float32)
    rows = np.concatenate([np.arange(QT)[None, :] * P + r[:, None], (PAST + r % NT)[:, None]], axis=1)
    ang = rows.astype(np.float32)[:, :, None] * inv
    parts["cos"] = np.cos(ang).astype(np.float32).reshape(P, -1)
    parts["sin"] = np.sin(ang).astype(np.float32).reshape(P, -1)
    parts["tril"] = (k <= q)
    parts["btril"] = (same & (k <= q))[:, :NS]
    parts["later"] = ((q // NPG == k // NPG) & (q > k))
    m = np.arange(NS // 2)[None, :]
    parts["hsum"] = ((q // (NH * NT) == m // NT) & (q % NT == m % NT))
    parts["hmask"] = ((r[:, None] % (NH * NT)) // NT == np.arange(NH)[None, :])
    parts["newneg"] = np.where(np.arange(NT)[None, :] > r[:, None] % NT, NEG, 0.0)
    parts["winneg"] = np.where(np.arange(NT)[None, :] <= r[:, None] % NT, NEG, 0.0)
    j = np.arange(NSB)
    parts["before"] = np.broadcast_to((j[None, :] < j[:, None]).reshape(1, -1), (P, NSB * NSB))
    at, cols, off = {}, [], 0
    for name, a in parts.items():
        a = np.ascontiguousarray(a, dtype=np.float32)
        at[name] = (off, a.shape[1])
        cols.append(a)
        off += a.shape[1]
    return at, np.concatenate(cols, axis=1)


CONST_AT, _ = shape_constants()
CONST_W = sum(w for _, w in CONST_AT.values())
ARENA_W = 53100


class Layout:

    def __init__(self, arena, start, end):
        self.arena, self.at, self.end = arena, start, end

    def take(self, cols, dtype=F32, **shape):
        words = cols if dtype == F32 else (cols + 1) // 2
        a = self.arena[:, self.at:self.at + words]
        self.at += words
        assert self.at <= self.end, (self.at, self.end)
        if dtype != F32:
            a = a.bitcast(dtype)
        if shape:
            names = list(shape)
            a = a.rearrange(f"p ({' '.join(names)}) -> p {' '.join(names)}", **shape)
        return a


class Chain:

    def __init__(self, eng, sem):
        self.eng, self.sem, self.n = eng, sem, 0

    def next(self):
        self.n += 1
        return self.n

    def restart(self):
        self.eng.sem_clear(self.sem)
        self.n = 0


def build_step(nc, A, O, layers=DEPTH, stop=99):
    ctx = ExitStack()
    with ctx, nc.allow_non_contiguous_dma(reason="columns of a few elements in small tables"):
        arena = ctx.enter_context(nc.sbuf_tensor("arena", [P, ARENA_W], F32))
        PS = ctx.enter_context(nc.psum_tensor("PS", [P, 4096], F32))

        def bank(n, cols=512, dtype=F32):
            return PS[:, n * 512:n * 512 + cols]

        def scratch(name, shape):
            return nc.dram_tensor(name, shape, F32).ap()

        qa_s = scratch("qa_s", (ROWS, NH, AUG))
        ka_s = scratch("ka_s", (ROWS, NH, AUG))
        va_s = scratch("va_s", (ROWS, NH, HD))
        qc_s = scratch("qc_s", (ROWS, NH, HD))
        kvc_s = scratch("kvc_s", (ROWS, 6, HD))
        g_s = scratch("g_s", (ROWS, 12))
        o_s = scratch("o_s", (ROWS, 4, NH, HD))
        y_s = scratch("y_s", (P, 2 * ROWS))
        suf_s = scratch("suf_s", (NB, NH, LK))
        sel_s = scratch("sel_s", (NS, NSB))
        oc_s = scratch("oc_s", (NB, NH * NT, HD))
        of_s = scratch("of_s", (NB, 2, NH * NT, HD))

        fixed = Layout(arena, 0, ARENA_W)
        const = fixed.take(CONST_W)

        def C(name, rows=P):
            off, w = CONST_AT[name]
            return const[0:rows, off:off + w]

        ident, ones, triu = C("ident"), C("ones"), C("triu")
        identb = fixed.take(P, BF16)
        cnegb = fixed.take(P, BF16)
        wnegb = fixed.take(P, BF16)
        pages = fixed.take(NB * NPG)[0:1, :].bitcast(I32)
        page_rows = fixed.take(1).bitcast(I32)
        XT = fixed.take(KD * ROWS, k=KD, n=ROWS)
        base = fixed.at

        lo = Layout(arena, base, ARENA_W)
        XNT = lo.take(KD * ROWS, k=KD, n=ROWS)
        after_xnt = lo.at
        Wt = lo.take(KD * TOKW, k=KD, n=TOKW)
        glu_at = lo.at
        Wg = lo.take(KD * 512, k=KD, n=512)
        SG = lo.take(ROWS)
        t1 = Layout(arena, glu_at, ARENA_W)
        Z = t1.take(1164)
        SQ = t1.take(1152)
        T10 = t1.take(640)
        SN = t1.take(640)
        XTT = [t1.take(KD * P, k=KD, n=P) for _ in range(2)]
        lo.at = max(lo.at, t1.at)
        tile_at = lo.at
        ZA = [lo.take(8 * AUG, g=8, d=AUG) for _ in range(2)]
        RN = [lo.take(640, g=10, d=HD) for _ in range(2)]
        VB = [lo.take(260) for _ in range(2)]
        UV = [lo.take(512) for _ in range(2)]
        VN = [lo.take(GW) for _ in range(2)]
        OD = [lo.take(GW) for _ in range(2)]
        G12 = [lo.take(12) for _ in range(2)]
        LF = [lo.take(4) for _ in range(2)]
        n1 = Layout(arena, tile_at, lo.at)
        SQ2 = n1.take(2 * ROWS, k=2, n=ROWS)
        RST = n1.take(ROWS)
        GV = n1.take(ROWS)
        n1 = Layout(arena, tile_at, lo.at)
        WMr = n1.take(4 * P, g=4, n=P)
        WM8r = n1.take(4 * NS, g=4, n=NS)
        GL = lo.take(2 * (CW - 1 + SEQ), c=2, n=CW - 1 + SEQ)
        GLS = lo.take(2 * NB * (CW - 1 + NT), c=2, b=NB, n=CW - 1 + NT)
        SGL = lo.take(2 * NS, c=2, n=NS)
        RSK = [lo.take(1) for _ in range(2)]
        RSC = lo.take(QT + 1)
        CS = lo.take(2 * GW, c=2, n=GW)
        CPO = CS.rearrange("p c n -> p (c n)")
        GQK = lo.take(2 * HD, a=2, d=HD)
        GN10 = lo.take(640, g=10, d=HD)
        LNG = lo.take(2 * GW, a=2, n=GW)
        BS = lo.take(4)
        BS8 = lo.take(4)
        BFB = lo.take(4)
        G1 = lo.take(KD)
        CWT = lo.take(2 * CW, c=2, j=CW)
        CB = lo.take(2)
        WMT = lo.take(4 * P, g=4, n=P)
        WM8T = lo.take(4 * NS, g=4, n=NS)
        SS18 = lo.take(19)
        EX = lo.take(64)
        CARRY = lo.take(4)
        BN6 = lo.take(6)
        BN2 = lo.take(2)

        lo = Layout(arena, base, ARENA_W)
        NTOK = NB * PAST + SEQ
        CT = lo.take(NTOK + BLK)
        PHI = lo.take(BLK * P, c=BLK, n=P)
        PG = [lo.take(4 * P, j=4, n=P) for _ in range(4)]
        CP8 = lo.take(QT * P, t=QT, n=P)
        PE2 = lo.take(P)
        LFP = lo.take(PAGE * NH, t=PAGE, h=NH)
        PFX = lo.take(NH * PAGE, h=NH, t=PAGE)
        TOT = lo.take(4)
        LAT = lo.take(4)
        Yc = lo.take(2 * ROWS, c=2, n=ROWS)
        assert lo.at <= tile_at
        assert lo.at <= ARENA_W - 700
        KVC = arena[:, ARENA_W - 545:ARENA_W]

        lo = Layout(arena, base, ARENA_W - 545)
        QF = [lo.take(QT * AUG, t=QT, d=AUG) for _ in range(2)]
        KF = [lo.take(QT * AUG, t=QT, d=AUG) for _ in range(2)]
        VF = [lo.take(QT * HD, t=QT, d=HD) for _ in range(2)]
        QN = [lo.take(QT * HD, t=QT, d=HD) for _ in range(2)]
        GH = [lo.take(QT * 3, t=QT, c=3) for _ in range(2)]
        KV4 = lo.take(QT * 4 * HD, t=QT, g=4, d=HD)
        QFT = lo.take(SEQ)
        KFT = lo.take(SEQ)
        QNT = lo.take(SEQ)
        KST = lo.take(SEQ)
        KWT = lo.take(SEQ)
        VREP = lo.take(P, i=4, n=NPB)
        VBD = lo.take(4 * HD, i=4, d=HD)
        PR = [lo.take(SEQ) for _ in range(2)]
        PTR = [lo.take(SEQ) for _ in range(2)]
        NMX = lo.take(24)
        RS = lo.take(24)
        RI = lo.take(24)
        SC = lo.take(QT * NPB, t=QT, n=NPB)
        SC8 = lo.take(QT)
        PTC = lo.take(2 * P, g=2, n=P)
        OF = [lo.take(QT * HD, t=QT, d=HD) for _ in range(2)]
        ON = [lo.take(QT * HD, t=QT, d=HD) for _ in range(2)]

        lo = Layout(arena, base, ARENA_W - 545)
        KVP = [lo.take(NPG * 512, j=NPG, n=512) for _ in range(2)]
        SLP = [lo.take(NPG * P, j=NPG, n=P) for _ in range(2)]
        WNP = [lo.take(4 * P, j=4, n=P) for _ in range(2)]
        KNEW = [lo.take(GW) for _ in range(2)]
        VNEW = [lo.take(GW) for _ in range(2)]
        KV4N = [lo.take(GW, g=4, d=HD) for _ in range(2)]
        KT2 = lo.take(2 * LK, a=2, n=LK)
        KSTs = lo.take(LK)
        KWTs = lo.take(WIN + NT)
        BIAS = lo.take(LK)
        SF = lo.take(LK)
        SSL = lo.take(LK)
        SW = lo.take(WIN + NT)
        WMASK = lo.take(WIN + NT)
        PTF = lo.take(17 * 32, j=17, n=32)
        OO = lo.take(GW)
        OH = [lo.take(HD) for _ in range(2)]
        OCM = [lo.take(HD) for _ in range(2)]
        QALL = lo.take(2 * NB * 32, a=2, b=NB, n=32)
        QNALL = lo.take(NB * 32, b=NB, n=32)
        QB = lo.take(2 * 32, a=2, n=32)
        QNB = lo.take(32)
        FQ = lo.take(NB)
        GB = lo.take(NB * 3, b=NB, c=3)
        SNB = lo.take(NB * NSB, b=NB, j=NSB)
        SNB1 = [lo.take(NSB) for _ in range(2)]
        OCB = lo.take(NB * HD, b=NB, d=HD)
        MX8 = lo.take(8)
        ST = lo.take(8)
        l2 = Layout(arena, base + 8192, base + 16384)
        QS = l2.take(NH * HD, h=NH, d=HD)
        QCS = l2.take(NH * HD, h=NH, d=HD)
        PC = l2.take(2 * NCB, g=2, n=NCB)
        PC4 = l2.take(4)
        PTCs = l2.take(2 * P, g=2, n=P)
        VCT = l2.take(NB * P, b=NB, n=P)
        IMP = l2.take(NSB)
        GT = l2.take(NSB * NSB, j=NSB, i=NSB)
        EQ = l2.take(NSB * NSB, j=NSB, i=NSB)
        RK = l2.take(NSB)
        OCS = l2.take(2 * HD, g=2, d=HD)

        lo = Layout(arena, base, ARENA_W)
        OTH = lo.take(KD * ROWS, BF16, k=KD, n=ROWS)
        OTL = lo.take(KD * ROWS, BF16, k=KD, n=ROWS)
        gemm_at = lo.at
        WF = [lo.take(16 * P, k=16, n=P) for _ in range(2)]
        WH = [lo.take(16 * P, BF16, k=16, n=P) for _ in range(2)]
        WL = [lo.take(16 * P, BF16, k=16, n=P) for _ in range(2)]
        RL = [lo.take(ROWS) for _ in range(2)]
        merge_at = lo.at
        OA = [lo.take(3 * GW, g=3, n=GW) for _ in range(2)]
        OAQ = lo.take(GW)
        GNB = lo.take(3 * GW, g=3, n=GW)
        S3 = [lo.take(3) for _ in range(2)]
        GCB = lo.take(2)
        CB2 = lo.take(2)
        CLG = lo.take(2)
        CLB = lo.take(2)
        YB = lo.take(2 * ROWS, c=2, n=ROWS)
        YQ = lo.take(2 * ROWS, c=2, n=ROWS)
        YM = lo.take(ROWS)
        XNH, XNL = OTH, OTL
        lo = Layout(arena, merge_at, ARENA_W)
        UH = lo.take(16 * ROWS, BF16, k=16, n=ROWS)
        UL = lo.take(16 * ROWS, BF16, k=16, n=ROWS)
        SQN = Layout(arena, merge_at, ARENA_W)
        SQN2 = SQN.take(2 * ROWS, k=2, n=ROWS)
        G2 = lo.take(KD)
        RST2 = lo.take(ROWS)

        lo = Layout(arena, base, ARENA_W)
        XS = [lo.take(DM) for _ in range(2)]
        XO = [lo.take(KD * P, k=KD, n=P) for _ in range(2)]

        def sem(name):
            return ctx.enter_context(nc.semaphore(name))

        phase_names = []
        S = {}

        def names(text):
            for n in text.split():
                S[n] = sem(n)
                phase_names.append(n)

        all_in = sem("all_in")
        all_in2 = sem("all_in2")
        go2 = {n: sem(f"go2_{n}") for n in ("pe", "act", "dve")}
        go = {n: sem(f"go_{n}") for n in ("pe", "act", "dve", "sp")}
        lfp_in = sem("lfp_in")
        loaded_once = sem("loaded_once")
        names("act_done dve_done")
        names("col_inv col_mean col_rstd row_mean row_rstd row_in0 row_in1 row_T row_ev row_out0 row_out1 row_cp")
        names("sq_ready sq_summed xn_ready g1_in w_glu0 w_glu1 w_tok gains glu_mm glu_in glu_sig glu_done")
        names("ct_in ct_T ct_ev wm_in wm_raw wm_T wm_ev")
        names("xt_ready z_mm z_ev z_free na_ready ex_ready lf_ready small_mm fin st0 st1 tail_T tail_ev tail_out y_out old_out")
        names("phi_in pe_in pg0 pg1 pg2 pg3 pg_T pg_ev cp_in lfp_ready page_next tot_ready lat_mm suf_ready suf_out kvc_mm kvc_ready zero_ready")
        names("head_in kv4_in tr_T tr_ev vb_ready s_mm nm_ready p_ready pt_T pt_evA pt_evD pv_mm o_done cs_mm cs_ready ce_ready cp_ready cpt_T cpt_ev cpv_mm on_ready o_ready o_out")
        names("q_in q_T q_ev vct_ev sm_ready imp_mm rank_ready rank_out aux_in kv_in0 kv_in1 kv_free0 kv_free1 bias_in bias_free os_out")
        names("oa_hi u_hi oa_in0 oa_in1 ss_ready oa_ready oa_T oa_ev y_in y_sq y_mm y_c y_done")
        names("xh_ready w_in0 w_in1 w_hi w_lo g_mm g_ev u_ready")
        batch_at = len(phase_names)
        names("pool_done2 new_T new_ev bias_ready os_stored")
        names("kt_T kt_evA kt_evD qb_ready sc_mm sc_ev mx_ready e_ready ptn_T ptn_ev ov_mm ov_done os_ready")
        first_sem, last_sem = S[phase_names[0]].num, S[phase_names[-1]].num
        assert last_sem - first_sem == len(phase_names) - 1, (first_sem, last_sem)

        batch_sem = S[phase_names[batch_at]].num

        block = ctx.enter_context(nc.Block())

        def arrive(e, who):
            e.drain().then_inc(all_in, 1)
            e.wait_ge(go[who], 1)
            e.sem_clear(go[who])

        def arrive2(e, who):
            e.drain().then_inc(all_in2, 1)
            e.wait_ge(go2[who], 1)
            e.sem_clear(go2[who])

        def over_tiles(e, step, chain=None, between=None):
            def peeled(t, k, m):
                step(t, k, m)
                if between and t in between:
                    between[t]()

            peeled(0, 0, 0)
            peeled(1, 1, 0)
            with e.Fori(0, 2) as i:
                if chain:
                    chain.restart()
                step(2 * i + 2, 0, i + 1)
                step(2 * i + 3, 1, i + 1)
            if chain:
                chain.restart()
            if between and 5 in between:
                between[5]()
            peeled(6, 0, 3)
            peeled(7, 1, 3)
            peeled(8, 0, 4)

        @block.sync
        def _(sp):
            sp.dma_start(const, A["consts"]).then_inc(loaded_once, 16)
            sp.dma_start(pages, A["page_table"].rearrange("b j -> (b j)").unsqueeze(0)).then_inc(loaded_once, 16)

            sp.dma_start(page_rows, A["page_table"].rearrange("b j -> (b j)").unsqueeze(1)).then_inc(loaded_once, 16)

            def row_in(t, k, m):
                if isinstance(t, int):
                    src = A["x_prompt"][0, t * P:(t + 1) * P, :] if t < QT else A["x_sample"].rearrange("b t d -> (b t) d")
                    rows = P if t < QT else NS
                else:
                    src, rows = A["x_prompt"][0, bass.ds(t * P, P), :], P
                if not (isinstance(t, int) and t < 2):
                    sp.wait_ge(S["row_T"], t - 1)
                sp.dma_start(XS[k][0:rows, :], src).then_inc(S[f"row_in{k}"], 16)

            over_tiles(sp, row_in)
            arrive(sp, "sp")

            with sp.Fori(0, layers) as l:
                def w(name):
                    return A[name][bass.ds(l, 1)]

                sp.dma_start(G1, w("norm1_g").rearrange("o (k p) -> p (o k)", p=P)).then_inc(S["g1_in"], 16)
                for f in range(2):
                    for half in range(2):
                        n = (2 * half + f) * P
                        sp.dma_start(Wg[:, :, n:n + P], w("w_in")[:, :, C_GLU + n:C_GLU + n + P]
                                     .rearrange("o (k p) n -> p (o k) n", p=P)).then_inc(S[f"w_glu{f}"], 16)
                sp.dma_start(CS[0:4 * (CW - 1), :, :],
                    w("state_conv").rearrange("o (g b) r n -> (o b r) g n", g=2)).then_inc(S["ct_in"], 16)
                def spread(dst, src, name="gains"):
                    sp.dma_start(dst, src.to_broadcast([dst.shape[0], src.shape[-1]])).then_inc(S[name], 16)

                spread(GQK[:, 0, :], w("fox_qn_g"))
                spread(GQK[:, 1, :], w("fox_kn_g"))
                for h in range(NH):
                    spread(GN10[:, h, :], w("nsa_qn_g"))
                for b in range(3):
                    spread(GN10[:, NH + 2 * b, :], w("nsa_kn_g")[:, b, :])
                spread(LNG[:, 0, :], w("gmlp_ln_g"))
                spread(LNG[:, 1, :], w("gmlp_ln_b"))
                spread(BFB, w("fox_bf"))
                sp.dma_start(BS, w("gmlp_bs").rearrange("o g t -> t (o g)")).then_inc(S["gains"], 16)
                for b in range(NB):
                    sp.dma_start(BS8[b * NT:(b + 1) * NT, :], w("gmlp_bs")[:, :, 0:NT].rearrange("o g t -> t (o g)")).then_inc(S["gains"], 16)
                for c in range(2):
                    sp.dma_start(CWT[:, c, :], w("conv_w")[:, :, c * P:(c + 1) * P].rearrange("o j p -> p (o j)")).then_inc(S["gains"], 16)
                sp.dma_start(CB, w("conv_b").rearrange("o (c p) -> p (o c)", p=P)).then_inc(S["gains"], 16)
                for c, (a, b) in enumerate(CHUNKS):
                    src = a if a < C_GLU else a - C_GLU + C_NSA
                    sp.dma_start(Wt[:, :, a:b], w("w_in")[:, :, src:src + b - a].rearrange("o (k p) n -> p (o k) n", p=P)).then_inc(S["w_tok"], 16)
                sp.wait_ge(S["sq_summed"], KD)
                sp.wait_ge(S["xn_ready"], KD)
                sp.dma_start(WMr, w("gmlp_ws").rearrange("o g t s -> t (o g) s")).then_inc(S["wm_in"], 16)
                for b in range(NB):
                    for c in range(NB):
                        sp.dma_start(WM8r[b * NT:(b + 1) * NT, :, c * NT:(c + 1) * NT],
                            w("gmlp_ws")[:, :, 0:NT, 0:NT].rearrange("o g t s -> t (o g) s")).then_inc(S["wm_in"], 16)
                sp.dma_start(O["nsa_win_s"][bass.ds(l, 1), :, 0:WIN - NT], w("state_nsa_win")[:, :, NT:WIN]).then_inc(S["old_out"], 16)
                sp.dma_start(O["conv_s"][bass.ds(l, 1), :, 0:CW - 1 - NT], w("state_conv")[:, :, NT:CW - 1]).then_inc(S["old_out"], 16)

                def store_tile(t, k):
                    s = f"st{k}"
                    sp.wait_ge(S["fin"], t + 1)
                    if isinstance(t, int) and t == QT:
                        rows = NS
                        r = slice(SEQ, ROWS)
                        fox = O["fox_kv_s"][bass.ds(l, 1)].rearrange("o b t c h d -> (o b t) c h d")
                        nsa = O["nsa_kv_s"][bass.ds(l, 1)].rearrange("o b t c d -> (o b t) c d")
                        logf = O["fox_logf_s"][bass.ds(l, 1)].rearrange("o b t h -> (o b t) h")
                    else:
                        rows = P
                        r = bass.ds(t * P, P)
                        fox = O["fox_kv_p"][bass.ds(l, 1), 0, r].rearrange("o r c h d -> (o r) c h d")
                        nsa = O["nsa_kv_p"][bass.ds(l, 1), 0, r].rearrange("o r c d -> (o r) c d")
                        logf = O["fox_logf_p"][bass.ds(l, 1), 0, r].rearrange("o r h -> (o r) h")
                    v3 = VB[k][0:rows, 0:GW].rearrange("p (h d) -> p h d", h=NH)
                    sp.dma_start(qa_s[r], ZA[k][0:rows, 0:NH, :]).then_inc(S[s], 16)
                    sp.dma_start(ka_s[r], ZA[k][0:rows, NH:2 * NH, :]).then_inc(S[s], 16)
                    sp.dma_start(va_s[r], v3).then_inc(S[s], 16)
                    sp.dma_start(fox[:, 0], ZA[k][0:rows, NH:2 * NH, 0:HD]).then_inc(S[s], 16)
                    sp.dma_start(fox[:, 1], v3).then_inc(S[s], 16)
                    sp.dma_start(qc_s[r], RN[k][0:rows, 0:NH, :]).then_inc(S[s], 16)
                    sp.dma_start(kvc_s[r], RN[k][0:rows, NH:, :]).then_inc(S[s], 16)
                    sp.dma_start(nsa, RN[k][0:rows, NH:NH + 4, :]).then_inc(S[s], 16)
                    sp.dma_start(g_s[r], G12[k][0:rows, :]).then_inc(S[s], 16)
                    sp.dma_start(o_s[r, 3].rearrange("r h d -> r (h d)"), OD[k][0:rows, :]).then_inc(S[s], 16)
                    sp.dma_start(logf, LF[k][0:rows, :]).then_inc(S[s], 16)
                    if isinstance(t, int) and t == QT:
                        sp.dma_start(O["gmlp_v_s"][bass.ds(l, 1)].rearrange("o b t n -> (o b t) n"), VN[k][0:NS, :]).then_inc(S[s], 16)

                def store_step(t, k, m):
                    if not (isinstance(t, int) and t == 0):
                        store_tile(t - 1, 1 - k)

                over_tiles(sp, store_step)
                store_tile(8, 0)
                sp.wait_ge(S["tail_ev"], 1)
                sp.dma_start(O["conv_p"][bass.ds(l, 1)].rearrange("o b r n -> (o b r) n"), CPO[0:CW - 1, 0:GW]).then_inc(S["tail_out"], 16)
                sp.dma_start(O["conv_s"][bass.ds(l, 1), :, CW - 1 - NT:].rearrange("o b t n -> (o b) t n"),
                    CPO[0:NS, GW:2 * GW]).then_inc(S["tail_out"], 16)
                sp.wait_ge(S["st0"], 16 * (11 * 5 + 1))
                sp.wait_ge(S["st1"], 16 * 11 * 4)
                sp.wait_ge(S["w_tok"], 80)
                sp.wait_ge(S["tail_out"], 32)
                sp.wait_ge(S["old_out"], 32)
                arrive(sp, "sp")
                if stop <= 2:
                    return

                sp.dma_start(PE2[0:BLK, :].rearrange("p (s d) -> p s d", s=2), w("nsa_pe").rearrange("o s c d -> c (o s) d")).then_inc(S["pe_in"], 16)
                sp.dma_start(CP8.rearrange("p t (s d) -> p t s d", s=2), kvc_s[0:SEQ, 0:2, :].rearrange("(t p) s d -> p t s d", p=P)).then_inc(S["cp_in"], 16)
                with sp.Fori(0, NB) as i:
                    for k in (0, 2):
                        for j in range(4):
                            page = sp.value_load(pages[:, bass.ds(i * NPG + (4 * k + j), 1)], min_val=0, max_val=POOL - 1)
                            if j == 0:
                                sp.wait_ge(S["pg_T"], 4 * i + k + 1)
                            sp.dma_start(PG[k][:, j, :].rearrange("p (s d) -> p s d", s=2),
                                         A["cache_nsa_kv"][bass.ds(l, 1), bass.ds(page, 1), :, 0:2, :]
                                         .rearrange("o a p s d -> (o a p) s d")).then_inc(S[f"pg{k}"], 16)
                sp.dma_start(O["nsa_win_p"][bass.ds(l, 1), 0].rearrange("o r c d -> (o r) c d"), kvc_s[SEQ - WIN:SEQ, 4:6, :]).then_inc(S["old_out"], 16)
                sp.dma_start(O["nsa_win_s"][bass.ds(l, 1), :, WIN - NT:].rearrange("o b t c d -> (o b) t c d"),
                    kvc_s[SEQ:ROWS, 4:6, :].rearrange("(b t) c d -> b t c d", b=NB)).then_inc(S["old_out"], 16)
                for h in range(NH):
                    sp.dma_start(suf_s[:, h, PAST:LK], ka_s[SEQ:ROWS, h, HD + 1].rearrange("(b t) -> b t", b=NB)).then_inc(S["old_out"], 16)
                sp.wait_ge(S["suf_ready"], 1)
                for b in range(NB):
                    sp.dma_start(suf_s[b, :, 0:PAST].rearrange("h (j t) -> j h t", j=NPG),
                        PFX[b * NPG:(b + 1) * NPG, :, :]).then_inc(S["suf_out"], 16)
                sp.wait_ge(S["suf_out"], 16 * NB)
                sp.wait_ge(S["old_out"], 16 * (2 + NH))
                sp.wait_ge(S["y_done"], 1)
                sp.dma_start(y_s, Yc.rearrange("p c n -> p (c n)")).then_inc(S["y_out"], 16)
                sp.wait_ge(S["y_out"], 16)
                sp.wait_ge(S["kvc_ready"], 1)
                arrive(sp, "sp")
                if stop <= 3:
                    return

                def head_in(h):
                    def rows_of(x, width):
                        return x[0:SEQ, h, 0:width].rearrange("(t p) d -> p t d", p=P)

                    k = h % 2
                    sp.dma_start(QF[k], rows_of(qa_s, AUG)).then_inc(S["head_in"], 16)
                    sp.dma_start(KF[k], rows_of(ka_s, AUG)).then_inc(S["head_in"], 16)
                    sp.dma_start(VF[k], rows_of(va_s, HD)).then_inc(S["head_in"], 16)
                    sp.dma_start(QN[k], rows_of(qc_s, HD)).then_inc(S["head_in"], 16)
                    sp.dma_start(GH[k], g_s[0:SEQ, 3 * h:3 * h + 3].rearrange("(t p) c -> p t c", p=P)).then_inc(S["head_in"], 16)

                def head_out(h):
                    for n, o in ((0, OF), (2, ON)):
                        sp.dma_start(o_s[0:SEQ, n, h, :].rearrange("(t p) d -> p t d", p=P), o[h % 2]).then_inc(S["o_out"], 16)

                sp.dma_start(KV4, kvc_s[0:SEQ, 2:6, :].rearrange("(t p) g d -> p t g d", p=P)).then_inc(S["kv4_in"], 16)
                head_in(0)
                sp.wait_ge(S["kv4_in"], 16)
                sp.wait_ge(S["head_in"], 80)
                arrive(sp, "sp")
                for h in range(NH):
                    if h:
                        head_out(h - 1)
                    if h + 1 < NH:
                        head_in(h + 1)
                        sp.wait_ge(S["head_in"], 80)
                    if h:
                        sp.wait_ge(S["o_out"], 32)
                    if h + 1 == NH:
                        sp.wait_ge(S["o_ready"], 1)
                        head_out(h)
                        sp.wait_ge(S["o_out"], 64)
                    arrive(sp, "sp")
                if stop <= 4:
                    return

                sp.dma_start(QS[0:NS], qa_s[SEQ:ROWS, :, 0:HD]).then_inc(S["q_in"], 16)
                sp.dma_start(QCS[0:NS], qc_s[SEQ:ROWS]).then_inc(S["q_in"], 16)
                for h in range(NH):
                    r = slice(h * NT, (h + 1) * NT)
                    sp.dma_start(FQ[r, :], qa_s[SEQ:ROWS, h, HD].rearrange("(b t) -> t b", t=NT)).then_inc(S["aux_in"], 16)
                    sp.dma_start(GB[r], g_s[SEQ:ROWS, 3 * h:3 * h + 3].rearrange("(b t) c -> t b c", t=NT)).then_inc(S["aux_in"], 16)
                def request_in(b, k):
                    bb = bass.ds(b, 1)
                    row = bass.ds(SEQ + b * NT, NT)
                    for j in range(NPG):
                        page = sp.value_load(pages[:, bass.ds(b * NPG + j, 1)], min_val=0, max_val=POOL - 1)
                        at = A["cache_fox_kv"][bass.ds(l, 1), bass.ds(page, 1)]
                        sp.dma_start(KVP[k][:, j, :], at.rearrange("o a p c h d -> (o a p) (c h d)")).then_inc(S[f"kv_in{k}"], 16)
                        at = A["cache_nsa_kv"][bass.ds(l, 1), bass.ds(page, 1), :, 2:4, :]
                        sp.dma_start(SLP[k][:, j, :].rearrange("p (s d) -> p s d", s=2),
                                     at.rearrange("o a p s d -> (o a p) s d")).then_inc(S[f"kv_in{k}"], 16)
                    sp.dma_start(WNP[k], A["state_nsa_win"][bass.ds(l, 1), bb]
                                 .rearrange("o b (j p) s d -> p (o b j) (s d)", p=P)).then_inc(S[f"kv_in{k}"], 16)
                    sp.dma_start(KNEW[k][0:NT, :].rearrange("p (h d) -> p h d", h=NH), ka_s[row, :, 0:HD]).then_inc(S[f"kv_in{k}"], 16)
                    sp.dma_start(VNEW[k][0:NT, :].rearrange("p (h d) -> p h d", h=NH), va_s[row]).then_inc(S[f"kv_in{k}"], 16)
                    sp.dma_start(KV4N[k][0:NT], kvc_s[row, 2:6, :]).then_inc(S[f"kv_in{k}"], 16)

                def bias_in(b):
                    for h in range(NH):
                        sp.dma_start(BIAS[h * NT:(h + 1) * NT, :],
                                     suf_s[bass.ds(b, 1), h, :].to_broadcast([NT, LK])).then_inc(S["bias_in"], 16)

                request_in(0, 0)
                bias_in(0)
                sp.wait_ge(S["kv_free1"], 1)
                request_in(1, 1)
                sp.wait_ge(S["bias_free"], 1)
                bias_in(1)
                with sp.Fori(0, NB // 2 - 1) as i:
                    for k in range(2):
                        b = 2 * i + 2 + k
                        sp.wait_ge(S[f"kv_free{k}"], i + 1 + k)
                        request_in(b, k)
                        sp.wait_ge(S["bias_free"], 2 * i + 2 + k)
                        bias_in(b)
                sp.wait_ge(S["os_out"], 16 * 2 * NB)
                arrive(sp, "sp")
                if stop <= 6:
                    return

                sp.dma_start(YB, y_s.rearrange("p (c n) -> p c n", c=2)).then_inc(S["y_in"], 16)
                sp.dma_start(GCB, w("gnorm_g")[:, 1, :].rearrange("o (c p) -> p (o c)", p=P)).then_inc(S["y_in"], 16)
                sp.dma_start(CLG, w("conv_ln_g").rearrange("o (c p) -> p (o c)", p=P)).then_inc(S["y_in"], 16)
                sp.dma_start(CLB, w("conv_ln_b").rearrange("o (c p) -> p (o c)", p=P)).then_inc(S["y_in"], 16)
                for n, g in enumerate((0, 2, 3)):
                    spread(GNB[:, n, :], w("gnorm_g")[:, g, :], "y_in")

                def oa_in(t, k, m):
                    rows = NS if isinstance(t, int) and t == QT else P
                    r = slice(SEQ, ROWS) if rows == NS else bass.ds(t * P, P)
                    if not (isinstance(t, int) and t < 2):
                        sp.wait_ge(S["oa_T"], t - 1)
                    if rows == NS:
                        for b in range(NB):
                            for g in range(2):
                                sp.dma_start(OA[k][b * NT:(b + 1) * NT, g, :].rearrange("p (h d) -> p h d", h=NH),
                                    of_s[b, g].rearrange("(h t) d -> t h d", h=NH)).then_inc(S[f"oa_in{k}"], 16)
                    else:
                        sp.dma_start(OA[k][0:rows, 0, :], o_s[r, 0].rearrange("r h d -> r (h d)")).then_inc(S[f"oa_in{k}"], 16)
                        sp.dma_start(OA[k][0:rows, 1, :], o_s[r, 2].rearrange("r h d -> r (h d)")).then_inc(S[f"oa_in{k}"], 16)
                    sp.dma_start(OA[k][0:rows, 2, :], o_s[r, 3].rearrange("r h d -> r (h d)")).then_inc(S[f"oa_in{k}"], 16)

                def out_block(n, k):
                    sp.wait_ge(S["w_lo"], n + 1)
                    sp.dma_start(WF[k][:, 0:KD, :], w("w_out")[:, :, bass.ds(n * P, P)]
                                 .rearrange("o (k p) n -> p (o k) n", p=P)).then_inc(S[f"w_in{k}"], 16)

                out_block(0, 0)
                out_block(1, 1)
                over_tiles(sp, oa_in)
                with sp.Fori(0, KD // 2 - 1) as i:
                    for k in range(2):
                        out_block(2 * i + 2 + k, k)
                arrive(sp, "sp")
                if stop <= 7:
                    return

                sp.dma_start(G2, w("norm2_g").rearrange("o (k p) -> p (o k)", p=P)).then_inc(S["gains"], 16)
                sp.wait_ge(S["gains"], 16)
                arrive(sp, "sp")
                with sp.Fori(0, 2) as half:
                    with sp.Fori(0, 8) as i:
                        for k in range(2):
                            n = 2 * i + k
                            sp.wait_ge(S["w_lo"], n + 1)
                            sp.dma_start(WF[k][:, 0:KD, :], w("w_ff1")[:, :, bass.ds(half * (DFF // 2) + n * P, P)]
                                .rearrange("o (k p) n -> p (o k) n", p=P)).then_inc(S[f"w_in{k}"], 16)
                    with sp.Fori(0, KD // 2) as i:
                        for k in range(2):
                            n = 2 * i + k
                            sp.wait_ge(S["w_lo"], 16 + n + 1)
                            sp.dma_start(WF[k], w("w_ff2")[:, bass.ds(half * (DFF // 2), DFF // 2), bass.ds(n * P, P)]
                                .rearrange("o (k p) n -> p (o k) n", p=P)).then_inc(S[f"w_in{k}"], 16)
                    arrive(sp, "sp")

            def row_out(t, k, m):
                sp.wait_ge(S["row_ev"], t + 1)
                if isinstance(t, int):
                    dst = O["y_prompt"][0, t * P:(t + 1) * P, :] if t < QT else O["y_sample"].rearrange("b t d -> (b t) d")
                    rows = P if t < QT else NS
                else:
                    dst, rows = O["y_prompt"][0, bass.ds(t * P, P), :], P
                sp.dma_start(dst, XS[k][0:rows, :]).then_inc(S[f"row_out{k}"], 16)

            over_tiles(sp, row_out)
            sp.wait_ge(S["row_out0"], 16 * 5)
            sp.wait_ge(S["row_out1"], 16 * 4)

        @block.tensor
        def _(pe):
            mm, tr = nc.tensor.matmul, nc.tensor.transpose

            def rows_of(t):
                return NS if isinstance(t, int) and t == QT else P

            pe.wait_ge(loaded_once, 48)

            def row_T(t, k, m):
                r = rows_of(t)
                pe.wait_ge(S[f"row_in{k}"], 16 * (m + 1))
                if not (isinstance(t, int) and t < 2):
                    pe.wait_ge(S["row_ev"], t - 1)
                for j in range(KD):
                    at = (2 * k + j // 4) * 512 + (j % 4) * P
                    last = tr(PS[:, at:at + r], XS[k][0:r, j * P:(j + 1) * P], ident[0:r, 0:r])
                last.then_inc(S["row_T"], 1)

            over_tiles(pe, row_T)
            arrive(pe, "pe")

            def sum_squares(src, k):
                pe.wait_ge(S["sq_ready"], k + 1)
                for a, n, at in zip(STARTS, WIDTHS, SUMS_AT):
                    last = mm(PS[:, at:at + n], ones, src[:, k % 2, a:a + n], start=k == 0, stop=k == KD - 1)
                last.then_inc(S["sq_summed"], 1)

            def gemm(k, blocks, xh, xl, wh, wl):
                for c in range(blocks):
                    for n, (ww, xx) in enumerate(((wh, xh), (wh, xl), (wl, xh))):
                        for a, wd in zip(STARTS, WIDTHS):
                            last = mm(PS[:, 1536 * k + a:1536 * k + a + wd], ww[:, c, :], xx[:, c, a:a + wd],
                                      start=c == 0 and n == 0, stop=c == blocks - 1 and n == 2)
                return last

            with pe.Fori(0, layers) as l:
                for f in range(2):
                    pe.wait_ge(S[f"w_glu{f}"], 32)
                    if f:
                        pe.wait_ge(S["glu_done"], 1)
                    for s in range(2):
                        if f == 0 and s == 1:
                            pe.wait_ge(S["col_mean"], 1)
                        for k in range(KD):
                            if f == 0 and s == 0:
                                pe.wait_ge(S["xn_ready"], k + 1)
                                sum_squares(SQ2, k)
                            for a, n in zip(STARTS, WIDTHS):
                                last = mm(PS[:, 1536 * s + a:1536 * s + a + n],
                                          Wg[:, k, (2 * s + f) * P:(2 * s + f + 1) * P],
                                          XNT[:, k, a:a + n], start=k == 0, stop=k == KD - 1)
                    last.then_inc(S["glu_mm"], 1)
                pe.wait_ge(S["ct_in"], 16)
                n = NB // 2 * (CW - 1)
                for g in range(2):
                    for c in range(2):
                        at = 3072 + (2 * g + c) * n
                        last = tr(PS[:, at:at + n], CS[0:n, g, c * P:(c + 1) * P], ident[0:n, 0:n])
                last.then_inc(S["ct_T"], 1)
                pe.wait_ge(S["wm_raw"], 2)
                for g in range(4):
                    last = tr(PS[:, 3584 + g * P:3584 + (g + 1) * P], WMr[:, g, :], ident)
                last.then_inc(S["wm_T"], 1)
                pe.wait_ge(S["glu_done"], 2)
                for g in range(4):
                    last = tr(PS[0:NS, g * NS:(g + 1) * NS], WM8r[0:NS, g, :], ident[0:NS, 0:NS])
                last.then_inc(S["wm_T"], 1)
                pe.wait_ge(S["wm_ev"], 2)
                pe.wait_ge(S["w_tok"], 80)

                def small(t, k):
                    r = rows_of(t)
                    pe.wait_ge(S["lf_ready"], t + 1)
                    if not (isinstance(t, int) and t == 0):
                        pe.wait_ge(S["fin"], t)
                    tri, wm = (triu, WMT) if r == P else (C("btriu"), WM8T)
                    mm(PS[0:r, 2560:2564], tri[0:r, 0:r], LF[k][0:r, :], start=True, stop=True)
                    mm(PS[0:r, 2564:2568], ones[0:r, 0:r], LF[k][0:r, :], start=True, stop=True)
                    for g in range(4):
                        last = mm(PS[0:r, 3072 + g * HD:3072 + (g + 1) * HD], wm[0:r, g, :],
                                  VN[k][0:r, g * HD:(g + 1) * HD], start=True, stop=True)
                    last.then_inc(S["small_mm"], 1)

                def z_step(t, k, m):
                    r = rows_of(t)
                    pe.wait_ge(S["xt_ready"], t + 1)
                    for c, (a, b) in enumerate(CHUNKS):
                        if not (isinstance(t, int) and t == 0):
                            pe.wait_ge(S["z_ev"], 8 * (t - 1) + (2, 3, 5, 7, 8)[c])
                        for j in range(KD):
                            last = mm(PS[0:r, c * 512:c * 512 + b - a], XTT[k][:, j, 0:r], Wt[:, j, a:b],
                                      start=j == 0, stop=j == KD - 1)
                        last.then_inc(S["z_mm"], 1)
                    if not (isinstance(t, int) and t == 0):
                        small(t - 1, 1 - k)

                over_tiles(pe, z_step)
                small(8, 0)
                for c in range(2):
                    tr(PS[0:CW - 1, 3584 + c * P:3584 + (c + 1) * P], GL[:, c, SEQ:SEQ + CW - 1], ident)
                    last = tr(PS[0:NS, 3840 + c * P:3840 + (c + 1) * P], SGL[:, c, :], ident)
                last.then_inc(S["tail_T"], 1)
                arrive(pe, "pe")
                if stop <= 2:
                    return

                pe.sem_inc(S["pg_T"], 4)
                pe.wait_ge(S["pe_in"], 16)
                tr(bank(6, BLK), PE2[0:BLK, :], ident[0:BLK, 0:BLK]).then_inc(S["kvc_mm"], 1)
                pe.wait_ge(S["cp_in"], 16)
                for g in range(2):
                    for j in range(4):
                        last = tr(bank(4 + g)[:, j * P:(j + 1) * P], CP8[:, 4 * g + j, :], ident)
                last.then_inc(S["kvc_mm"], 1)
                with pe.Fori(0, NB) as i:
                    for k in range(4):
                        pe.wait_ge(S[f"pg{k}"], 64 * i + 64)
                        pe.wait_ge(S["pg_ev"], 4 * i + k + 1)
                        for j in range(4):
                            last = tr(bank(k)[:, j * P:(j + 1) * P], PG[k][:, j, :], ident)
                        last.then_inc(S["pg_T"], 1)
                pe.wait_ge(S["tot_ready"], 1)
                mm(bank(7, 4), C("later"), TOT, start=True, stop=True).then_inc(S["lat_mm"], 1)
                pe.wait_ge(S["phi_in"], 32)
                pe.wait_ge(S["pg_ev"], 4 * NB + 4)
                blocks = CT.rearrange("p (n c) -> p n c", c=BLK)
                for a, n in ((0, 272), (272, 273)):
                    for c in range(BLK):
                        last = mm(bank(0 if a == 0 else 1, n), PHI[:, c, :], blocks[:, a:a + n, c],
                                  start=c == 0, stop=c == BLK - 1)
                last.then_inc(S["kvc_mm"], 1)
                arrive(pe, "pe")
                if stop <= 3:
                    return

                def transposes(src, dst_rows, g, at_bank):
                    for j in range(4):
                        last = tr(bank(at_bank)[0:dst_rows, j * P:(j + 1) * P], src[:, 4 * g + j, :], ident)
                    last.then_inc(S["tr_T"], 1)

                pe.wait_ge(S["kv4_in"], 16)
                for n, (src, g) in enumerate(((0, 0), (0, 1), (2, 0), (2, 1))):
                    if n >= 2:
                        pe.wait_ge(S["tr_ev"], n - 1)
                    transposes(KV4[:, :, src, :], HD, g, 4 + n % 2)
                pe.wait_ge(S["vb_ready"], 1)
                tr(bank(7, HD), VREP[HD:P].rearrange("p i n -> p (i n)"), ident[HD:P, HD:P]).then_inc(S["vb_ready"], 1)
                arrive(pe, "pe")

                units = [(kind, i) for i in reversed(range(QT)) for kind in ("sel", "fox", "win")]

                def keys_of(u):
                    kind, i = units[u]
                    return list(range(max(0, i - WIN // P) if kind == "win" else 0, i + 1))

                def head(k):
                    for n, (src, r) in enumerate(((QN[k], HD), (QN[k], HD), (QF[k], AUG), (QF[k], AUG), (KF[k], AUG), (KF[k], AUG))):
                        if n >= 2:
                            pe.wait_ge(S["tr_ev"], n - 1)
                        transposes(src, r, n % 2, 4 + n % 2)
                    pe.wait_ge(S["tr_ev"], 6)
                    for i in range(QT):
                        last = mm(bank(7)[:, i * NPB:(i + 1) * NPB], QNT[0:HD, i * P:(i + 1) * P], KVC[0:HD, 512:544],
                                  start=True, stop=True)
                    last.then_inc(S["cs_mm"], 1)

                    def scores(u):
                        kind, i = units[u]
                        if u >= 2:
                            pe.wait_ge(S["p_ready"], u - 1)
                        q, kt, rows = {"sel": (QNT, KST, HD), "win": (QNT, KWT, HD), "fox": (QFT, KFT, AUG)}[kind]
                        js = keys_of(u)
                        for a in range(0, len(js), 4):
                            part = js[a:a + 4]
                            at = (u % 2) * 1024 + a * P
                            masks = []
                            if kind == "win" and i >= 4 and a == 0:
                                masks.append((0, wnegb))
                            if part[-1] == i:
                                masks.append((len(part) - 1, cnegb))
                            last = mm(PS[:, at:at + len(part) * P], q[0:rows, i * P:(i + 1) * P],
                                      kt[0:rows, part[0] * P:(part[-1] + 1) * P], start=True, stop=not masks)
                            for n, (c, mask) in enumerate(masks):
                                last = mm(PS[:, at + c * P:at + (c + 1) * P], identb, mask,
                                          start=False, stop=n == len(masks) - 1)
                        last.then_inc(S["s_mm"], 1)

                    groups = 0
                    scores(0)
                    scores(1)
                    pe.wait_ge(S["cp_ready"], 1)
                    for g in range(2):
                        last = tr(bank(7)[:, 256 + g * P:256 + (g + 1) * P],
                                  SC.rearrange("p t n -> p (t n)")[:, g * P:(g + 1) * P], ident)
                    last.then_inc(S["cpt_T"], 1)
                    pe.wait_ge(S["cpt_ev"], 1)
                    for g in range(2):
                        last = mm(bank(7)[:, g * GW:(g + 1) * GW], PTC[:, g, :],
                                  VBD.rearrange("p i d -> p (i d)"), start=True, stop=True)
                    last.then_inc(S["cpv_mm"], 1)
                    def values(u, groups):
                        kind, i = units[u]
                        js = keys_of(u)
                        pe.wait_ge(S["pt_evD"], (groups + 1) // 2)
                        if groups >= 2:
                            pe.wait_ge(S["pt_evA"], groups // 2)
                        if u >= 2:
                            pe.wait_ge(S["o_done"], u - 1)
                        if u == 1:
                            pe.wait_ge(S["on_ready"], 1)
                        for n, j in enumerate(js):
                            v = {"fox": VF[k][:, j, :], "sel": KV4[:, j, 1, :], "win": KV4[:, j, 3, :]}[kind]
                            last = mm(bank(6 + u % 2, HD), PTR[u % 2][:, n * P:(n + 1) * P], v,
                                      start=n == 0, stop=n == len(js) - 1)
                        last.then_inc(S["pv_mm"], 1)

                    counts = []
                    for u, (kind, i) in enumerate(units):
                        js = keys_of(u)
                        if u + 2 < len(units):
                            scores(u + 2)
                        pe.wait_ge(S["p_ready"], u + 1)
                        for a in range(0, len(js), 4):
                            if groups >= 2:
                                pe.wait_ge(S["pt_evA" if groups % 2 else "pt_evD"], groups // 2)
                            for j in range(a, min(a + 4, len(js))):
                                last = tr(bank(4 + groups % 2)[:, (j - a) * P:(j - a + 1) * P],
                                          PR[u % 2][:, j * P:(j + 1) * P], ident)
                            last.then_inc(S["pt_T"], 1)
                            groups += 1
                        counts.append(groups)
                        if u >= 1:
                            values(u - 1, counts[u - 1])
                    values(len(units) - 1, groups)
                    arrive(pe, "pe")

                with pe.Fori(0, NH // 2) as _:
                    for k in range(2):
                        head(k)
                if stop <= 4:
                    return

                pe.wait_ge(S["q_in"], 32)
                for a in range(2):
                    tr(bank(0)[:, a * NS:(a + 1) * NS], QS[0:NS].rearrange("p h d -> p (h d)")[:, a * P:(a + 1) * P], ident[0:NS, 0:NS])
                for h in range(NH):
                    last = tr(bank(1)[0:HD, h * NS:(h + 1) * NS], QCS[0:NS, h, :], ident[0:NS, 0:NS])
                last.then_inc(S["q_T"], 1)
                for b in range(NB):
                    last = tr(bank(2 + b // 4)[0:NCB, (b % 4) * P:(b % 4 + 1) * P], KVC[:, b * NCB:(b + 1) * NCB], ident)
                last.then_inc(S["q_T"], 1)
                pe.wait_ge(S["q_ev"], 1)
                for b in range(NB):
                    g, r = b // 4, (b % 4) * 32
                    last = mm(bank(4)[r:r + 32, g * NCB:(g + 1) * NCB], QNALL[0:HD, b, :],
                              KVC[0:HD, b * NCB:(b + 1) * NCB], start=True, stop=True)
                last.then_inc(S["sc_mm"], 1)
                pe.wait_ge(S["sm_ready"], 1)
                for g in range(2):
                    mm(bank(5)[g * 32:(g + 1) * 32, 0:NCB], C("hsum"), PC[:, g, :], start=True, stop=True)
                for g in range(2):
                    last = tr(bank(6)[0:NCB, g * P:(g + 1) * P], PC[:, g, :], ident)
                last.then_inc(S["imp_mm"], 1)
                pe.wait_ge(S["vct_ev"], 3)
                for b in range(NB):
                    g, r = b // 4, (b % 4) * 32
                    last = mm(bank(7)[r:r + 32, g * HD:(g + 1) * HD], PTCs[0:NCB, g, r:r + 32],
                              VCT[0:NCB, b, HD:P], start=True, stop=True)
                last.then_inc(S["imp_mm"], 1)
                arrive2(pe, "pe")
                if stop <= 5:
                    return

                def key_groups(k, what):
                    if what == "fox":
                        return [(KVP[k][:, 4 * g:4 * g + 4, a * P:(a + 1) * P], P) for a in range(2) for g in range(4)]
                    if what == "sel":
                        return [(SLP[k][:, 4 * g:4 * g + 4, 0:HD], HD) for g in range(4)]
                    return [(WNP[k][:, :, 0:HD], HD)]

                pe.sem_inc(S["kv_free1"], 1)
                with pe.Fori(0, NB // 2) as i:
                    count = {"kt": 0, "s": 0, "pt": 0}

                    def key_T(k, what):
                        for src, r in key_groups(k, what):
                            g = count["kt"]
                            if g >= 2:
                                pe.wait_ge(S["kt_evA" if g % 2 == 0 else "kt_evD"], g // 2)
                            for j in range(4):
                                last = tr(bank(g % 2)[0:r, j * P:(j + 1) * P], src[:, j, :], ident)
                            last.then_inc(S["kt_T"], 1)
                            count["kt"] += 1

                    def keys_out(groups):
                        pe.wait_ge(S["kt_evA"], (groups + 1) // 2)
                        pe.wait_ge(S["kt_evD"], groups // 2)

                    def sample_scores(parts, keys):
                        for a in range(0, keys, 512):
                            n = min(512, keys - a)
                            if count["s"] >= 2:
                                pe.wait_ge(S["sc_ev"], count["s"] - 1)
                            for m, (q, kt, r) in enumerate(parts):
                                last = mm(bank(2 + count["s"] % 2)[0:32, 0:n], q[0:r, :], kt[0:r, a:a + n],
                                          start=m == 0, stop=m == len(parts) - 1)
                            last.then_inc(S["sc_mm"], 1)
                            count["s"] += 1

                    def mix(k, probs, pages_n, value, new_value, width, col, order):
                        pe.wait_ge(S["e_ready"], order)
                        if count["pt"] >= 1:
                            pe.wait_ge(S["ptn_ev"], count["pt"])
                        for j in range(pages_n):
                            tr(bank(4)[:, j * 32:(j + 1) * 32], probs[0:32, j * P:(j + 1) * P], ident[0:32, 0:32])
                        tr(bank(6)[0:NT, 0:32], probs[0:32, pages_n * P:pages_n * P + NT],
                           ident[0:32, 0:32]).then_inc(S["ptn_T"], 1)
                        count["pt"] += 1
                        pe.wait_ge(S["ptn_ev"], count["pt"])
                        if order > 1:
                            pe.wait_ge(S["ov_done"], order - 1)
                        for j in range(pages_n):
                            mm(bank(5)[0:32, col:col + width], PTF[:, j, :], value(j), start=j == 0, stop=False)
                        mm(bank(5)[0:32, col:col + width], PTF[0:NT, 16, :], new_value, start=False,
                           stop=True).then_inc(S["ov_mm"], 1)

                    for k in range(2):
                        pe.wait_ge(S[f"kv_in{k}"], 576 * i + 576)
                        key_T(k, "fox")
                        for a in range(2):
                            tr(bank(7)[:, a * NT:(a + 1) * NT], KNEW[k][0:NT, a * P:(a + 1) * P], ident[0:NT, 0:NT])
                        tr(bank(7)[0:HD, 16:24], KV4N[k][0:NT, 0, :], ident[0:NT, 0:NT])
                        tr(bank(7)[0:HD, 24:32], KV4N[k][0:NT, 2, :], ident[0:NT, 0:NT]).then_inc(S["new_T"], 1)
                        pe.wait_ge(S["new_ev"], k + 1)
                        pe.wait_ge(S["qb_ready"], k + 1)
                        key_T(k, "sel")
                        keys_out(13 * k + 8)
                        sample_scores([(QB[:, 0, :], KT2[:, 0, :], P), (QB[:, 1, :], KT2[:, 1, :], P)], LK)
                        key_T(k, "win")
                        keys_out(13 * k + 12)
                        sample_scores([(QNB, KSTs, HD)], LK)
                        keys_out(13 * k + 13)
                        sample_scores([(QNB, KWTs, HD)], WIN + NT)
                        mix(k, SF, NPG, lambda j: KVP[k][:, j, GW:2 * GW], VNEW[k][0:NT, :], GW, 0, 3 * k + 1)
                        mix(k, SSL, NPG, lambda j: SLP[k][:, j, HD:P], KV4N[k][0:NT, 1, :], HD, GW, 3 * k + 2)
                        mix(k, SW, 4, lambda j: WNP[k][:, j, HD:P], KV4N[k][0:NT, 3, :], HD, GW + HD, 3 * k + 3)
                        pe.drain().then_inc(S[f"kv_free{k}"], 1)
                    arrive2(pe, "pe")
                arrive(pe, "pe")
                if stop <= 6:
                    return

                pe.wait_ge(S["y_in"], 112)
                def channel_sums(n):
                    if n:
                        pe.wait_ge(S["y_sq"], n)
                    src = (YB, YQ, YQ)[n]
                    for c in range(2):
                        for a, wd in zip(STARTS, WIDTHS):
                            last = mm(PS[:, a:a + wd], ones, src[:, c, a:a + wd], start=c == 0, stop=c == 1)
                    last.then_inc(S["y_mm"], 1)

                pe.sem_inc(S["g_mm"], 2)
                channel_sums(0)

                def oa_T(t, k, m):
                    r = rows_of(t)
                    pe.wait_ge(S["oa_ready"], t + 1)
                    if not (isinstance(t, int) and t < 2):
                        pe.wait_ge(S["oa_ev"], t - 1)
                    for j in range(6):
                        at = (4 + 2 * k) * 512 + j * P if j < 2 else (5 + 2 * k) * 512 + (j - 2) * P
                        last = tr(PS[:, at:at + r], OA[k][0:r, j // 2, (j % 2) * P:(j % 2 + 1) * P], ident[0:r, 0:r])
                    last.then_inc(S["oa_T"], 1)

                over_tiles(pe, oa_T, between={0: lambda: channel_sums(1), 1: lambda: channel_sums(2)})
                arrive2(pe, "pe")
                with pe.Fori(0, KD // 2) as i:
                    for k in range(2):
                        n = 2 * i + k
                        pe.wait_ge(S["w_lo"], n + 3)
                        pe.wait_ge(S["g_ev"], n + 1)
                        gemm(k, KD, OTH, OTL, WH[k], WL[k]).then_inc(S["g_mm"], 1)
                arrive(pe, "pe")
                if stop <= 7:
                    return

                arrive(pe, "pe")
                for k in range(KD):
                    sum_squares(SQN2, k)
                arrive2(pe, "pe")
                with pe.Fori(0, 2) as half:
                    pe.sem_inc(S["g_mm"], 2)
                    with pe.Fori(0, 8) as i:
                        for k in range(2):
                            n = 2 * i + k
                            pe.wait_ge(S["w_lo"], n + 3)
                            pe.wait_ge(S["g_ev"], n + 1)
                            gemm(k, KD, XNH, XNL, WH[k], WL[k]).then_inc(S["g_mm"], 1)
                    pe.wait_ge(S["u_ready"], 18)
                    with pe.Fori(0, KD // 2) as i:
                        for k in range(2):
                            n = 2 * i + k
                            pe.wait_ge(S["w_lo"], 16 + n + 3)
                            pe.wait_ge(S["g_ev"], 16 + n + 1)
                            gemm(k, 16, UH, UL, WH[k], WL[k]).then_inc(S["g_mm"], 1)
                    arrive(pe, "pe")

            def row_out(t, k, m):
                r = rows_of(t)
                pe.wait_ge(S["row_cp"], t + 1)
                if not (isinstance(t, int) and t < 2):
                    pe.wait_ge(S["row_ev"], t - 1)
                for j in range(KD):
                    at = (2 * k + j // 4) * 512 + (j % 4) * P
                    last = tr(PS[0:r, at:at + P], XO[k][:, j, 0:r], ident)
                last.then_inc(S["row_T"], 1)

            over_tiles(pe, row_out)

        @block.scalar
        def _(act):
            run = nc.scalar.activation

            def rows_of(t):
                return NS if isinstance(t, int) and t == QT else P

            def cols(t):
                return bass.ds(t * P, rows_of(t)) if not isinstance(t, int) else slice(t * P, t * P + rows_of(t))

            def row_ev(t, k, m):
                r = rows_of(t)
                act.wait_ge(S["row_T"], t + 1)
                for g in range(2):
                    last = run(XT[:, 4 * g:4 * g + 4, cols(t)],
                               PS[:, (2 * k + g) * 512:(2 * k + g + 1) * 512].rearrange("p (j n) -> p j n", j=4)[:, :, 0:r],
                               ACT.Copy)
                last.then_inc(S["row_ev"], 1)

            over_tiles(act, row_ev)
            arrive(act, "act")

            def squares(dst):
                for k in range(KD):
                    if k >= 2:
                        act.wait_ge(S["sq_summed"], k - 1)
                    run(dst[:, k % 2, :], XT[:, k, :], ACT.Square).then_inc(S["sq_ready"], 1)

            def root(x, n):
                act.wait_ge(S["col_mean"], n)
                run(x, x, ACT.Sqrt).then_inc(S["col_rstd"], 1)

            def split_weights(k, blocks, n, pair):
                act.wait_ge(S[f"w_in{k}"], 16 * (pair + 1))
                act.wait_ge(S["g_mm"], n + 1)
                run(WH[k][:, 0:blocks, :], WF[k][:, 0:blocks, :], ACT.Copy).then_inc(S["w_hi"], 1)

            with act.Fori(0, layers) as l:
                def w(name):
                    return A[name][bass.ds(l, 1)]

                chain = Chain(act, S["act_done"])
                squares(SQ2)
                root(RST, 1)
                for f in range(2):
                    act.wait_ge(S["glu_in"], f + 1)
                    run(SG, SG, ACT.Sigmoid).then_inc(S["glu_sig"], 1)
                act.wait_ge(S["ct_T"], 1)
                n = NB // 2 * (CW - 1)
                for g in range(2):
                    for c in range(2):
                        at = 3072 + (2 * g + c) * n
                        last = run(GLS[:, c, 4 * g:4 * g + 4, 0:CW - 1],
                                   PS[:, at:at + n].rearrange("p (b r) -> p b r", r=CW - 1), ACT.Copy)
                last.then_inc(S["ct_ev"], 1)
                act.wait_ge(S["wm_T"], 1)
                run(WMT, PS[:, 3584:4096].rearrange("p (g n) -> p g n", g=4), ACT.Copy).then_inc(S["wm_ev"], 1)
                act.wait_ge(S["wm_T"], 2)
                run(WM8T[0:NS], PS[0:NS, 0:4 * NS].rearrange("p (g n) -> p g n", g=4), ACT.Copy).then_inc(S["wm_ev"], 1)
                act.wait_ge(S["glu_done"], 2)

                def xt(t, k):
                    r = rows_of(t)
                    if not (isinstance(t, int) and t < 2):
                        act.wait_ge(S["z_mm"], 5 * (t - 1))
                    run(RSK[k][0:r, :], RSC[0:r, bass.ds(t, 1)], ACT.Copy)
                    run(XTT[k][:, :, 0:r], XNT[:, :, cols(t)], ACT.Copy).then_inc(S["xt_ready"], 1)

                xt(0, 0)

                def z_out(t, k, m):
                    r = rows_of(t)
                    if not (isinstance(t, int) and t == QT):
                        xt(t + 1, 1 - k)
                    if not (isinstance(t, int) and t == 0):
                        act.wait_ge(S["z_free"], t)
                    if not (isinstance(t, int) and t < 2):
                        act.wait_ge(S[f"st{k}"], 176 * m)
                        act.wait_ge(S["fin"], t - 1)

                    def out(c, dst, width, func=ACT.Copy):
                        act.wait_ge(S["z_mm"], 5 * t + c + 1)
                        run(dst, PS[0:r, c * 512:c * 512 + width], func, scale=RSK[k][0:r, :]).then_inc(S["z_ev"], 1)

                    out(0, Z[0:r, 0:512], 512)
                    out(0, SQ[0:r, 0:512], 512, ACT.Square)
                    out(1, VB[k][0:r, :], 260)
                    out(2, Z[0:r, 512:896], 384)
                    out(2, SQ[0:r, 512:896], 384, ACT.Square)
                    out(3, Z[0:r, 896:1164], 268)
                    out(3, SQ[0:r, 896:1152], 256, ACT.Square)
                    out(4, UV[k][0:r, :], 512)
                    act.wait_ge(S["z_ev"], 8 * t + 8)
                    run(EX[0:r, 0:12], Z[0:r, 1152:1164], ACT.Exp, scale=-1.0).then_inc(S["ex_ready"], 1)
                    act.wait_ge(S["na_ready"], t + 1)
                    run(EX[0:r, 16:20], EX[0:r, 32:36], ACT.Exp).then_inc(S["ex_ready"], 1)

                over_tiles(act, z_out)
                act.wait_ge(S["tail_T"], 1)
                run(CPO[0:CW - 1, 0:GW], PS[0:CW - 1, 3584:3584 + GW], ACT.Copy)
                run(CPO[0:NS, GW:2 * GW], PS[0:NS, 3840:3840 + GW], ACT.Copy).then_inc(S["tail_ev"], 1)
                arrive(act, "act")
                if stop <= 2:
                    return

                def pages_in(k, i):
                    for j in range(4):
                        page = act.value_load(pages[:, bass.ds(i * NPG + (4 * k + j), 1)], min_val=0, max_val=POOL - 1)
                        act.dma_start(PG[k][:, j, :].rearrange("p (s d) -> p s d", s=2),
                                      A["cache_nsa_kv"][bass.ds(l, 1), bass.ds(page, 1), :, 0:2, :]
                                      .rearrange("o a p s d -> (o a p) s d")).then_inc(S[f"pg{k}"], 16)

                for k in (1, 3):
                    pages_in(k, 0)
                act.wait_ge(S["zero_ready"], 1)
                act.dma_start(PHI[0:HD, :, 0:HD], w("nsa_phi_k").rearrange("o (c d) e -> d (o c) e", d=HD)).then_inc(S["phi_in"], 16)
                act.dma_start(PHI[HD:P, :, HD:P], w("nsa_phi_v").rearrange("o (c d) e -> d (o c) e", d=HD)).then_inc(S["phi_in"], 16)
                act.sem_inc(S["pg_ev"], 1)
                act.wait_ge(S["kvc_mm"], 1)
                run(CT[:, NTOK:NTOK + BLK], bank(6, BLK), ACT.Copy).then_inc(S["pg_ev"], 1)
                act.wait_ge(S["kvc_mm"], 2)
                for g in range(2):
                    run(CT[:, NB * PAST + 512 * g:NB * PAST + 512 * (g + 1)], bank(4 + g), ACT.Copy).then_inc(S["pg_ev"], 1)
                def page_group(i, k):
                    act.wait_ge(S["pg_T"], 4 * i + k + 5)
                    run(CT[:, bass.ds((4 * i + k) * 512, 512)], bank(k), ACT.Copy).then_inc(S["pg_ev"], 1)

                with act.Fori(0, NB - 1) as i:
                    for k in range(4):
                        page_group(i, k)
                        if k % 2:
                            pages_in(k, i + 1)
                for k in range(4):
                    page_group(NB - 1, k)
                arrive(act, "act")
                if stop <= 3:
                    return

                for n, dst in enumerate((KST, KST, KWT, KWT)):
                    act.wait_ge(S["tr_T"], n + 1)
                    run(dst[0:HD, (n % 2) * 512:(n % 2 + 1) * 512], bank(4 + n % 2)[0:HD, :], ACT.Copy).then_inc(S["tr_ev"], 1)
                arrive(act, "act")
                units = [(kind, i) for i in reversed(range(QT)) for kind in ("sel", "fox", "win")]
                def head(k):
                    for n, (dst, r) in enumerate(((QNT, HD), (QNT, HD), (QFT, AUG), (QFT, AUG), (KFT, AUG), (KFT, AUG))):
                        act.wait_ge(S["tr_T"], n + 1)
                        run(dst[0:r, (n % 2) * 512:(n % 2 + 1) * 512], bank(4 + n % 2)[0:r, :], ACT.Copy).then_inc(S["tr_ev"], 1)
                    act.wait_ge(S["cs_ready"], 1)
                    run(SC, SC, ACT.Exp).then_inc(S["ce_ready"], 1)
                    widths = [P * (min(i, WIN // P) + 1 if kind == "win" else i + 1) for kind, i in units]
                    done = [0]
                    for width in widths:
                        done.append(done[-1] + -(-width // 512))

                    def probs(u):
                        act.wait_ge(S["nm_ready"], u + 1)
                        if u >= 2:
                            act.wait_ge(S["pt_T"], done[u - 1])
                        run(PR[u % 2][:, 0:widths[u]], PS[:, (u % 2) * 1024:(u % 2) * 1024 + widths[u]], ACT.Exp,
                            bias=NMX[:, u:u + 1], accum_out=RS[:, u:u + 1]).then_inc(S["p_ready"], 1)

                    def odd_groups(u):
                        for g in range(done[u], done[u + 1]):
                            if g % 2:
                                a = (g - done[u]) * 512
                                w4 = min(512, widths[u] - a)
                                if u >= 2:
                                    act.wait_ge(S["pv_mm"], u - 1)
                                act.wait_ge(S["pt_T"], g + 1)
                                run(PTR[u % 2][:, a:a + w4], bank(4 + g % 2, w4), ACT.Copy).then_inc(S["pt_evA"], 1)

                    probs(0)
                    for u in range(len(units)):
                        if u + 1 < len(units):
                            probs(u + 1)
                        if u == 0:
                            act.wait_ge(S["cpt_T"], 1)
                            run(PTC, bank(7)[:, 256:512].rearrange("p (g n) -> p g n", g=2), ACT.Copy).then_inc(S["cpt_ev"], 1)
                        odd_groups(u)
                    arrive(act, "act")

                with act.Fori(0, NH // 2) as _:
                    for k in range(2):
                        head(k)
                if stop <= 4:
                    return

                act.wait_ge(S["q_T"], 2)
                for g in range(2):
                    run(VCT[0:NCB, 4 * g:4 * g + 4, :], bank(2 + g)[0:NCB, :].rearrange("p (b n) -> p b n", b=4),
                        ACT.Copy).then_inc(S["vct_ev"], 1)
                act.wait_ge(S["mx_ready"], 1)
                run(PC, PC, ACT.Exp).then_inc(S["e_ready"], 1)
                act.wait_ge(S["imp_mm"], 1)
                run(PTCs[0:NCB], bank(6)[0:NCB, 0:2 * P].rearrange("p (g n) -> p g n", g=2), ACT.Copy).then_inc(S["vct_ev"], 1)
                act.wait_ge(S["rank_ready"], 1)
                act.dma_start(sel_s, RK[0:NS, :]).then_inc(S["rank_out"], 16)
                act.wait_ge(S["os_ready"], 1)
                for g in range(2):
                    act.dma_start(oc_s[4 * g:4 * g + 4].rearrange("b r d -> (b r) d"), OCS[:, g, :]).then_inc(S["rank_out"], 16)
                act.wait_ge(S["rank_out"], 48)
                act.dma_start(OCB[0:32], oc_s.rearrange("b r d -> r b d")).then_inc(S["aux_in"], 16)
                for h in range(NH):
                    r = slice(h * NT, (h + 1) * NT)
                    act.dma_start(SNB[r], sel_s.rearrange("(b t) j -> t b j", t=NT)).then_inc(S["aux_in"], 16)
                act.wait_ge(S["aux_in"], 16 * 13)
                arrive2(act, "act")
                if stop <= 5:
                    return

                with act.Fori(0, NB // 2) as i:
                    for k in range(2):
                        def keys_out(what):
                            first = 13 * k + {"fox": 0, "sel": 8, "win": 12}[what]
                            n = {"fox": 8, "sel": 4, "win": 1}[what]
                            for g in range(first, first + n):
                                if g % 2:
                                    continue
                                j = g - first
                                act.wait_ge(S["kt_T"], g + 1)
                                if what == "fox":
                                    dst, r = KT2[:, j // 4, (j % 4) * 512:(j % 4 + 1) * 512], P
                                elif what == "sel":
                                    dst, r = KSTs[0:HD, j * 512:(j + 1) * 512], HD
                                else:
                                    dst, r = KWTs[0:HD, 0:512], HD
                                run(dst, bank(g % 2)[0:r, :], ACT.Copy).then_inc(S["kt_evA"], 1)

                        def probs(n, s, width):
                            act.wait_ge(S["mx_ready"], 3 * k + n + 1)
                            run(s[0:32, 0:width], s[0:32, 0:width], ACT.Exp, bias=ST[0:32, n:n + 1],
                                accum_out=ST[0:32, 3 + n:4 + n]).then_inc(S["e_ready"], 1)

                        def probs_T(n, pages_n):
                            act.wait_ge(S["ptn_T"], 3 * k + n + 1)
                            run(PTF[:, 0:pages_n, :], bank(4)[:, 0:pages_n * 32].rearrange("p (j n) -> p j n", n=32), ACT.Copy)
                            run(PTF[0:NT, 16, :], bank(6)[0:NT, 0:32], ACT.Copy).then_inc(S["ptn_ev"], 1)

                        keys_out("fox")
                        keys_out("sel")
                        if k:
                            act.wait_ge(S["ov_done"], 3)
                        probs(0, SF, LK)
                        keys_out("win")
                        probs(1, SSL, LK)
                        probs_T(0, NPG)
                        probs(2, SW, WIN + NT)
                        probs_T(1, NPG)
                        probs_T(2, 4)
                        b = 2 * i + k
                        act.wait_ge(S["os_ready"], 2 * k + 2)
                        act.dma_start(of_s[bass.ds(b, 1), 0].rearrange("b r d -> (b r) d"), OH[k][0:32, :]).then_inc(S["os_out"], 16)
                        act.dma_start(of_s[bass.ds(b, 1), 1].rearrange("b r d -> (b r) d"), OCM[k][0:32, :]).then_inc(S["os_out"], 16)
                    arrive2(act, "act")
                arrive(act, "act")
                if stop <= 6:
                    return

                def gate():
                    act.wait_ge(S["y_c"], 1)
                    run(YQ, YB, ACT.Sigmoid).then_inc(S["y_c"], 1)

                def channels_high():
                    act.wait_ge(S["y_c"], 3)
                    run(OTH[:, 2:4, :], YQ, ACT.Copy).then_inc(S["y_c"], 1)

                chain.restart()

                def oa_squares(t, k, m):
                    r = rows_of(t)
                    if isinstance(t, int) and t == QT:
                        act.wait_ge(S[f"oa_in{k}"], 48 * m + 17 * 16)
                    else:
                        act.wait_ge(S[f"oa_in{k}"], 48 * m + 48)
                    if not (isinstance(t, int) and t < 2):
                        act.wait_ge(S["oa_ready"], t - 1)
                    for g in range(3):
                        run(OAQ[0:r, :], OA[k][0:r, g, :], ACT.Square, accum_out=S3[k][0:r, g:g + 1]).then_inc(S["act_done"], 1)
                        act.wait_ge(S["act_done"], chain.next())
                    act.sem_inc(S["ss_ready"], 1)

                oa_squares(0, 0, 0)

                def oa(t, k, m):
                    r = rows_of(t)
                    if not (isinstance(t, int) and t == QT):
                        oa_squares(t + 1, 1 - k, m if k == 0 else m + 1)
                    act.wait_ge(S["oa_T"], t + 1)
                    run(OTH[:, 0:2, cols(t)], PS[:, (4 + 2 * k) * 512:(4 + 2 * k) * 512 + 256]
                        .rearrange("p (j n) -> p j n", j=2)[:, :, 0:r], ACT.Copy)
                    run(OTH[:, 4:8, cols(t)], PS[:, (5 + 2 * k) * 512:(6 + 2 * k) * 512]
                        .rearrange("p (j n) -> p j n", j=4)[:, :, 0:r], ACT.Copy).then_inc(S["oa_hi"], 1)

                def first_weights():
                    for k in range(2):
                        split_weights(k, KD, k, 0)

                over_tiles(act, oa, chain, between={0: lambda: root(YM, 1), 1: gate, 5: lambda: root(YM, 2),
                                                    6: channels_high, 7: first_weights})
                arrive2(act, "act")
                with act.Fori(0, KD // 2 - 1) as i:
                    for k in range(2):
                        split_weights(k, KD, 2 * i + 2 + k, i + 1)
                arrive(act, "act")
                if stop <= 7:
                    return

                arrive(act, "act")
                for k in range(KD):
                    run(XNH[:, k, :], XT[:, k, :], ACT.Copy, scale=G2[:, k:k + 1]).then_inc(S["xh_ready"], 1)
                squares(SQN2)
                root(RST2, 1)
                arrive2(act, "act")
                with act.Fori(0, 2) as half:
                    chain.restart()

                    def up(n, k):
                        act.wait_ge(S["g_ev"], n + 3)
                        run(RL[k], RL[k], ACT.Square).then_inc(S["act_done"], 1)
                        act.wait_ge(S["act_done"], chain.next())
                        run(UH[:, bass.ds(n, 1), :].rearrange("p o n -> p (o n)"), RL[k], ACT.Copy).then_inc(S["u_hi"], 1)

                    split_weights(0, KD, 0, 0)
                    split_weights(1, KD, 1, 0)
                    with act.Fori(0, 7) as i:
                        chain.restart()
                        for k in range(2):
                            split_weights(k, KD, 2 * i + k + 2, i + 1)
                            up(2 * i + k, k)
                    chain.restart()
                    for k in range(2):
                        split_weights(k, 16, 16 + k, 8)
                        up(14 + k, k)
                    with act.Fori(0, 3) as i:
                        for k in range(2):
                            split_weights(k, 16, 18 + 2 * i + k, i + 9)
                    arrive(act, "act")

            def row_out(t, k, m):
                r = rows_of(t)
                act.wait_ge(S["row_T"], t + 1)
                if not (isinstance(t, int) and t < 2):
                    act.wait_ge(S[f"row_out{k}"], 16 * m)
                run(XS[k][0:r, 0:512], PS[0:r, 1024 * k:1024 * k + 512], ACT.Copy)
                run(XS[k][0:r, 512:1024], PS[0:r, 1024 * k + 512:1024 * k + 1024], ACT.Copy).then_inc(S["row_ev"], 1)

            over_tiles(act, row_out)

        @block.vector
        def _(dve):
            V = nc.vector

            def rows_of(t):
                return NS if isinstance(t, int) and t == QT else P

            def cols(t):
                return bass.ds(t * P, rows_of(t)) if not isinstance(t, int) else slice(t * P, t * P + rows_of(t))

            dve.wait_ge(loaded_once, 48)
            V.tensor_copy(identb, ident)
            V.tensor_copy(cnegb, C("cneg"))
            V.tensor_copy(wnegb, C("wneg"))
            arrive(dve, "dve")

            def rstd(out, sums, count, which, n):
                V.tensor_scalar(out, sums, 1.0 / count, EPS, ALU.mult, ALU.add).then_inc(S[f"{which}_mean"], 1)
                dve.wait_ge(S[f"{which}_rstd"], n)
                if which == "col":
                    V.reciprocal(out, out).then_inc(S["col_inv"], 1)
                    dve.wait_ge(S["col_inv"], n)

            def row_mean(rst):
                dve.wait_ge(S["sq_summed"], KD)
                for a, n, at in zip(STARTS, WIDTHS, SUMS_AT):
                    last = V.tensor_scalar(rst[:, a:a + n], PS[:, at:at + n], 1.0 / DM, EPS, ALU.mult, ALU.add)
                last.then_inc(S["col_mean"], 1)

            def row_inverse(rst):
                dve.wait_ge(S["col_rstd"], 1)
                V.reciprocal(rst, rst).then_inc(S["col_inv"], 1)
                dve.wait_ge(S["col_inv"], 1)

            def low_weights(k, blocks, n):
                dve.wait_ge(S["w_hi"], n + 1)
                V.tensor_tensor(WL[k][:, 0:blocks, :], WF[k][:, 0:blocks, :], WH[k][:, 0:blocks, :], ALU.subtract)\
                    .then_inc(S["w_lo"], 1)

            with dve.Fori(0, layers) as l:
                chain = Chain(dve, S["dve_done"])
                dve.wait_ge(S["g1_in"], 16)
                for k in range(KD):
                    V.tensor_scalar(XNT[:, k, :], XT[:, k, :], G1[:, k:k + 1], None, ALU.mult).then_inc(S["xn_ready"], 1)
                row_mean(RST)
                row_inverse(RST)
                for t in range(QT + 1):
                    r = P if t < QT else NS
                    V.tensor_tensor(GV[0:r, 0:r], RST[0:r, t * P:t * P + r], ident[0:r, 0:r], ALU.mult).then_inc(S["dve_done"], 1)
                    dve.wait_ge(S["dve_done"], chain.next())
                    V.reduce_sum(RSC[0:r, t:t + 1], GV[0:r, 0:r], AX).then_inc(S["dve_done"], 1)
                    dve.wait_ge(S["dve_done"], chain.next())
                V.memset(GL[:, :, 0:CW - 1], 0.0).then_inc(S["dve_done"], 1)
                dve.wait_ge(S["dve_done"], chain.next())
                for f in range(2):
                    dve.wait_ge(S["glu_mm"], f + 1)
                    V.tensor_tensor(SG, PS[:, 1536:1536 + ROWS], RST, ALU.mult).then_inc(S["glu_in"], 1)
                    V.tensor_tensor(GV, PS[:, 0:ROWS], RST, ALU.mult).then_inc(S["dve_done"], 1)
                    dve.wait_ge(S["dve_done"], chain.next())
                    dve.wait_ge(S["glu_sig"], f + 1)
                    V.tensor_tensor(GL[:, f, CW - 1:], GV[:, 0:SEQ], SG[:, 0:SEQ], ALU.mult)
                    V.tensor_tensor(GLS[:, f, :, CW - 1:], GV[:, SEQ:ROWS].rearrange("p (b t) -> p b t", b=NB),
                                    SG[:, SEQ:ROWS].rearrange("p (b t) -> p b t", b=NB), ALU.mult)
                    V.tensor_tensor(SGL[:, f, :], GV[:, SEQ:ROWS], SG[:, SEQ:ROWS], ALU.mult).then_inc(S["glu_done"], 1)
                dve.wait_ge(S["gains"], 384)
                dve.wait_ge(S["wm_in"], 1040)
                V.tensor_tensor(WMr, WMr, C("tril").unsqueeze(1).to_broadcast([P, 4, P]), ALU.mult).then_inc(S["wm_raw"], 1)
                V.tensor_tensor(WM8r[0:NS], WM8r[0:NS], C("btril", NS).unsqueeze(1).to_broadcast([NS, 4, NS]),
                                ALU.mult).then_inc(S["wm_raw"], 1)
                dve.wait_ge(S["glu_mm"], 2)
                dve.wait_ge(S["wm_T"], 2)
                for x in ZA:
                    V.memset(x[:, 0:NH, HD + 1:HD + 2], 1.0)
                    V.memset(x[:, NH:2 * NH, HD:HD + 1], 1.0)
                V.memset(GN10[:, 5:10:2, :], 1.0)
                V.memset(CARRY, 0.0)
                V.tensor_scalar(GQK[:, 0, :], GQK[:, 0, :], HD ** -0.5, None, ALU.mult)
                V.tensor_scalar(GN10[:, 0:NH, :], GN10[:, 0:NH, :], HD ** -0.5, None, ALU.mult).then_inc(S["dve_done"], 1)
                dve.wait_ge(S["dve_done"], chain.next())

                def norm_rows(t, k, m):
                    r = rows_of(t)
                    bf = lambda x, shape: x.to_broadcast(shape)
                    dve.wait_ge(S["z_ev"], 8 * t + 3)
                    if not (isinstance(t, int) and t < 2):
                        dve.wait_ge(S[f"st{k}"], 176 * m)
                    x, na, lf = EX[0:r, 36:40], EX[0:r, 32:36], LF[k][0:r, :]
                    V.tensor_tensor(x, VB[k][0:r, 256:260], BFB[0:r, :], ALU.add).then_inc(S["dve_done"], 1)
                    dve.wait_ge(S["dve_done"], chain.next())
                    V.tensor_scalar(na, x, -1.0, None, ALU.mult).then_inc(S["dve_done"], 1)
                    dve.wait_ge(S["dve_done"], chain.next())
                    V.tensor_tensor(na, x, na, ALU.min).then_inc(S["na_ready"], 1)
                    V.tensor_scalar(x, x, 0.0, None, ALU.min).then_inc(S["dve_done"], 1)
                    dve.wait_ge(S["dve_done"], chain.next())
                    dve.wait_ge(S["z_ev"], 8 * t + 7)
                    V.reduce_sum(SS18[0:r, 0:18], SQ[0:r, :].rearrange("p (g d) -> p g d", d=HD), AX)
                    dve.wait_ge(S["z_ev"], 8 * t + 8)
                    vd, vn = UV[k][0:r, GW:2 * GW], VN[k][0:r, :]
                    V.bn_stats(BN6[0:r, :], vd).then_inc(S["dve_done"], 1)
                    dve.wait_ge(S["dve_done"], chain.next())
                    V.bn_aggr(BN2[0:r, :], BN6[0:r, :]).then_inc(S["dve_done"], 1)
                    dve.wait_ge(S["dve_done"], chain.next())
                    V.tensor_scalar(SS18[0:r, 18:19], BN2[0:r, 1:2], float(HD), None, ALU.mult).then_inc(S["dve_done"], 1)
                    dve.wait_ge(S["dve_done"], chain.next())
                    rstd(SS18[0:r, :], SS18[0:r, :], HD, "row", t + 1)
                    za = ZA[k][0:r, :, 0:HD]
                    V.tensor_tensor(za, Z[0:r, 0:512].rearrange("p (g d) -> p g d", d=HD),
                                    bf(SS18[0:r, 0:8].unsqueeze(2), [r, 8, HD]), ALU.mult).then_inc(S["dve_done"], 1)
                    dve.wait_ge(S["dve_done"], chain.next())
                    t10 = T10[0:r, :].rearrange("p (g d) -> p g d", d=HD)
                    z10 = Z[0:r, 512:1152].rearrange("p (g d) -> p g d", d=HD)
                    for s in range(2):
                        zs = ZA[k][0:r, 4 * s:4 * s + 4, 0:HD]
                        V.tensor_tensor(zs, zs, bf(GQK[0:r, s, :].unsqueeze(1), [r, NH, HD]), ALU.mult)
                    V.tensor_tensor(t10, z10, bf(SS18[0:r, 8:18].unsqueeze(2), [r, 10, HD]), ALU.mult).then_inc(S["dve_done"], 1)
                    dve.wait_ge(S["dve_done"], chain.next())
                    V.tensor_tensor(t10, t10, GN10[0:r], ALU.mult).then_inc(S["dve_done"], 1)
                    dve.wait_ge(S["dve_done"], chain.next())
                    v4 = T10[0:r, :].rearrange("p (g s d) -> p g s d", s=2, d=32)
                    sn4 = SN[0:r, :].rearrange("p (g s d) -> p g s d", s=2, d=32)
                    ca4 = SQ[0:r, 0:640].rearrange("p (g s d) -> p g s d", s=2, d=32)
                    rn4 = RN[k][0:r].rearrange("p g (s d) -> p g s d", s=2)
                    cos, sin = (bf(C(n, r)[:, bass.ds(t * 32, 32)].unsqueeze(1), [r, 10, 32]) for n in ("cos", "sin"))
                    for s in range(2):
                        V.tensor_tensor(ca4[:, :, s, :], v4[:, :, s, :], cos, ALU.mult)
                        V.tensor_tensor(sn4[:, :, s, :], v4[:, :, 1 - s, :], sin, ALU.mult).then_inc(S["dve_done"], 1)
                        dve.wait_ge(S["dve_done"], chain.next())
                    V.tensor_tensor(rn4[:, :, 0, :], ca4[:, :, 0, :], sn4[:, :, 0, :], ALU.subtract)
                    V.tensor_tensor(rn4[:, :, 1, :], ca4[:, :, 1, :], sn4[:, :, 1, :], ALU.add).then_inc(S["dve_done"], 1)
                    dve.wait_ge(S["dve_done"], chain.next())
                    V.tensor_copy(RN[k][0:r, 5:10:2, :], z10[:, 5:10:2, :]).then_inc(S["dve_done"], 1)
                    dve.wait_ge(S["dve_done"], chain.next())
                    dve.wait_ge(S["ex_ready"], 2 * t + 1)
                    V.tensor_scalar(EX[0:r, 0:12], EX[0:r, 0:12], 1.0, None, ALU.add).then_inc(S["dve_done"], 1)
                    dve.wait_ge(S["dve_done"], chain.next())
                    V.reciprocal(G12[k][0:r, :], EX[0:r, 0:12]).then_inc(S["dve_done"], 1)
                    dve.wait_ge(S["dve_done"], chain.next())
                    dve.wait_ge(S["ex_ready"], 2 * t + 2)
                    e, s1, s2, q = EX[0:r, 16:20], EX[0:r, 40:44], EX[0:r, 44:48], EX[0:r, 48:52]
                    V.tensor_scalar(s1, e, 2.0, None, ALU.add).then_inc(S["dve_done"], 1)
                    dve.wait_ge(S["dve_done"], chain.next())
                    V.reciprocal(s1, s1).then_inc(S["dve_done"], 1)
                    dve.wait_ge(S["dve_done"], chain.next())
                    V.tensor_tensor(s1, s1, e, ALU.mult).then_inc(S["dve_done"], 1)
                    dve.wait_ge(S["dve_done"], chain.next())
                    V.tensor_tensor(s2, s1, s1, ALU.mult).then_inc(S["dve_done"], 1)
                    dve.wait_ge(S["dve_done"], chain.next())
                    V.tensor_scalar(q, s2, 1.0 / 15, None, ALU.mult).then_inc(S["dve_done"], 1)
                    dve.wait_ge(S["dve_done"], chain.next())
                    for n in (13, 11, 9, 7, 5, 3):
                        V.scalar_tensor_tensor(q, q, 1.0 / n, s2, ALU.add, ALU.mult).then_inc(S["dve_done"], 1)
                        dve.wait_ge(S["dve_done"], chain.next())
                    V.scalar_tensor_tensor(q, q, 1.0, s1, ALU.add, ALU.mult).then_inc(S["dve_done"], 1)
                    dve.wait_ge(S["dve_done"], chain.next())
                    V.scalar_tensor_tensor(lf, q, -2.0, x, ALU.mult, ALU.add).then_inc(S["dve_done"], 1)
                    dve.wait_ge(S["dve_done"], chain.next())
                    dve.sem_inc(S["z_free"], 1)
                    V.tensor_scalar(vn, vd, BN2[0:r, 0:1], SS18[0:r, 18:19], ALU.subtract, ALU.mult).then_inc(S["dve_done"], 1)
                    dve.wait_ge(S["dve_done"], chain.next())
                    V.tensor_tensor(vn, vn, LNG[0:r, 0, :], ALU.mult).then_inc(S["dve_done"], 1)
                    dve.wait_ge(S["dve_done"], chain.next())
                    V.tensor_tensor(vn, vn, LNG[0:r, 1, :], ALU.add).then_inc(S["lf_ready"], 1)

                def finish(t, k):
                    r = rows_of(t)
                    dve.wait_ge(S["small_mm"], t + 1)
                    fq, fk = ZA[k][0:r, 0:NH, HD], ZA[k][0:r, NH:2 * NH, HD + 1]
                    sums = PS[0:r, 2560:2564]
                    if r == P:
                        V.tensor_tensor(fq, sums, CARRY, ALU.add).then_inc(S["dve_done"], 1)
                        dve.wait_ge(S["dve_done"], chain.next())
                        V.tensor_tensor(CARRY, PS[0:r, 2564:2568], CARRY, ALU.add)
                    else:
                        V.tensor_copy(fq, sums).then_inc(S["dve_done"], 1)
                        dve.wait_ge(S["dve_done"], chain.next())
                    V.tensor_scalar(fk, fq, -1.0, None, ALU.mult)
                    od = OD[k][0:r, :]
                    bs = BS if r == P else BS8
                    V.tensor_tensor(od.rearrange("p (g d) -> p g d", d=HD),
                                    PS[0:r, 3072:3072 + GW].rearrange("p (g d) -> p g d", d=HD),
                                    bs[0:r, :].unsqueeze(2).to_broadcast([r, 4, HD]), ALU.add).then_inc(S["dve_done"], 1)
                    dve.wait_ge(S["dve_done"], chain.next())
                    V.tensor_tensor(od, od, UV[k][0:r, 0:GW], ALU.mult).then_inc(S["fin"], 1)

                def z_step(t, k, m):
                    norm_rows(t, k, m)
                    if not (isinstance(t, int) and t == 0):
                        finish(t - 1, 1 - k)

                over_tiles(dve, z_step, chain)
                finish(8, 0)
                chain.restart()
                dve.wait_ge(S["ct_ev"], 1)
                arrive(dve, "dve")
                if stop <= 2:
                    return

                chain.restart()
                V.memset(PHI, 0.0).then_inc(S["zero_ready"], 1)
                dve.wait_ge(S["lfp_ready"], 1)
                for h in range(NH):
                    last = V.tensor_tensor_scan(PFX[:, h, :], ones, LFP[:, :, h], 0.0, ALU.mult, ALU.add)
                last.then_inc(S["dve_done"], 1)
                dve.wait_ge(S["dve_done"], chain.next())
                V.tensor_copy(TOT, PFX[:, :, PAGE - 1]).then_inc(S["tot_ready"], 1)
                chain.restart()
                V.memset(Yc, 0.0).then_inc(S["dve_done"], 1)
                dve.wait_ge(S["dve_done"], chain.next())
                for c in range(2):
                    last = V.tensor_scalar(Yc[:, c, :], Yc[:, c, :], CB[:, c:c + 1], None, ALU.add)
                last.then_inc(S["dve_done"], 1)
                dve.wait_ge(S["dve_done"], chain.next())
                with dve.Fori(0, CW) as j:
                    chain.restart()
                    tap = bass.ds(j, 1)
                    for c in range(2):
                        for y, x in ((Yc[:, c, 0:SEQ], GL[:, c, bass.ds(j, SEQ)]),
                                     (Yc[:, c, SEQ:].rearrange("p (b t) -> p b t", b=NB), GLS[:, c, :, bass.ds(j, NT)])):
                            last = V.scalar_tensor_tensor(y, x, CWT[:, c, tap], y, ALU.mult, ALU.add)
                    last.then_inc(S["dve_done"], 1)
                    dve.wait_ge(S["dve_done"], chain.next())
                dve.sem_inc(S["y_done"], 1)
                chain.restart()
                dve.wait_ge(S["lat_mm"], 1)
                V.tensor_tensor(LAT, bank(7, 4), TOT, ALU.add).then_inc(S["dve_done"], 1)
                dve.wait_ge(S["dve_done"], chain.next())
                for h in range(NH):
                    last = V.tensor_scalar(PFX[:, h, :], PFX[:, h, :], -1.0, LAT[:, h:h + 1], ALU.mult, ALU.add)
                last.then_inc(S["suf_ready"], 1)
                chain.restart()
                dve.wait_ge(S["kvc_mm"], 3)
                V.tensor_copy(TOT[:, 0:1], bank(1)[:, 272:273]).then_inc(S["dve_done"], 1)
                dve.wait_ge(S["dve_done"], chain.next())
                V.tensor_scalar(KVC[:, 0:272], bank(0, 272), TOT[:, 0:1], None, ALU.add)
                V.tensor_scalar(KVC[:, 272:544], bank(1, 272), TOT[:, 0:1], None, ALU.add).then_inc(S["kvc_ready"], 1)
                arrive(dve, "dve")
                if stop <= 3:
                    return

                chain.restart()
                V.tensor_copy(VREP[HD:P],
                              KVC[HD:P, 512:544].unsqueeze(1).to_broadcast([HD, 4, NPB])).then_inc(S["vb_ready"], 1)
                V.memset(VBD, 0.0).then_inc(S["dve_done"], 1)
                dve.wait_ge(S["dve_done"], chain.next())
                dve.wait_ge(S["vb_ready"], 2)
                for i in range(4):
                    V.tensor_copy(VBD[i * NPB:(i + 1) * NPB, i, :], bank(7)[i * NPB:(i + 1) * NPB, 0:HD])
                arrive(dve, "dve")

                units = [(kind, i) for i in reversed(range(QT)) for kind in ("sel", "fox", "win")]

                def blocks_of(u):
                    kind, i = units[u]
                    return min(i, WIN // P) + 1 if kind == "win" else i + 1

                def head(k):
                    chain.restart()
                    dve.wait_ge(S["cs_mm"], 1)
                    scf = SC.rearrange("p t n -> p (t n)")
                    V.tensor_tensor(scf, bank(7, 256), C("cmpneg"), ALU.add).then_inc(S["dve_done"], 1)
                    dve.wait_ge(S["dve_done"], chain.next())
                    V.reduce_max(SC8, SC, AX).then_inc(S["dve_done"], 1)
                    dve.wait_ge(S["dve_done"], chain.next())
                    V.tensor_tensor(SC, SC, SC8.unsqueeze(2).to_broadcast([P, QT, NPB]), ALU.subtract).then_inc(S["cs_ready"], 1)

                    def row_max(u):
                        dve.wait_ge(S["s_mm"], u + 1)
                        V.reduce_max(NMX[:, u:u + 1], PS[:, (u % 2) * 1024:(u % 2) * 1024 + blocks_of(u) * P], AX,
                                     negate=True).then_inc(S["nm_ready"], 1)

                    row_max(0)
                    row_max(1)
                    dve.wait_ge(S["ce_ready"], 1)
                    V.tensor_tensor(scf, scf, C("cmp01"), ALU.mult).then_inc(S["dve_done"], 1)
                    dve.wait_ge(S["dve_done"], chain.next())
                    V.reduce_sum(SC8, SC, AX).then_inc(S["dve_done"], 1)
                    dve.wait_ge(S["dve_done"], chain.next())
                    V.tensor_scalar(SC8, SC8, 1e-30, None, ALU.max).then_inc(S["dve_done"], 1)
                    dve.wait_ge(S["dve_done"], chain.next())
                    V.reciprocal(SC8, SC8).then_inc(S["dve_done"], 1)
                    dve.wait_ge(S["dve_done"], chain.next())
                    V.tensor_tensor(SC, SC, SC8.unsqueeze(2).to_broadcast([P, QT, NPB]), ALU.mult).then_inc(S["cp_ready"], 1)

                    dve.wait_ge(S["cpv_mm"], 1)
                    V.tensor_tensor(ON[k], bank(7).rearrange("p (t d) -> p t d", d=HD),
                                    GH[k][:, :, 0].unsqueeze(2).to_broadcast([P, QT, HD]), ALU.mult).then_inc(S["on_ready"], 1)
                    dve.wait_ge(S["on_ready"], 1)

                    def output(u):
                        kind, i = units[u]
                        dve.wait_ge(S["pv_mm"], u + 1)
                        ri = RI[:, u:u + 1]
                        V.tensor_scalar(ri, RS[:, u:u + 1], 1e-30, None, ALU.max).then_inc(S["dve_done"], 1)
                        dve.wait_ge(S["dve_done"], chain.next())
                        V.reciprocal(ri, ri).then_inc(S["dve_done"], 1)
                        dve.wait_ge(S["dve_done"], chain.next())
                        o = bank(6 + u % 2, HD)
                        if kind == "fox":
                            V.tensor_scalar(OF[k][:, i, :], o, ri, None, ALU.mult).then_inc(S["o_done"], 1)
                        else:
                            V.tensor_tensor(ri, ri, GH[k][:, i, 1 if kind == "sel" else 2].unsqueeze(1), ALU.mult).then_inc(S["dve_done"], 1)
                            dve.wait_ge(S["dve_done"], chain.next())
                            V.scalar_tensor_tensor(ON[k][:, i, :], o, ri, ON[k][:, i, :], ALU.mult, ALU.add).then_inc(S["o_done"], 1)

                    groups = 0
                    for u in range(len(units)):
                        n = blocks_of(u)
                        if u + 2 < len(units):
                            row_max(u + 2)
                        for a in range(0, n, 4):
                            if groups % 2 == 0:
                                w4 = min(4, n - a) * P
                                if u >= 2:
                                    dve.wait_ge(S["pv_mm"], u - 1)
                                dve.wait_ge(S["pt_T"], groups + 1)
                                V.tensor_copy(PTR[u % 2][:, a * P:a * P + w4], bank(4 + groups % 2, w4)).then_inc(S["pt_evD"], 1)
                            groups += 1
                        if u >= 2:
                            output(u - 2)
                    output(len(units) - 2)
                    output(len(units) - 1)
                    dve.wait_ge(S["o_done"], len(units))
                    dve.sem_inc(S["o_ready"], 1)
                    arrive(dve, "dve")

                with dve.Fori(0, NH // 2) as _:
                    for k in range(2):
                        head(k)
                if stop <= 4:
                    return

                chain.restart()
                V.memset(QALL, 0.0)
                V.memset(WMASK[0:32, :], 0.0).then_inc(S["dve_done"], 1)
                dve.wait_ge(S["dve_done"], chain.next())
                V.tensor_copy(WMASK[0:32, 0:NT], C("winneg", 32))
                V.tensor_copy(WMASK[0:32, WIN:], C("newneg", 32))
                dve.wait_ge(S["q_T"], 1)
                for h in range(NH):
                    r = slice((h % 2) * HD, (h % 2 + 1) * HD)
                    V.tensor_copy(QALL[r, h // 2, :, h * NT:(h + 1) * NT],
                                  bank(0)[r, (h // 2) * NS:(h // 2 + 1) * NS].rearrange("p (b t) -> p b t", b=NB))
                    last = V.tensor_copy(QNALL[0:HD, :, h * NT:(h + 1) * NT],
                                         bank(1)[0:HD, h * NS:(h + 1) * NS].rearrange("p (b t) -> p b t", b=NB))
                last.then_inc(S["q_ev"], 1)
                dve.wait_ge(S["sc_mm"], 1)
                s4 = bank(4, 2 * NCB).rearrange("p (g n) -> p g n", g=2)
                V.reduce_max(PC4[:, 0:2], s4, AX).then_inc(S["dve_done"], 1)
                dve.wait_ge(S["dve_done"], chain.next())
                V.tensor_tensor(PC, s4, PC4[:, 0:2].unsqueeze(2).to_broadcast([P, 2, NCB]), ALU.subtract).then_inc(S["mx_ready"], 1)
                dve.wait_ge(S["e_ready"], 1)
                V.reduce_sum(PC4[:, 2:4], PC, AX).then_inc(S["dve_done"], 1)
                dve.wait_ge(S["dve_done"], chain.next())
                V.tensor_scalar(PC4[:, 2:4], PC4[:, 2:4], 1e-30, None, ALU.max).then_inc(S["dve_done"], 1)
                dve.wait_ge(S["dve_done"], chain.next())
                V.reciprocal(PC4[:, 2:4], PC4[:, 2:4]).then_inc(S["dve_done"], 1)
                dve.wait_ge(S["dve_done"], chain.next())
                V.tensor_tensor(PC, PC, PC4[:, 2:4].unsqueeze(2).to_broadcast([P, 2, NCB]), ALU.mult).then_inc(S["sm_ready"], 1)
                dve.wait_ge(S["imp_mm"], 1)
                imp = IMP[0:NS, :]
                V.reduce_sum(imp[:, 0:NSB - 1], bank(5)[0:NS, 0:NCB].rearrange("p (j s) -> p j s", s=2), AX).then_inc(S["dve_done"], 1)
                dve.wait_ge(S["dve_done"], chain.next())
                V.memset(imp[:, 0:1], 1e4)
                V.memset(imp[:, NSB - 2:NSB], 1e4).then_inc(S["dve_done"], 1)
                dve.wait_ge(S["dve_done"], chain.next())
                full = [NS, NSB, NSB]
                V.tensor_tensor(GT[0:NS], imp.unsqueeze(1).to_broadcast(full), imp.unsqueeze(2).to_broadcast(full), ALU.is_gt)
                V.tensor_tensor(EQ[0:NS], imp.unsqueeze(1).to_broadcast(full), imp.unsqueeze(2).to_broadcast(full),
                                ALU.is_equal).then_inc(S["dve_done"], 1)
                dve.wait_ge(S["dve_done"], chain.next())
                V.tensor_tensor(EQ[0:NS], EQ[0:NS], C("before", NS).rearrange("p (j i) -> p j i", j=NSB), ALU.mult).then_inc(S["dve_done"], 1)
                dve.wait_ge(S["dve_done"], chain.next())
                V.tensor_tensor(GT[0:NS], GT[0:NS], EQ[0:NS], ALU.add).then_inc(S["dve_done"], 1)
                dve.wait_ge(S["dve_done"], chain.next())
                V.reduce_sum(RK[0:NS, :], GT[0:NS], AX).then_inc(S["dve_done"], 1)
                dve.wait_ge(S["dve_done"], chain.next())
                V.tensor_scalar(RK[0:NS, :], RK[0:NS, :], NSEL - 0.5, NEG, ALU.is_gt, ALU.mult).then_inc(S["rank_ready"], 1)
                dve.wait_ge(S["imp_mm"], 2)
                V.tensor_copy(OCS, bank(7, 2 * HD).rearrange("p (g d) -> p g d", g=2)).then_inc(S["os_ready"], 1)
                arrive2(dve, "dve")
                if stop <= 5:
                    return

                with dve.Fori(0, NB // 2) as i:
                    chain.restart()
                    for k in range(2):
                        b = 2 * i + k
                        bb = bass.ds(b, 1)
                        def keys_out(what):
                            first = 13 * k + {"fox": 0, "sel": 8, "win": 12}[what]
                            n = {"fox": 8, "sel": 4, "win": 1}[what]
                            for g in range(first, first + n):
                                if g % 2 == 0:
                                    continue
                                j = g - first
                                dve.wait_ge(S["kt_T"], g + 1)
                                if what == "fox":
                                    dst, r = KT2[:, j // 4, (j % 4) * 512:(j % 4 + 1) * 512], P
                                elif what == "sel":
                                    dst, r = KSTs[0:HD, j * 512:(j + 1) * 512], HD
                                else:
                                    dst, r = KWTs[0:HD, 0:512], HD
                                V.tensor_copy(dst, bank(g % 2)[0:r, :]).then_inc(S["kt_evD"], 1)

                        def scores_out(n, dst, keys, mask):
                            c0 = chunk_of[n]
                            parts = list(range(0, keys, 512))
                            if k:
                                dve.wait_ge(S["ptn_T"], n + 1)
                            for m, a in enumerate(parts):
                                wd = min(512, keys - a)
                                dve.wait_ge(S["sc_mm"], c0 + m + 1)
                                out, src = dst[0:32, a:a + wd], bank(2 + (c0 + m) % 2)[0:32, 0:wd]
                                in1 = mask(a, wd)
                                if len(in1.shape) == 3:
                                    out = out.rearrange("p (j n) -> p j n", n=SEL)
                                    src = src.rearrange("p (j n) -> p j n", n=SEL)
                                V.tensor_tensor_reduce(out=out, in0=src, in1=in1, scale=1.0, scalar=-3e38, op0=ALU.add,
                                                       op1=ALU.max, accum_out=MX8[0:32, m:m + 1]).then_inc(S["sc_ev"], 1)
                            dve.wait_ge(S["sc_ev"], c0 + len(parts))
                            if k:
                                dve.wait_ge(S["e_ready"], n + 1)
                            V.reduce_max(ST[0:32, n:n + 1], MX8[0:32, 0:len(parts)], AX, negate=True).then_inc(S["mx_ready"], 1)
                            dve.wait_ge(S["mx_ready"], 3 * k + n + 1)

                        chunk_of = [12 * k, 12 * k + 5, 12 * k + 10]

                        def block_mask(a, wd):
                            if a == PAST:
                                return C("newneg", 32)
                            return SNB1[k][0:32, a // SEL:a // SEL + 8].unsqueeze(2)\
                                .to_broadcast([32, 8, SEL])

                        keys_out("fox")
                        dve.wait_ge(S["new_T"], k + 1)
                        V.tensor_copy(KT2[:, :, PAST:LK], bank(7, 2 * NT).rearrange("p (a n) -> p a n", a=2))
                        V.tensor_copy(KSTs[0:HD, PAST:LK], bank(7)[0:HD, 16:24])
                        V.tensor_copy(KWTs[0:HD, WIN:], bank(7)[0:HD, 24:32]).then_inc(S["new_ev"], 1)
                        keys_out("sel")
                        dve.wait_ge(S["bias_ready"], k + 1)
                        scores_out(0, SF, LK, lambda a, wd: BIAS[0:32, a:a + wd])
                        dve.sem_inc(S["bias_free"], 1)
                        keys_out("win")
                        scores_out(1, SSL, LK, block_mask)
                        scores_out(2, SW, WIN + NT, lambda a, wd: WMASK[0:32, a:a + wd])
                        ri = ST[0:32, 6:7]

                        def inverse_sum(n):
                            V.tensor_scalar(ri, ST[0:32, 3 + n:4 + n], 1e-30, None, ALU.max).then_inc(S["dve_done"], 1)
                            dve.wait_ge(S["dve_done"], chain.next())
                            V.reciprocal(ri, ri).then_inc(S["dve_done"], 1)
                            dve.wait_ge(S["dve_done"], chain.next())

                        dve.wait_ge(S["ov_mm"], 3 * k + 1)
                        inverse_sum(0)
                        oo = OO[0:32, :].rearrange("p (h d) -> p h d", h=NH)
                        V.tensor_tensor(oo, bank(5)[0:32, 0:GW].rearrange("p (h d) -> p h d", h=NH),
                                        C("hmask", 32).unsqueeze(2).to_broadcast([32, NH, HD]), ALU.mult).then_inc(S["ov_done"], 1)
                        dve.wait_ge(S["ov_done"], 3 * k + 1)
                        V.reduce_sum(OH[k][0:32, :], oo.rearrange("p h d -> p d h"), AX).then_inc(S["dve_done"], 1)
                        dve.wait_ge(S["dve_done"], chain.next())
                        V.tensor_scalar(OH[k][0:32, :], OH[k][0:32, :], ri, None, ALU.mult).then_inc(S["os_ready"], 1)
                        dve.wait_ge(S["os_ready"], 2 * k + 1)
                        oc = OCM[k][0:32, :]
                        gate = lambda c: GB[0:32, bb, c:c + 1].rearrange("p o c -> p (o c)")
                        V.tensor_scalar(oc, OCB[0:32, bb, :].rearrange("p o d -> p (o d)"), gate(0), None, ALU.mult).then_inc(S["dve_done"], 1)
                        dve.wait_ge(S["dve_done"], chain.next())
                        for n in (1, 2):
                            dve.wait_ge(S["ov_mm"], 3 * k + n + 1)
                            inverse_sum(n)
                            V.tensor_tensor(ri, ri, gate(n), ALU.mult).then_inc(S["dve_done"], 1)
                            dve.wait_ge(S["dve_done"], chain.next())
                            o = bank(5)[0:32, GW + (n - 1) * HD:GW + n * HD]
                            V.scalar_tensor_tensor(oc, o, ri, oc, ALU.mult, ALU.add).then_inc(S["ov_done"], 1)
                            dve.wait_ge(S["ov_done"], 3 * k + n + 1)
                        dve.sem_inc(S["os_ready"], 1)
                    arrive2(dve, "dve")
                arrive(dve, "dve")
                if stop <= 6:
                    return

                chain.restart()
                both = [P, 2, ROWS]
                dve.sem_inc(S["w_lo"], 2)
                dve.wait_ge(S["y_in"], 112)

                def centred():
                    dve.wait_ge(S["y_mm"], 1)
                    V.tensor_scalar(YM, PS[:, 0:ROWS], 1.0 / GW, None, ALU.mult).then_inc(S["dve_done"], 1)
                    dve.wait_ge(S["dve_done"], chain.next())
                    V.tensor_tensor(YB, YB, YM.unsqueeze(1).to_broadcast(both), ALU.subtract).then_inc(S["dve_done"], 1)
                    dve.wait_ge(S["dve_done"], chain.next())
                    V.tensor_tensor(YQ, YB, YB, ALU.mult).then_inc(S["y_sq"], 1)

                def mean_square(n):
                    dve.wait_ge(S["y_mm"], n + 1)
                    V.tensor_scalar(YM, PS[:, 0:ROWS], 1.0 / GW, EPS, ALU.mult, ALU.add).then_inc(S["col_mean"], 1)

                def inverse_root(n):
                    dve.wait_ge(S["col_rstd"], n)
                    V.reciprocal(YM, YM).then_inc(S["col_inv"], 1)
                    dve.wait_ge(S["col_inv"], n)

                def layer_norm():
                    inverse_root(1)
                    V.tensor_tensor(YB, YB, YM.unsqueeze(1).to_broadcast(both), ALU.mult).then_inc(S["dve_done"], 1)
                    dve.wait_ge(S["dve_done"], chain.next())
                    for c in range(2):
                        last = V.tensor_scalar(YB[:, c, :], YB[:, c, :], CLG[:, c:c + 1], CLB[:, c:c + 1], ALU.mult, ALU.add)
                    last.then_inc(S["y_c"], 1)

                def silu():
                    dve.wait_ge(S["y_c"], 2)
                    V.tensor_tensor(YB, YB, YQ, ALU.mult).then_inc(S["dve_done"], 1)
                    dve.wait_ge(S["dve_done"], chain.next())
                    V.tensor_tensor(YQ, YB, YB, ALU.mult).then_inc(S["y_sq"], 1)

                def channels_norm():
                    inverse_root(2)
                    for c in range(2):
                        last = V.scalar_tensor_tensor(YQ[:, c, :], YB[:, c, :], GCB[:, c:c + 1], YM, ALU.mult, ALU.mult)
                    last.then_inc(S["y_c"], 1)

                def channels_low():
                    dve.wait_ge(S["y_c"], 4)
                    V.tensor_tensor(OTL[:, 2:4, :], YQ, OTH[:, 2:4, :], ALU.subtract)

                centred()

                def group_norm(t, k):
                    r = rows_of(t)
                    dve.wait_ge(S["ss_ready"], t + 1)
                    rstd(S3[k][0:r, :], S3[k][0:r, :], GW, "row", t + 1)
                    V.tensor_tensor(OA[k][0:r], OA[k][0:r], S3[k][0:r, :].unsqueeze(2).to_broadcast([r, 3, GW]), ALU.mult).then_inc(S["dve_done"], 1)
                    dve.wait_ge(S["dve_done"], chain.next())
                    V.tensor_tensor(OA[k][0:r], OA[k][0:r], GNB[0:r], ALU.mult).then_inc(S["oa_ready"], 1)

                group_norm(0, 0)

                def oa(t, k, m):
                    r = rows_of(t)
                    if not (isinstance(t, int) and t == QT):
                        group_norm(t + 1, 1 - k)
                    dve.wait_ge(S["oa_hi"], t + 1)
                    V.tensor_tensor(OTL[:, 0:2, cols(t)], PS[:, (4 + 2 * k) * 512:(4 + 2 * k) * 512 + 256]
                                    .rearrange("p (j n) -> p j n", j=2)[:, :, 0:r], OTH[:, 0:2, cols(t)], ALU.subtract)
                    V.tensor_tensor(OTL[:, 4:8, cols(t)], PS[:, (5 + 2 * k) * 512:(6 + 2 * k) * 512]
                                    .rearrange("p (j n) -> p j n", j=4)[:, :, 0:r], OTH[:, 4:8, cols(t)],
                                    ALU.subtract).then_inc(S["oa_ev"], 1)

                over_tiles(dve, oa, chain, between={0: lambda: mean_square(1), 1: lambda: (layer_norm(), silu()),
                                                    5: lambda: mean_square(2), 6: channels_norm, 7: channels_low,
                                                    8: lambda: [low_weights(k, KD, k) for k in range(2)]})
                arrive2(dve, "dve")

                def residual(n, k, before):
                    dve.wait_ge(S["g_mm"], before + n + 3)
                    x = XT[:, bass.ds(n, 1), :].rearrange("p o n -> p (o n)")
                    V.tensor_tensor(x, PS[:, 1536 * k:1536 * k + ROWS], x, ALU.add).then_inc(S["g_ev"], 1)

                def residuals(blocks, before):
                    with dve.Fori(0, KD // 2 - 1) as i:
                        for k in range(2):
                            residual(2 * i + k, k, before)
                            low_weights(k, blocks, before + 2 * i + k + 2)
                    for k in range(2):
                        residual(KD - 2 + k, k, before)

                dve.sem_inc(S["g_ev"], 2)
                residuals(KD, 0)
                arrive(dve, "dve")
                if stop <= 7:
                    return

                arrive(dve, "dve")
                chain.restart()
                for k in range(KD):
                    dve.wait_ge(S["xh_ready"], k + 1)
                    V.scalar_tensor_tensor(XNL[:, k, :], XT[:, k, :], G2[:, k:k + 1], XNH[:, k, :], ALU.mult, ALU.subtract)
                row_mean(RST2)
                arrive2(dve, "dve")
                for half in range(2):
                    dve.sem_inc(S["w_lo"], 2)
                    dve.sem_inc(S["g_ev"], 2)
                    dve.sem_inc(S["u_ready"], 2)

                    def positive(n, k):
                        dve.wait_ge(S["g_mm"], n + 3)
                        V.scalar_tensor_tensor(RL[k], PS[:, 1536 * k:1536 * k + ROWS], 0.0, RST2, ALU.max, ALU.mult)\
                            .then_inc(S["g_ev"], 1)

                    def low_up(n, k):
                        dve.wait_ge(S["u_hi"], n + 1)
                        V.tensor_tensor(UL[:, bass.ds(n, 1), :].rearrange("p o n -> p (o n)"), RL[k],
                                        UH[:, bass.ds(n, 1), :].rearrange("p o n -> p (o n)"),
                                        ALU.subtract).then_inc(S["u_ready"], 1)

                    for k in range(2):
                        low_weights(k, KD, k)
                    if half == 0:
                        row_inverse(RST2)
                    with dve.Fori(0, 7) as i:
                        for k in range(2):
                            positive(2 * i + k, k)
                            low_weights(k, KD, 2 * i + k + 2)
                            low_up(2 * i + k, k)
                    for k in range(2):
                        positive(14 + k, k)
                        low_weights(k, 16, 16 + k)
                        low_up(14 + k, k)
                    residuals(16, 16)
                    arrive(dve, "dve")

            def row_cp(t, k, m):
                r = rows_of(t)
                if not (isinstance(t, int) and t < 2):
                    dve.wait_ge(S["row_T"], t - 1)
                V.tensor_copy(XO[k][:, :, 0:r], XT[:, :, cols(t)]).then_inc(S["row_cp"], 1)

            over_tiles(dve, row_cp)

        @block.gpsimd
        def _(pool):
            G = nc.gpsimd

            def release(first, last, entry, ways, stored=None):
                pool.drain()
                if stored is not None:
                    pool.wait_ge(S["os_out"], stored)
                    pool.sem_inc(S["os_stored"], 1)
                pool.wait_ge(entry, len(ways))
                pool.sem_clear(range(first, last + 1))
                pool.sem_clear(entry)
                for s in ways.values():
                    pool.sem_inc(s, 1)

            def everyone():
                release(first_sem, last_sem, all_in, go)

            def computers(stored=None):
                release(batch_sem, last_sem, all_in2, go2, stored)

            def power(x, which, n):
                pool.wait_ge(S[f"{which}_mean"], n)
                G.tensor_tensor(x, x, C("mhalf", x.shape[0]).to_broadcast(list(x.shape)), ALU.pow).then_inc(S[f"{which}_rstd"], 1)

            def row_powers(of):
                def step(t, k, m):
                    r = NS if isinstance(t, int) and t == QT else P
                    power(of(k)[0:r, :], "row", t + 1)
                over_tiles(pool, step)

            pool.wait_ge(loaded_once, 48)
            everyone()
            with pool.Fori(0, layers) as l:
                row_powers(lambda k: SS18)
                everyone()
                if stop <= 2:
                    return
                G.indirect_dma_start(LFP.rearrange("p t h -> p (t h)"), None,
                                     A["cache_fox_logf"].rearrange("l n t h -> (l n) (t h)"),
                                     bass.IndirectOffsetOnAxis(page_rows, 0)).then_inc(lfp_in, 16)
                pool.wait_ge(lfp_in, 16 * l + 16)
                pool.sem_inc(S["lfp_ready"], 1)
                G.tensor_scalar(page_rows, page_rows, POOL, None, ALU.add).then_inc(S["page_next"], 1)
                pool.wait_ge(S["page_next"], 1)
                everyone()
                if stop <= 3:
                    return
                everyone()
                with pool.Fori(0, NH) as h:
                    everyone()
                if stop <= 4:
                    return
                computers()
                if stop <= 5:
                    return
                with pool.Fori(0, NB // 2) as i:
                    for k in range(2):
                        b = 2 * i + k
                        bb = bass.ds(b, 1)
                        if k:
                            pool.wait_ge(S["sc_mm"], 12)
                        G.tensor_copy(QB, QALL[:, :, bb, :].rearrange("p a o n -> p a (o n)"))
                        G.tensor_copy(SNB1[k][0:32, :], SNB[0:32, bb, :].rearrange("p o j -> p (o j)"))
                        G.tensor_copy(QNB[0:HD, :], QNALL[0:HD, bb, :].rearrange("p o n -> p (o n)")).then_inc(S["qb_ready"], 1)
                        pool.wait_ge(S["bias_in"], 64 * b + 64)
                        G.tensor_tensor(BIAS[0:32, :], BIAS[0:32, :], FQ[0:32, bb].to_broadcast([32, LK]), ALU.add)\
                            .then_inc(S["pool_done2"], 1)
                        pool.wait_ge(S["pool_done2"], k + 1)
                        G.tensor_tensor(BIAS[0:32, PAST:], BIAS[0:32, PAST:], C("newneg", 32), ALU.add)\
                            .then_inc(S["bias_ready"], 1)
                    computers(64 * i + 64)
                everyone()
                if stop <= 6:
                    return
                row_powers(lambda k: S3[k])
                computers()
                everyone()
                if stop <= 7:
                    return
                everyone()
                computers()
                with pool.Fori(0, 2) as half:
                    everyone()


_OUTS = [
    ("y_prompt", (1, SEQ, DM)), ("y_sample", (NB, NT, DM)),
    ("fox_kv_p", (DEPTH, 1, SEQ, 2, NH, HD)), ("fox_kv_s", (DEPTH, NB, NT, 2, NH, HD)),
    ("fox_logf_p", (DEPTH, 1, SEQ, NH)), ("fox_logf_s", (DEPTH, NB, NT, NH)),
    ("nsa_kv_p", (DEPTH, 1, SEQ, 4, HD)), ("nsa_kv_s", (DEPTH, NB, NT, 4, HD)),
    ("nsa_win_p", (DEPTH, 1, WIN, 2, HD)), ("nsa_win_s", (DEPTH, NB, WIN, 2, HD)),
    ("conv_p", (DEPTH, 1, CW - 1, GW)), ("conv_s", (DEPTH, NB, CW - 1, GW)),
    ("gmlp_v_s", (DEPTH, NB, NT, GW)),
]


def program(nc, arrays, layers=DEPTH, stop=99):
    ins = {n: nc.dram_tensor(f"in_{n}", a.shape, mybir.dt.from_np(a.dtype), kind="ExternalInput").ap()
           for n, a in arrays.items()}
    outs = {n: nc.dram_tensor(f"out_{n}", shape, F32, kind="ExternalOutput").ap() for n, shape in _OUTS}
    build_step(nc, ins, outs, layers, stop)


def kernel(**inputs):
    import concourse.bacc as _bacc
    from concourse.bass_utils import run_bass_kernel_spmd as _run

    nc = _bacc.Bacc("TRN2", target_bir_lowering=False, num_devices=1)
    arrays = {n: np.ascontiguousarray(a) for n, a in inputs.items()}
    arrays["consts"] = shape_constants()[1]
    program(nc, arrays)
    r = _run(nc, [{f"in_{n}": a for n, a in arrays.items()}], core_ids=[0])
    return tuple(r.results[0][f"out_{n}"] for n, _ in _OUTS)
```
